# Optimizing a Trainium2 kernel written in Bass

```python
import functools
import jax, jax.numpy as jnp
from jax import lax
import numpy as np

D_MODEL = 1024
BATCH = 1
SEQ = 512
DEPTH = 2
DEC_BATCH = 8
DEC_SEQ = 1
PAST_LEN = 1024
PAGE_SIZE = 128

N_EVEN = (DEPTH + 1) // 2
N_ODD = DEPTH // 2
A_WIDTH = D_MODEL // 2
DH_A = 128
H_A = A_WIDTH // DH_A
DK_B = 128
DV_B = 128
H_B = (D_MODEL // 2) // DK_B
PROJ_SPLITS = (A_WIDTH, 2 * A_WIDTH, 3 * A_WIDTH, 3 * A_WIDTH + H_B * DK_B,
               3 * A_WIDTH + 2 * H_B * DK_B, 3 * A_WIDTH + 2 * H_B * DK_B + H_B * DV_B)
N_PROJ = 3 * A_WIDTH + 2 * H_B * DK_B + 2 * H_B * DV_B
DILATED = ((128, 1), (512, 4), (2048, 16))
W_MAX = 2048
Q_BLOCK = 128
NUM_BUCKETS = 32
MAX_DISTANCE = 2048
HGRN_CHUNK = 64
POOL_WINDOWS = (2, 4, 8, 16)
POOL_GROUP = D_MODEL // 4
POOL_KEEP = 15
N_GROUPS = 4
EXPERTS_PER_GROUP = 8
N_EXPERTS = 32
TOP_K = 2
D_EXPERT = 512
MOE_BLOCK = 128
MOE_BLOCK_SMALL = 8
EPS = 1e-6

kernel_name = 'hybrid_dilated_hgrn2_pool_hmoe_step'

def rmsnorm(x, g):
    xf = x.astype(jnp.float32)
    y = xf * lax.rsqrt(jnp.mean(xf * xf, -1, keepdims=True) + EPS) * g.astype(jnp.float32)
    return y.astype(x.dtype)

def t5_bucket(dist):
    max_exact = NUM_BUCKETS // 2
    d = np.asarray(dist)
    large = max_exact + np.floor(np.log(np.maximum(d, 1) / max_exact)
                                 / np.log(MAX_DISTANCE / max_exact) * (NUM_BUCKETS - max_exact)).astype(np.int32)
    large = np.minimum(large, NUM_BUCKETS - 1)
    return np.where(d < max_exact, d, large).astype(np.int32)

def dilated_attention(q, k, v, k_prev, v_prev, pos0, rel_bias):
    b_sz, t_len, n_h, d_h = q.shape
    f32 = jnp.float32
    qb = Q_BLOCK if t_len % Q_BLOCK == 0 else t_len
    n_blk = t_len // qb
    k_ext = jnp.concatenate([k_prev.astype(k.dtype), k], axis=1)
    v_ext = jnp.concatenate([v_prev.astype(v.dtype), v], axis=1)
    scale = d_h ** -0.5
    branches = []
    for w, d in DILATED:
        nk = w // d + 1
        dist = (d * np.arange(nk)).astype(np.int32)
        idx = (W_MAX + np.arange(qb)[:, None] - dist[None, :]).astype(np.int32)
        bias = rel_bias.astype(f32)[t5_bucket(dist)].T
        branches.append((dist, idx, bias))

    def block(bi):
        start = bi * qb
        qf = lax.dynamic_slice_in_dim(q, start, qb, 1).astype(f32) * scale
        ks = lax.dynamic_slice_in_dim(k_ext, start, W_MAX + qb, 1)
        vs = lax.dynamic_slice_in_dim(v_ext, start, W_MAX + qb, 1)
        qpos = pos0 + start + jnp.arange(qb, dtype=jnp.int32)
        ms, ss, us = [], [], []
        for dist, idx, bias in branches:
            kg = ks[:, idx].astype(f32)
            vg = vs[:, idx].astype(f32)
            logit = jnp.einsum('bqhd,bqjhd->bhqj', qf, kg) + bias[None, :, None, :]
            valid = (qpos[:, None] - dist[None, :]) >= 0
            logit = jnp.where(valid[None, None], logit, -jnp.inf)
            m = jnp.max(logit, -1)
            p = jnp.exp(logit - m[..., None])
            ms.append(m)
            ss.append(jnp.sum(p, -1))
            us.append(jnp.einsum('bhqj,bqjhd->bhqd', p, vg))
        m_all = jnp.stack(ms)
        s_all = jnp.stack(ss)
        u_all = jnp.stack(us)
        c = jnp.exp(m_all - jnp.max(m_all, 0, keepdims=True))
        den = jnp.sum(c * s_all, 0)
        num = jnp.sum(c[..., None] * u_all, 0)
        return (num / den[..., None]).transpose(0, 2, 1, 3)

    out = lax.map(block, jnp.arange(n_blk, dtype=jnp.int32))
    return out.transpose(1, 0, 2, 3, 4).reshape(b_sz, t_len, n_h, d_h)

def hgrn2(q, fpre, i, g, s0, lb, gnorm):
    b, t, _ = q.shape
    f32 = jnp.float32
    qf = jax.nn.silu(q.astype(f32)).reshape(b, t, H_B, DK_B)
    lbh = lb.reshape(H_B, DK_B)
    f = lbh + (1.0 - lbh) * jax.nn.sigmoid(fpre.astype(f32).reshape(b, t, H_B, DK_B))
    logf = jnp.log(f)
    kf = 1.0 - f
    vf = i.astype(f32).reshape(b, t, H_B, DV_B)
    c = HGRN_CHUNK if t % HGRN_CHUNK == 0 else t
    n_c = t // c

    def chunks(a):
        return a.reshape(b, n_c, c, H_B, a.shape[-1]).swapaxes(0, 1)

    tril = jnp.tril(jnp.ones((c, c), dtype=bool))[None, :, :, None, None]

    def step(s, inp):
        qc, kc, vc, lfc = inp
        cb = jnp.cumsum(lfc, axis=1)
        inter = jnp.einsum('bthk,bhkv->bthv', qc * jnp.exp(cb), s)
        decay = jnp.exp(jnp.where(tril, cb[:, :, None] - cb[:, None, :], -jnp.inf))
        scores = jnp.einsum('btshk,bshk->btsh', qc[:, :, None] * decay, kc)
        intra = jnp.einsum('btsh,bshv->bthv', scores, vc)
        cl = cb[:, -1]
        s_new = jnp.exp(cl)[..., None] * s + jnp.einsum('bshk,bshv->bhkv', kc * jnp.exp(cl[:, None] - cb), vc)
        return s_new, inter + intra

    s_fin, o = lax.scan(step, s0.astype(f32), (chunks(qf), chunks(kf), chunks(vf), chunks(logf)))
    o = o.swapaxes(0, 1).reshape(b, t, H_B, DV_B)
    o = o * lax.rsqrt(jnp.mean(o * o, -1, keepdims=True) + EPS) * gnorm.astype(f32)
    o = o.reshape(b, t, H_B * DV_B) * jax.nn.silu(g.astype(f32))
    return o, s_fin

def pool_mixer(h, prev, pos0, w_groups, scale):
    b, t, d = h.shape
    f32 = jnp.float32
    hf = h.astype(f32)
    ext = jnp.concatenate([prev.astype(f32), hf], axis=1)
    csum = jnp.concatenate([jnp.zeros((b, 1, d), f32), jnp.cumsum(ext, axis=1)], axis=1)
    pos = pos0 + jnp.arange(t, dtype=jnp.int32)
    outs = []
    for gi, w in enumerate(POOL_WINDOWS):
        sl = slice(gi * POOL_GROUP, (gi + 1) * POOL_GROUP)
        c_g = csum[:, :, sl]
        win_sum = c_g[:, POOL_KEEP + 1:POOL_KEEP + 1 + t] - c_g[:, POOL_KEEP + 1 - w:POOL_KEEP + 1 - w + t]
        cnt = jnp.minimum(w, pos + 1).astype(f32)
        mixed = win_sum / cnt[None, :, None] - hf[:, :, sl]
        outs.append(jnp.einsum('btc,cd->btd', mixed, w_groups[gi].astype(f32)))
    return jnp.concatenate(outs, -1) * scale.astype(f32)

def grouped_experts(xt, e, gate, w1, w3, w2):
    n, d = xt.shape
    a = e.shape[0]
    tok = jnp.repeat(jnp.arange(n, dtype=jnp.int32), TOP_K)
    blk = MOE_BLOCK if a >= MOE_BLOCK * N_EXPERTS else MOE_BLOCK_SMALL
    n_blk = (a + N_EXPERTS * (blk - 1) + blk - 1) // blk
    order = jnp.argsort(e)
    se = e[order]
    counts = jax.ops.segment_sum(jnp.ones((a,), jnp.int32), e, num_segments=N_EXPERTS)
    pcounts = (counts + blk - 1) // blk * blk
    start = jnp.cumsum(counts) - counts
    pend = jnp.cumsum(pcounts)
    pstart = pend - pcounts
    dest = pstart[se] + jnp.arange(a, dtype=jnp.int32) - start[se]
    tok_buf = jnp.full((n_blk * blk,), n, jnp.int32).at[dest].set(tok[order])
    gate_buf = jnp.zeros((n_blk * blk,), jnp.float32).at[dest].set(gate[order].astype(jnp.float32))
    blk_exp = jnp.minimum(jnp.searchsorted(pend, jnp.arange(n_blk, dtype=jnp.int32) * blk, side='right'),
                          N_EXPERTS - 1).astype(jnp.int32)
    x_pad = jnp.concatenate([xt, jnp.zeros((1, d), xt.dtype)], 0)

    def expert_block(args):
        tb, eb = args
        xb = x_pad[tb]
        return jnp.dot(jax.nn.silu(jnp.dot(xb, w1[eb])) * jnp.dot(xb, w3[eb]), w2[eb])

    yb = lax.map(expert_block, (tok_buf.reshape(n_blk, blk), blk_exp))
    y = jnp.zeros((n + 1, d), jnp.float32).at[tok_buf].add(yb.reshape(-1, d).astype(jnp.float32) * gate_buf[:, None])
    return y[:n]

def hier_moe(h, wg_group, bg_group, wg_exp, bg_exp, w1, w3, w2):
    b, t, d = h.shape
    n = b * t
    xt = h.reshape(n, d)
    glog = jnp.dot(xt, wg_group).astype(jnp.float32) + bg_group.astype(jnp.float32)
    pg, gsel = lax.top_k(jax.nn.softmax(glog, -1), 1)
    elog = (jnp.dot(xt, wg_exp).astype(jnp.float32) + bg_exp.astype(jnp.float32)).reshape(n, N_GROUPS, EXPERTS_PER_GROUP)
    elog = jnp.take_along_axis(elog, gsel[:, :, None], axis=1)[:, 0]
    pe, esel = lax.top_k(jax.nn.softmax(elog, -1), TOP_K)
    gate = pe / jnp.sum(pe, -1, keepdims=True) * pg
    eid = (gsel * EXPERTS_PER_GROUP + esel).astype(jnp.int32)
    y = grouped_experts(xt, eid.reshape(-1), gate.reshape(-1), w1, w3, w2)
    return y.reshape(b, t, d).astype(h.dtype)

def trunk(x, win_k_prev, win_v_prev, hgrn_prev, pool_prev, pos0, rel_bias, norm_mix, norm_ffn, norm_final,
          w_in, w_out, hgrn_lb, hgrn_gnorm, pool_w, pool_scale, moe_wg_group, moe_bg_group,
          moe_wg_exp, moe_bg_exp, moe_w1, moe_w3, moe_w2):
    b, t, _ = x.shape
    lb_all = jnp.cumsum(jax.nn.softmax(hgrn_lb.astype(jnp.float32), axis=0), axis=0)
    new_k, new_v, new_s, new_p = [], [], [], []
    for layer in range(DEPTH):
        h = rmsnorm(x, norm_mix[layer])
        if layer % 2 == 0:
            e = layer // 2
            proj = jnp.dot(h, w_in[e])
            qa, ka, va, qb, fb, ib, gb = jnp.split(proj, PROJ_SPLITS, axis=-1)
            ka = ka.reshape(b, t, H_A, DH_A)
            va = va.reshape(b, t, H_A, DH_A)
            oa = dilated_attention(qa.reshape(b, t, H_A, DH_A), ka, va, win_k_prev[e], win_v_prev[e], pos0, rel_bias)
            ob, s_fin = hgrn2(qb, fb, ib, gb, hgrn_prev[e], lb_all[e], hgrn_gnorm[e])
            mix = jnp.dot(jnp.concatenate([oa.reshape(b, t, A_WIDTH).astype(h.dtype), ob.astype(h.dtype)], -1), w_out[e])
            keep = min(W_MAX, t)
            new_k.append(ka[:, t - keep:])
            new_v.append(va[:, t - keep:])
            new_s.append(s_fin)
        else:
            o = layer // 2
            mix = pool_mixer(h, pool_prev[o], pos0, pool_w[o], pool_scale[o])
            keep = min(POOL_KEEP, t)
            new_p.append(h[:, t - keep:])
        x = x + mix.astype(x.dtype)
        h = rmsnorm(x, norm_ffn[layer])
        x = x + hier_moe(h, moe_wg_group[layer], moe_bg_group[layer], moe_wg_exp[layer], moe_bg_exp[layer],
                         moe_w1[layer], moe_w3[layer], moe_w2[layer])
    y = rmsnorm(x, norm_final)
    return y, jnp.stack(new_k), jnp.stack(new_v), jnp.stack(new_s), jnp.stack(new_p)

def setup_inputs(seed: int = 0) -> dict:
    key = jax.random.key(seed)
    ks = jax.random.split(key, 23)
    f32 = jnp.float32
    l_buf = min(W_MAX, PAST_LEN)

    def nrm(k, shape, scale):
        return jax.random.normal(k, shape, f32) * scale

    return {
        'x_prompt': nrm(ks[0], (BATCH, SEQ, D_MODEL), 1.0),
        'x_sample': nrm(ks[1], (DEC_BATCH, DEC_SEQ, D_MODEL), 1.0),
        'cache_win_k': nrm(ks[2], (N_EVEN, DEC_BATCH, l_buf, H_A, DH_A), 1.0),
        'cache_win_v': nrm(ks[3], (N_EVEN, DEC_BATCH, l_buf, H_A, DH_A), 1.0),
        'state_hgrn': nrm(ks[4], (N_EVEN, DEC_BATCH, H_B, DK_B, DV_B), 0.3),
        'state_pool': nrm(ks[5], (N_ODD, DEC_BATCH, POOL_KEEP, D_MODEL), 1.0),
        'rel_bias': nrm(ks[6], (NUM_BUCKETS, H_A), 0.5),
        'norm_mix': 1.0 + nrm(ks[7], (DEPTH, D_MODEL), 0.05),
        'norm_ffn': 1.0 + nrm(ks[8], (DEPTH, D_MODEL), 0.05),
        'norm_final': 1.0 + nrm(ks[9], (D_MODEL,), 0.05),
        'w_in': nrm(ks[10], (N_EVEN, D_MODEL, N_PROJ), D_MODEL ** -0.5),
        'w_out': nrm(ks[11], (N_EVEN, A_WIDTH + H_B * DV_B, D_MODEL), (A_WIDTH + H_B * DV_B) ** -0.5),
        'hgrn_lb': nrm(ks[12], (N_EVEN + 1, H_B * DK_B), 0.5),
        'hgrn_gnorm': 1.0 + nrm(ks[13], (N_EVEN, DV_B), 0.05),
        'pool_w': nrm(ks[14], (N_ODD, len(POOL_WINDOWS), POOL_GROUP, POOL_GROUP), POOL_GROUP ** -0.5),
        'pool_scale': 1.0 + nrm(ks[15], (N_ODD, D_MODEL), 0.05),
        'moe_wg_group': nrm(ks[16], (DEPTH, D_MODEL, N_GROUPS), D_MODEL ** -0.5),
        'moe_bg_group': nrm(ks[17], (DEPTH, N_GROUPS), 0.01),
        'moe_wg_exp': nrm(ks[18], (DEPTH, D_MODEL, N_EXPERTS), D_MODEL ** -0.5),
        'moe_bg_exp': nrm(ks[19], (DEPTH, N_EXPERTS), 0.01),
        'moe_w1': nrm(ks[20], (DEPTH, N_EXPERTS, D_MODEL, D_EXPERT), D_MODEL ** -0.5),
        'moe_w3': nrm(ks[21], (DEPTH, N_EXPERTS, D_MODEL, D_EXPERT), D_MODEL ** -0.5),
        'moe_w2': nrm(ks[22], (DEPTH, N_EXPERTS, D_EXPERT, D_MODEL), D_EXPERT ** -0.5),
    }

def reference(x_prompt, x_sample, cache_win_k, cache_win_v, state_hgrn, state_pool, rel_bias, norm_mix,
              norm_ffn, norm_final, w_in, w_out, hgrn_lb, hgrn_gnorm, pool_w, pool_scale, moe_wg_group,
              moe_bg_group, moe_wg_exp, moe_bg_exp, moe_w1, moe_w3, moe_w2):
    run = functools.partial(trunk, rel_bias=rel_bias, norm_mix=norm_mix, norm_ffn=norm_ffn, norm_final=norm_final,
                            w_in=w_in, w_out=w_out, hgrn_lb=hgrn_lb, hgrn_gnorm=hgrn_gnorm, pool_w=pool_w,
                            pool_scale=pool_scale, moe_wg_group=moe_wg_group, moe_bg_group=moe_bg_group,
                            moe_wg_exp=moe_wg_exp, moe_bg_exp=moe_bg_exp, moe_w1=moe_w1, moe_w3=moe_w3,
                            moe_w2=moe_w2)
    b = x_prompt.shape[0]
    zk = jnp.zeros((N_EVEN, b, W_MAX, H_A, DH_A), x_prompt.dtype)
    zs = jnp.zeros((N_EVEN, b, H_B, DK_B, DV_B), jnp.float32)
    zp = jnp.zeros((N_ODD, b, POOL_KEEP, D_MODEL), x_prompt.dtype)
    y_prompt, k_p, v_p, s_p, p_p = run(x_prompt, zk, zk, zs, zp, 0)
    l_buf = cache_win_k.shape[2]
    pad = ((0, 0), (0, 0), (W_MAX - l_buf, 0), (0, 0), (0, 0))
    y_sample, k_s, v_s, s_s, p_s = run(x_sample, jnp.pad(cache_win_k, pad), jnp.pad(cache_win_v, pad),
                                       state_hgrn, state_pool, PAST_LEN)
    return (y_prompt, y_sample, k_p, v_p, s_p, p_p, k_s, v_s, s_s, p_s)


_drawn_inputs = setup_inputs


def setup_inputs(seed=0):
    import zlib

    import numpy as np

    out = dict(_drawn_inputs(seed))
    spreads = {}
    factors = {'moe_bg_group': 3.428, 'moe_bg_exp': 2.817}
    for name, (base, spread) in spreads.items():
        noise = np.random.default_rng([zlib.crc32(name.encode()), seed]).standard_normal(out[name].shape)
        drawn = base * np.exp(spread * noise) if base else spread * noise
        out[name] = __import__('jax').numpy.asarray(drawn.astype(out[name].dtype))
    for name, factor in factors.items():
        out[name] = (out[name] * factor).astype(out[name].dtype)
    return out
```

```python
from contextlib import ExitStack

import numpy as np

import concourse.bass as bass
from concourse import mybir

ALU = mybir.AluOpType
ACT = mybir.ActivationFunctionType
F32 = mybir.dt.float32
I32 = mybir.dt.int32
U32 = mybir.dt.uint32
AX = mybir.AxisListType

P = 128
D = 1024
KC = D // P
SEQ = 512
NT = SEQ // P
NB = 8
TILES = NT + 1
TOK = SEQ + NB
HEADS = 4
DH = 128
AW = HEADS * DH
NPROJ = 7 * AW
PAST = 1024
NG = 4
EPG = 8
NE = 32
FE = 512
FC = FE // P
CAP = 64
NOV = 2 * TOK // (CAP + 1)
SLOTS = (NE + NOV) * CAP
THR = (TOK + CAP - 1) // CAP
EPS = 1e-6
SCALE = DH ** -0.5
PIECE = 4096
RING = 6
NEG = -1e30
BRANCHES = ((128, 1), (512, 4), (2048, 16))
BUCKETS = 32
MAXD = 2048
WINDOWS = (2, 4, 8, 16)
KEEP = 15
LEVELS = (128, 64, 32, 16)
ROWW = 640
NDEC = 257


def rows_of(t):
    return P if t < NT else NB


def shape_constants():
    def bucket(d):
        big = 16 + np.floor(np.log(np.maximum(d, 1) / 16) / np.log(MAXD / 16) * 16).astype(np.int32)
        return np.where(d < 16, d, np.minimum(big, BUCKETS - 1))

    def columns(dist):
        dist = np.asarray(dist)
        ok = dist >= 0
        d = np.where(ok, dist, 0)
        mult = sum(((d % s == 0) & (d <= w) & ok).astype(np.int32) for w, s in BRANCHES)
        out = np.zeros((BUCKETS + 1, len(d)), np.float32)
        out[bucket(d), np.arange(len(d))] = mult > 0
        out[BUCKETS] = np.where(mult > 0, np.log(np.maximum(mult, 1)), NEG)
        return out

    prompt = columns(SEQ - 1 - np.arange(ROWW))
    p = np.arange(P)
    near = P - p
    far = np.where(p < 96, 512 - 4 * p, 1024 - 16 * (p - 96))
    decode = columns(np.concatenate([near, far, [0]]))
    onehot = np.concatenate([prompt, decode], 1)

    s, t = np.arange(P)[:, None], np.arange(P)[None, :]
    levels = []
    for n in LEVELS[:-1]:
        levels.append((s // n == t // n) & (s % n < n // 2) & (t % n >= n // 2))
    levels.append((s // 16 == t // 16) & (s <= t))
    reset = np.broadcast_to((np.arange(SEQ) % P != 0).astype(np.float32), (P, SEQ))
    one = lambda a: np.broadcast_to(np.asarray(a, np.float32), (P, len(a)))
    valid = np.stack([(p < rows_of(k)) for k in range(TILES)], 1)
    square = np.concatenate([np.eye(P), np.ones((P, P)), s < t], 1)
    small = np.concatenate([one(np.arange(NE)), one(np.arange(NE) * CAP), one((np.arange(THR) + 1) * CAP), valid,
                            np.ones((P, NE))], 1)
    masks = np.concatenate(levels + [reset], 1)

    pool = np.zeros((P, 3, len(WINDOWS), P), np.float32)
    for g, w in enumerate(WINDOWS):
        own = ((s <= t) & (t - s < w)).astype(np.float32)
        before = (P + t - s < w).astype(np.float32)
        pool[:, 0, g] = own / np.minimum(w, t + 1) - np.eye(P)
        pool[:, 1, g] = own / w - np.eye(P)
        pool[:, 2, g] = before / w
    state = np.zeros((P, 2, len(WINDOWS), NB), np.float32)
    for g, w in enumerate(WINDOWS):
        for b in range(NB):
            state[b * KEEP + KEEP - (w - 1):(b + 1) * KEEP, 0, g, b] = 1 / w
            state[b, 1, g, b] = 1 / w - 1
    pools = np.concatenate([pool.reshape(P, -1), state.reshape(P, -1)], 1)
    return {k: np.ascontiguousarray(v, dtype=np.float32) for k, v in
            (("c_onehot", onehot), ("c_square", square), ("c_small", small), ("c_masks", masks), ("c_pool", pools))}


def build(nc, a, outs, consts):
    (y_prompt, y_sample, k_prompt, v_prompt, s_prompt, p_prompt, k_sample, v_sample, s_sample, p_sample) = outs
    slot_x = nc.dram_tensor("slot_x", (SLOTS, D), F32, kind="Internal").ap()
    slot_y = nc.dram_tensor("slot_y", (SLOTS, D), F32, kind="Internal").ap()
    bias_rows = nc.dram_tensor("bias_rows", (HEADS, P, ROWW), F32, kind="Internal").ap()

    with ExitStack() as ctx:
        ring = ctx.enter_context(nc.sbuf_tensor("ring", [P, RING, PIECE], F32))
        ARENA = 28600
        arena = ctx.enter_context(nc.sbuf_tensor("arena", [P, ARENA], F32))
        ps = ctx.enter_context(nc.psum_tensor("ps", [P, 8, 512], F32))

        def sem(name):
            return ctx.enter_context(nc.semaphore(name))

        def at(lo, *shape):
            n = int(np.prod(shape))
            assert lo + n <= ARENA, (lo, shape)
            v = arena[:, lo:lo + n]
            if len(shape) == 1:
                return v
            names = "abcd"[:len(shape)]
            return v.rearrange(f"p ({' '.join(names)}) -> p {' '.join(names)}",
                               **{k: s for k, s in zip(names, shape)})

        def wide(ap, shape, axis):
            return ap.unsqueeze(axis).broadcast_to(shape)

        hT = at(0, KC, TOK)
        catT = at(0, KC, TOK)
        qT = at(4160, HEADS, TOK)
        kT = at(6240, HEADS, TOK)
        vtok = at(8320, TILES, AW)
        qbT = at(10880, HEADS, TOK)
        fT = at(12960, HEADS, TOK)
        ib = at(15040, TILES, AW)
        gb = at(17600, TILES, AW)
        xin = [at(4160 + 1024 * t, D) for t in range(TILES)]
        hrow = at(22208, D)
        gain0 = at(23232, D)
        junk = at(24256, D)
        toep = at(20160, HEADS, SEQ)
        prob = [at(22208 + 512 * i, SEQ) for i in range(2)]
        probT = [at(23232 + 512 * i, NT, P) for i in range(2)]
        ktok = [at(24256 + 512 * i, AW) for i in range(2)]
        relx = at(25280, HEADS)
        relrep = at(25288, NB, HEADS)
        onehot = at(25320, ROWW + NDEC)
        brow = at(26220, ROWW)
        astat = at(26862, 96)
        keyT = [at(20160 + 1024 * i, 2 * HEADS, P) for i in range(2)]
        dscT = at(22208, 2, NB, HEADS)
        dlog = at(22272, NDEC)
        dprob = at(22532, NDEC)
        dbias = at(22792, NDEC)
        qkself = at(23052, NB, HEADS)
        diag = at(23084, 32)
        vrow = at(23116, DH)
        dprobT = at(23244, 2, 32)
        dstat = at(23310, 8)
        wl = [[at(4160 + 2560 * i + 512 * j, SEQ) for j in range(3)] for i in range(2)]
        q16 = [at(4160 + 2560 * i + 1536, SEQ) for i in range(2)]
        k16 = [at(4160 + 2560 * i + 2048, SEQ) for i in range(2)]
        qc = [at(20160 + 1024 * i, SEQ) for i in range(2)]
        kdT = [at(20160 + 1024 * i + 512, SEQ) for i in range(2)]
        lcum = at(22208, SEQ)
        ldif = at(22720, SEQ)
        lexp = at(23232, SEQ)
        kdtok = [at(23744 + 128 * i, P) for i in range(2)]
        smask = [at(24000 + 512 * i, 4, P) for i in range(2)]
        state = at(25024, HEADS, DH)
        sq = at(25536, HEADS, DH)
        gnb = at(26048, DH)
        ostage = at(26176, HEADS, DH)
        hstat = at(26688, 160)
        vonly = at(22208, AW)
        tmp_kv = at(22720, HEADS, DH)
        osq = at(23232, 32)
        osT = at(23264, HEADS, NB)
        gsT = at(23296, HEADS, NB)
        gncol = at(23328, 1)
        sstat = at(23332, 128)
        masks = at(26970, 4, P)
        reset = at(27482, SEQ)
        zero = at(26970, D)
        x = at(4160, TILES, D)
        hall = at(9280, TILES, D)
        xg = at(9280, D)
        yst = at(10304, D)
        gat = [at(9280 + 1024 * i, D) for i in range(4)]
        htile = at(14400, KC, P)
        wr = at(15424, 2, KC, NG + NE)
        rbias = at(16000, 2, NG + NE)
        xgT = at(16072, KC, 2 * CAP)
        sg = at(17096, FE)
        hact = at(17608, FE)
        hactT = at(26900, FC, 2 * CAP)
        gain = [at(18120 + 1024 * i, D) for i in range(2)]
        R = 20168
        lg = at(R, TILES, NG + NE)
        g8 = at(R + 180, TILES, 8)
        gm8 = at(R + 220, TILES, 8)
        e8 = at(R + 260, TILES, 8)
        em8 = at(R + 300, TILES, 8)
        gi8 = at(R + 340, TILES, 8).bitcast(U32)
        ei8 = at(R + 380, TILES, 8).bitcast(U32)
        gsel = at(R + 420, TILES)
        g4 = at(R + 425, TILES, NG)
        eid = at(R + 445, TILES, 2)
        dexp = at(R + 455, TILES, 5)
        gden = at(R + 480, TILES)
        sel = at(R + 485, TILES, NG, EPG)
        oh = at(R + 645, TILES, 2, NE)
        mem = at(R + 965, TILES, NE)
        over = at(R + 1125, TILES, NE)
        ohs = at(R + 1285, TILES, 2, NE)
        novx = at(R + 1605, NE)
        ovend = at(R + 1637, NE)
        dbase = at(R + 1669, NE)
        ovf = at(R + 1701, NOV)
        cmp = at(R + 1725, NE, THR)
        assert THR * NE <= 320 and NOV <= 24
        poolc = at(22216, 3, len(WINDOWS), P)
        poolstate = at(22216 + 1536, 2, len(WINDOWS), NB)
        prev = at(23816, D)
        mixT = at(24840, KC, P)
        pscale = at(25864, D)
        poolw = at(0, NG, 2, 256)
        spare = at(26900, D)
        ecmp = at(2048, NOV, NE)
        C = 28000
        ident = at(C, P)
        ones = at(C + 128, P)
        tri = at(C + 256, P)
        small = at(C + 384, 2 * NE + THR + TILES + NE)
        iota = small[:, 0:NE]
        ebase = small[:, NE:2 * NE]
        thr = small[:, 2 * NE:2 * NE + THR]
        valid = small[:, 2 * NE + THR:2 * NE + THR + TILES]
        ones32 = small[:, 2 * NE + THR + TILES:]
        M = C + 384 + 3 * NE + THR + TILES
        ssq = at(M, TILES)
        rms = at(M + 5, TILES)
        gates = at(M + 10, TILES, 2)
        slotu = at(M + 20, TILES, 2).bitcast(U32)
        slotf = at(M + 30, TILES, 2)
        tables = [at(lo, NOV + 1).bitcast(I32) for lo in (M + 40, M + 85)]
        lbl = at(M + 65, 2, HEADS)
        lb = at(M + 73, HEADS)
        oml = at(M + 77, HEADS)
        lbs = at(M + 81, HEADS)
        assert M + 85 + NOV + 1 <= ARENA and NOV + 1 <= 25

        consts_in = sem("consts_in")
        masks_in = sem("masks_in")
        x_in = [sem(f"x_in{i}") for i in range(TILES)]
        gain_in = sem("gain_in")
        meansq = sem("meansq")
        root = sem("root")
        h_ready = sem("h_ready")
        h_turned = sem("h_turned")
        hT_ready = sem("hT_ready")
        w_in = [sem(f"w_in{i}") for i in range(7)]
        kv_in = [sem(f"kv_in{i}") for i in range(4)]
        kv_used = sem("kv_used")
        state_in = sem("state_in")
        wout_in = [sem(f"wout_in{i}") for i in range(2)]
        unit_done = sem("unit_done")
        unit_out = sem("unit_out")
        kt_turned = sem("kt_turned")
        ktok_ready = sem("ktok_ready")
        ktok_stored = [sem(f"ktok_stored{i}") for i in range(2)]
        stored = sem("stored")
        rel_in = sem("rel_in")
        rel_ready = sem("rel_ready")
        brow_done = sem("brow_done")
        brow_ready = sem("brow_ready")
        brow_stored = sem("brow_stored")
        toep_in = sem("toep_in")
        logit_done = sem("logit_done")
        logit_ready = sem("logit_ready")
        prob_ready = sem("prob_ready")
        prob_normed = sem("prob_normed")
        prob_turned = sem("prob_turned")
        probT_ready = sem("probT_ready")
        att_done = sem("att_done")
        att_out = sem("att_out")
        dbias_done = sem("dbias_done")
        key_turned = sem("key_turned")
        keyT_ready = sem("keyT_ready")
        dscore_done = sem("dscore_done")
        dscore_part = sem("dscore_part")
        dscT_ready = sem("dscT_ready")
        dlog_done = sem("dlog_done")
        qkself_ready = sem("qkself_ready")
        dlog_ready = sem("dlog_ready")
        dprob_exp = sem("dprob_exp")
        dprob_ready = sem("dprob_ready")
        dprob_turned = sem("dprob_turned")
        dprobT_ready = sem("dprobT_ready")
        vrow_in = sem("vrow_in")
        datt_done = sem("datt_done")
        vs_stored = sem("vs_stored")
        zeros_ready = sem("zeros_ready")
        slots_cleared = sem("slots_cleared")
        lb_in = sem("lb_in")
        lb_exp = sem("lb_exp")
        lbl_ready = sem("lbl_ready")
        f_ready = sem("f_ready")
        logf_ready = sem("logf_ready")
        dif_ready = sem("dif_ready")
        exp_ready = sem("exp_ready")
        ops_ready = sem("ops_ready")
        lvl_done = sem("lvl_done")
        smask_ready = sem("smask_ready")
        kd_turned = sem("kd_turned")
        kdtok_ready = sem("kdtok_ready")
        o_done = sem("o_done")
        o_out = sem("o_out")
        state_ready = sem("state_ready")
        state_stored = sem("state_stored")
        gn_in = sem("gn_in")
        ohead_sq = sem("ohead_sq")
        ohead_ms = sem("ohead_ms")
        ohead_root = sem("ohead_root")
        og_ready = sem("og_ready")
        og_turned = sem("og_turned")
        og_out = sem("og_out")
        vonly_ready = sem("vonly_ready")
        vb_done = sem("vb_done")
        snew_ready = sem("snew_ready")
        snew_stored = sem("snew_stored")
        os_done = sem("os_done")
        osq_ready = sem("osq_ready")
        oss_done = sem("oss_done")
        oms_ready = sem("oms_ready")
        oroot = sem("oroot")
        cat_ready = sem("cat_ready")
        mixers_done = sem("mixers_done")
        xres_in = sem("xres_in")
        wo_done = sem("wo_done")
        x_added = sem("x_added")
        router_in = sem("router_in")
        act_chain = sem("act_chain")
        dve_chain = sem("dve_chain")
        hn_ready = sem("hn_ready")
        hn_turned = sem("hn_turned")
        htile_ready = sem("htile_ready")
        rlog_done = sem("rlog_done")
        dexp_ready = sem("dexp_ready")
        gexp_ready = sem("gexp_ready")
        mem_ready = sem("mem_ready")
        rank_done = sem("rank_done")
        slots_ready = sem("slots_ready")
        scattered = sem("scattered")
        gathered = [sem(f"gathered{i}") for i in range(2)]
        gat_used = sem("gat_used")
        y_all_stored = [sem(f"y_all_stored{i}") for i in range(2)]
        pool_in = sem("pool_in")
        poolw_in = sem("poolw_in")
        mix_done = sem("mix_done")
        mixT_ready = sem("mixT_ready")
        pool_done = sem("pool_done")
        y_final = sem("y_final")

        wt_in = [sem(f"wt_in{i}") for i in range(RING)]
        w1_used = sem("w1_used")
        xg_in = sem("xg_in")
        x_turned = sem("x_turned")
        xT_ready = sem("xT_ready")
        h_done = sem("h_done")
        silu_ready = sem("silu_ready")
        hact_ready = sem("hact_ready")
        hact_turned = sem("hact_turned")
        hactT_ready = sem("hactT_ready")
        y_done = sem("y_done")
        y_out = sem("y_out")
        y_stored = sem("y_stored")
        PAIRS = NE // 2
        over_in = [sem(f"over_in{l}") for l in range(2)]
        over_step = [sem(f"over_step{l}") for l in range(2)]
        over_stored = [sem(f"over_stored{l}") for l in range(2)]
        over_seen = sem("over_seen")
        TURNED, COLUMNS, PRODUCTS, SILU, GATED, ACT_TURNED, ACT_COLUMNS, ROWS, OUT = range(1, 10)

        def over_count(j, step):
            return 9 * j + step

        FIRST = 14

        UNITS = [4, 8, 13, 17, 21, 26, 31]

        def piece_slot(half, j):
            return (FIRST + 2 * j + half) % RING

        w1v = ring[:, :, :].rearrange("p s (k f) -> p s k f", k=KC)
        w2v = ring[:, :, :].rearrange("p s (k d) -> p s k d", k=FC)
        kvv = ring[:, :, :].rearrange("p s (b w t c) -> p s b w t c", b=2, w=2, t=2)
        stv = ring[:, 11 % RING, :].rearrange("p (b h v) -> p b h v", b=NB, h=HEADS)

        xp = a["x_prompt"].rearrange("b (t p) d -> p (b t) d", p=P)
        xs = a["x_sample"].rearrange("b t d -> (b t) d")

        def x_rows(t):
            return xp[:, t, :] if t < NT else xs

        def gate_rows(name, layer, e):
            return a[name][layer, bass.ds(e, 1), :, :].rearrange("a (k p) f -> p (a k) f", p=P)

        def slot_rows(tensor, block):
            return tensor[bass.ds(block * CAP, CAP), :]

        def chained(eng, signal):
            n = [0]

            def link(instruction):
                n[0] += 1
                instruction.then_inc(signal, 1)
                eng.wait_ge(signal, n[0])
            return link

        block = ctx.enter_context(nc.Block())

        @block.sync
        def _(sp):
            for t in range(TILES):
                sp.dma_start(xin[t][0:rows_of(t)], x_rows(t)).then_inc(x_in[t], 16)
            for c in range(RING):
                sp.dma_start(w1v[:, c], a["w_in"][0, :, c * AW:(c + 1) * AW].rearrange(
                    "(k p) f -> p k f", p=P)).then_inc(w_in[c], 16)
            sp.wait_ge(unit_done, UNITS[1 - 1])
            sp.dma_start(w1v[:, 0], a["w_in"][0, :, 6 * AW:7 * AW].rearrange(
                "(k p) f -> p k f", p=P)).then_inc(w_in[6], 16)
            for c in range(4):
                sp.wait_ge(unit_done, UNITS[c + 1])
                for b in range(2):
                    for w, name in enumerate(("cache_win_k", "cache_win_v")):
                        src = a[name][0, 2 * c + b].rearrange("r h d -> r (h d)")
                        dst = kvv[:, (7 + c) % RING, b, w]
                        for to, of in ((dst[:, 0, :], src[PAST - P:PAST, :]),
                                       (dst[0:96, 1, :], src[512:893:4, :]),
                                       (dst[96:P, 1, :], src[0:497:16, :])):
                            sp.dma_start(to, of).then_inc(kv_in[c], 16)
            sp.wait_ge(unit_done, UNITS[6 - 1])
            sp.dma_start(stv[:, :, :, :], a["state_hgrn"][0].rearrange("b h k v -> k b h v")).then_inc(state_in, 16)
            for c in range(2):
                if c == 0:
                    sp.wait_ge(unit_done, UNITS[7 - 1])
                else:
                    sp.wait_ge(kv_used, 1)
                sp.dma_start(w1v[:, (12 + c) % RING], a["w_out"][0, :, c * 512:(c + 1) * 512].rearrange(
                    "(k p) f -> p k f", p=P)).then_inc(wout_in[c], 16)

            def load(l, e, half, j, before):
                if before is not None:
                    sp.wait_ge((w1_used, h_done, y_done)[j], before)
                s = piece_slot(half, j)
                name = ("moe_w1", "moe_w3", "moe_w2")[j]
                sp.dma_start(w2v[:, s] if j == 2 else w1v[:, s], gate_rows(name, l, e)).then_inc(wt_in[s], 16)

            for l in range(2):
                for j in range(3):
                    for half in range(2):
                        if l == 0 and (half, j) == (0, 0):
                            sp.wait_ge(kv_used, 4)
                        if l == 0 and (half, j) == (1, 1):
                            sp.wait_ge(snew_stored, 16)
                            sp.wait_ge(wo_done, 2 * TILES)
                        load(l, half, half, j, None if l == 0 else PAIRS)
                with sp.Fori(1, PAIRS) as i:
                    for j in range(3):
                        for half in range(2):
                            load(l, 2 * i + half, half, j, PAIRS * l + i)
                sp.wait_ge(slots_ready, l + 1)
                n_over = sp.value_load(tables[l][0:1, NOV:NOV + 1], min_val=0, max_val=NOV)
                with sp.If(n_over > 0):
                    sp.wait_ge(y_done, PAIRS * (l + 1))
                    with sp.Fori(0, NOV) as j:
                        with sp.If(n_over > j):
                            e = sp.value_load(tables[l][0:1, bass.ds(j, 1)], min_val=0, max_val=NE - 1)
                            for k, name in enumerate(("moe_w1", "moe_w3", "moe_w2")):
                                s = piece_slot(0, k)
                                dst = w2v[:, s] if k == 2 else w1v[:, s]
                                sp.dma_start(dst, gate_rows(name, l, e)).then_inc(over_in[l], 16)
                            sp.wait_ge(over_step[l], over_count(j, ROWS))
                            sp.sem_inc(over_seen, 1)
                        with sp.Else():
                            sp.nop()
                    sp.nop()
                with sp.Else():
                    sp.nop()
                sp.nop()

        @block.gpsimd
        def _(pool):
            nc.gpsimd.memset(zero, 0.0).then_inc(zeros_ready, 1)
            pool.wait_ge(brow_ready, 1)
            pool.dma_start(bias_rows, wide(brow[0:HEADS], [HEADS, P, ROWW], 1)).then_inc(brow_stored, 16)
            pool.wait_ge(brow_stored, 16)
            pool.dma_start(toep, bass.AP(bias_rows.tensor, P - 1, [[ROWW - 1, P], [P * ROWW, HEADS], [1, SEQ]])).then_inc(toep_in, 16)
            pool.wait_ge(zeros_ready, 1)
            pool.wait_ge(unit_done, UNITS[1])
            for table, lo in ((slot_x, 0), (slot_y, NE * CAP)):
                rows = table[lo:SLOTS, :].rearrange("(p j) d -> p j d", p=P)
                pool.dma_start(rows, wide(zero, [P, rows.shape[1], D], 1)).then_inc(slots_cleared, 16)
            pool.wait_ge(slots_cleared, 32)
            pool.dma_start(at(26970, 4 * P + SEQ), consts["c_masks"]).then_inc(masks_in, 16)
            for l in range(2):
                pool.wait_ge(slots_ready, l + 1)
                for t in range(TILES):
                    for k in range(2):
                        n = rows_of(t)
                        pool.indirect_dma_start(
                            out=slot_x[:, :], out_offset=bass.IndirectOffsetOnAxis(ap=slotu[0:n, t, k:k + 1], axis=0),
                            in_=hall[0:n, t, :], in_offset=None).then_inc(scattered, 16)
                pool.wait_ge(y_all_stored[l], 1)
                for t in range(TILES):
                    for k in range(2):
                        n = rows_of(t)
                        g = TILES * l + t
                        if t >= 2:
                            pool.wait_ge(gat_used, g - 1)
                        pool.indirect_dma_start(
                            out=gat[2 * (t % 2) + k][0:n, :], out_offset=None, in_=slot_y[:, :],
                            in_offset=bass.IndirectOffsetOnAxis(ap=slotu[0:n, t, k:k + 1], axis=0),
                        ).then_inc(gathered[t % 2], 16)

        @block.scalar
        def _(act):
            link = chained(act, act_chain)
            act.dma_start(gain0, a["norm_mix"][0:1, :].partition_broadcast(P).rearrange("p a d -> p (a d)")).then_inc(gain_in, 16)
            act.dma_start(at(C, 384), consts["c_square"]).then_inc(consts_in, 16)
            act.dma_start(small, consts["c_small"]).then_inc(consts_in, 16)
            with nc.allow_non_contiguous_dma(reason="1024 words of the gates' lower bound, once"):
                for j in range(2):
                    act.dma_start(lbl[:, j, :], a["hgrn_lb"][j].rearrange("(h k) -> k h", k=P)).then_inc(lb_in, 16)
            act.dma_start(onehot[0:BUCKETS + 1], consts["c_onehot"]).then_inc(rel_in, 16)
            act.dma_start(relx[0:BUCKETS, :], a["rel_bias"]).then_inc(rel_in, 16)
            def roots(t, m):
                act.wait_ge(meansq, m + 1)
                nc.scalar.activation(rms[0:rows_of(t), t:t + 1], ssq[0:rows_of(t), t:t + 1], ACT.Sqrt).then_inc(root, 1)

            for t in range(TILES):
                n = rows_of(t)
                roots(t, t)
                act.wait_ge(h_turned, t + 1)
                b = 2 * (t % 2)
                nc.scalar.activation(hT[:, :, t * P:t * P + n],
                                     ps[:, b:b + 2, :].rearrange("p b (k c) -> p (b k) c", k=4)[:, :, 0:n],
                                     ACT.Copy).then_inc(hT_ready, 1)

            unit = 0
            for c in range(7):
                if c in (0, 1, 3, 4):
                    dst = {0: qT, 1: kT, 3: qbT, 4: fT}[c]
                    fn = {0: ACT.Copy, 1: ACT.Copy, 3: ACT.Silu, 4: ACT.Sigmoid}[c]
                    for h in range(HEADS):
                        act.wait_ge(unit_done, unit + 1)
                        nc.scalar.activation(dst[:, h, 0:SEQ], ps[:, unit % 2, :], fn)
                        nc.scalar.activation(dst[:, h, SEQ:TOK], ps[:, 2 + unit % 2, 0:NB], fn).then_inc(unit_out, 1)
                        unit += 1
                else:
                    dst = {2: vtok, 5: ib, 6: gb}[c]
                    fn = ACT.Silu if c == 6 else ACT.Copy
                    for t in range(TILES):
                        n = rows_of(t)
                        act.wait_ge(unit_done, unit + 1)
                        nc.scalar.activation(dst[0:n, t, :], ps[0:n, unit % 2, :], fn).then_inc(unit_out, 1)
                        unit += 1
                if c == 2:
                    act.wait_ge(unit_out, unit)
                    act.dma_start(v_prompt.rearrange("a b (t p) h d -> p (a b t) (h d)", p=P), vtok[:, 0:NT, :]).then_inc(stored, 16)
                    act.dma_start(v_sample.rearrange("a b t h d -> (a b t) (h d)"), vtok[0:NB, NT, :]).then_inc(vs_stored, 16)
            for t in range(TILES):
                n = rows_of(t)
                act.wait_ge(kt_turned, t + 1)
                if t >= 2:
                    act.wait_ge(ktok_stored[t % 2], 16 * (t // 2))
                nc.scalar.activation(ktok[t % 2][0:n, :], ps[0:n, 4 + t % 2, :], ACT.Copy).then_inc(ktok_ready, 1)
                act.wait_ge(ktok_ready, t + 1)
                dst = (k_prompt.rearrange("a b (t p) h d -> p (a b t) (h d)", p=P)[:, t, :] if t < NT
                       else k_sample.rearrange("a b t h d -> (a b t) (h d)"))
                act.dma_start(dst, ktok[t % 2][0:n, :]).then_inc(ktok_stored[t % 2], 16)

            for n in range(HEADS * NT):
                i = n % NT
                w = (i + 1) * P
                act.wait_ge(logit_ready, n + 1)
                nc.scalar.activation(prob[n % 2][:, 0:w], prob[n % 2][:, 0:w], ACT.Exp,
                                     bias=astat[:, n:n + 1], accum_out=astat[:, 16 + n:17 + n]).then_inc(prob_ready, 1)
                act.wait_ge(prob_turned, n + 1)
                nc.scalar.activation(probT[n % 2][:, 0:i + 1, :],
                                     ps[:, 2 + n % 2, 0:w].rearrange("p (a b) -> p a b", b=P), ACT.Copy).then_inc(probT_ready, 1)
            for b in range(NB):
                act.wait_ge(key_turned, b + 1)
                if b == 0:
                    act.wait_ge(att_out, HEADS * NT)
                p2 = 2 * (b % 2)
                nc.scalar.activation(keyT[b % 2][:, :, :],
                                     ps[:, p2:p2 + 2, :].rearrange("p b (k c) -> p (b k) c", k=4), ACT.Copy).then_inc(keyT_ready, 1)
            act.wait_ge(vs_stored, 16)
            act.wait_ge(att_out, HEADS * NT)
            act.dma_start(vrow[0:32], v_sample.rearrange("a b t h d -> (a b t h) d")).then_inc(vrow_in, 16)
            act.wait_ge(dlog_ready, 1)
            nc.scalar.activation(dprob[0:32], dlog[0:32], ACT.Exp, bias=dstat[0:32, 0:1],
                                 accum_out=dstat[0:32, 1:2]).then_inc(dprob_exp, 1)

            act.wait_ge(lbl_ready, 1)
            nc.scalar.activation(lbl, lbl, ACT.Exp).then_inc(lb_exp, 1)
            act.wait_ge(att_out, HEADS * NT + 1)
            act.dma_start(gnb, a["hgrn_gnorm"][0:1, :].partition_broadcast(P).rearrange("p a d -> p (a d)")).then_inc(gn_in, 16)
            def decays(h):
                act.wait_ge(f_ready, h + 1)
                nc.scalar.activation(ldif, fT[:, h, 0:SEQ], ACT.Ln).then_inc(logf_ready, 1)
                for step in range(6):
                    act.wait_ge(dif_ready, 6 * h + step + 1)
                    if step < 3:
                        link(nc.scalar.activation(lexp, ldif, ACT.Abs))
                        nc.scalar.activation(lexp, lexp, ACT.Exp, scale=-1.0).then_inc(exp_ready, 1)
                    elif step == 3:
                        link(nc.scalar.activation(lexp, ldif, ACT.Exp))
                        nc.scalar.activation(ldif, ldif, ACT.Exp, scale=-1.0).then_inc(exp_ready, 1)
                    elif step == 4:
                        nc.scalar.activation(lexp, lcum, ACT.Exp).then_inc(exp_ready, 1)
                    else:
                        nc.scalar.activation(lexp, ldif, ACT.Exp, scale=-1.0).then_inc(exp_ready, 1)

            decays(0)
            for h in range(HEADS):
                if h + 1 < HEADS:
                    decays(h + 1)
                for t in range(NT):
                    m = NT * h + t
                    act.wait_ge(kd_turned, m + 1)
                    nc.scalar.activation(kdtok[m % 2], ps[:, 2 + m % 2, 0:P], ACT.Copy).then_inc(kdtok_ready, 1)
                    act.wait_ge(o_done, m + 1)
                    nc.scalar.activation(ib[:, t, h * DH:(h + 1) * DH], ps[:, 4 + m % 2, 0:P],
                                         ACT.Copy).then_inc(o_out, 1)
                act.wait_ge(state_ready, NT * (h + 1))
                act.dma_start(s_prompt[0, 0, h], state[:, h, :]).then_inc(state_stored, 16)
            for t in range(NT):
                act.wait_ge(o_out, HEADS * NT)
                if t >= 1:
                    act.wait_ge(ohead_ms, t)
                nc.scalar.activation(sq.rearrange("p a b -> p (a b)"), ib[:, t, :], ACT.Square).then_inc(ohead_sq, 1)
                act.wait_ge(ohead_ms, t + 1)
                nc.scalar.activation(hstat[:, 8 * t + 4:8 * t + 8], hstat[:, 8 * t:8 * t + 4], ACT.Sqrt).then_inc(ohead_root, 1)
                act.wait_ge(og_turned, t + 1)
                nc.scalar.activation(catT[:, HEADS:2 * HEADS, t * P:(t + 1) * P],
                                     ps[:, 4 + t % 2, :].rearrange("p (h c) -> p h c", h=HEADS), ACT.Copy).then_inc(og_out, 1)
            act.dma_start(gncol, a["hgrn_gnorm"][0].rearrange("(k a) -> k a", a=1)).then_inc(gn_in, 16)
            act.wait_ge(snew_ready, NB)
            act.dma_start(s_sample[0].rearrange("b h k v -> k b h v"), stv[:, :, :, :]).then_inc(snew_stored, 16)
            act.wait_ge(oms_ready, 1)
            nc.scalar.activation(sstat[:, 32:64], sstat[:, 0:32], ACT.Sqrt).then_inc(oroot, 1)

            act.wait_ge(mixers_done, 1)
            for t in range(TILES):
                act.dma_start(x[0:rows_of(t), t, :], x_rows(t)).then_inc(xres_in, 16)
            act.dma_start(gain[1], a["norm_ffn"][0:1, :].partition_broadcast(P).rearrange("p a d -> p (a d)")).then_inc(router_in, 16)
            for l in range(2):
                act.dma_start(wr[:, l, :, 0:NG], a["moe_wg_group"][l].rearrange("(k p) g -> p k g", p=P)).then_inc(router_in, 16)
                act.dma_start(wr[:, l, :, NG:], a["moe_wg_exp"][l].rearrange("(k p) g -> p k g", p=P)).then_inc(router_in, 16)
                act.dma_start(rbias[:, l, 0:NG], a["moe_bg_group"][l:l + 1, :].partition_broadcast(P).rearrange("p a d -> p (a d)")).then_inc(router_in, 16)
                act.dma_start(rbias[:, l, NG:], a["moe_bg_exp"][l:l + 1, :].partition_broadcast(P).rearrange("p a d -> p (a d)")).then_inc(router_in, 16)
            act.dma_start(at(22216, 1536 + 64), consts["c_pool"]).then_inc(pool_in, 16)
            act.dma_start(prev[0:NB * KEEP], a["state_pool"][0].rearrange("b r d -> (b r) d")).then_inc(pool_in, 16)
            act.dma_start(pscale, a["pool_scale"].partition_broadcast(P).rearrange("p a d -> p (a d)")).then_inc(pool_in, 16)
            act.dma_start(gain[0], a["norm_mix"][1:2, :].partition_broadcast(P).rearrange("p a d -> p (a d)")).then_inc(pool_in, 16)

            def experts(l):
                for t in range(TILES):
                    m = TILES * (1 if l == 0 else 3) + t
                    g = TILES * l + t
                    roots(t, m)
                    n = rows_of(t)
                    act.wait_ge(hn_turned, g + 1)
                    if g:
                        act.wait_ge(rlog_done, g)
                    b = 2 * (t % 2)
                    nc.scalar.activation(htile[:, :, 0:n],
                                         ps[:, b:b + 2, :].rearrange("p b (k c) -> p (b k) c", k=4)[:, :, 0:n],
                                         ACT.Copy).then_inc(htile_ready, 1)
                act.wait_ge(dexp_ready, l + 1)
                nc.scalar.activation(dexp, dexp, ACT.Exp).then_inc(gexp_ready, 1)
                def load_rows(i):
                    act.dma_start(xg, slot_x[bass.ds(i * 2 * CAP, 2 * CAP), :]).then_inc(xg_in, 16)

                def pair(i, first, last):
                    if not last:
                        act.wait_ge(x_turned, PAIRS * l + i + 1)
                        load_rows(i + 1)
                    act.wait_ge(h_done, PAIRS * l + i + 1)
                    nc.scalar.activation(sg, ps[:, 2, :], ACT.Silu).then_inc(silu_ready, 1)
                    act.wait_ge(y_done, PAIRS * l + i + 1)
                    if not first:
                        act.wait_ge(y_stored, 16 * PAIRS * l + 16 * i)
                    nc.scalar.activation(yst, ps[:, 5:7, :].rearrange("p a b -> p (a b)"), ACT.Copy).then_inc(y_out, 1)
                    act.wait_ge(y_out, PAIRS * l + i + 1)
                    act.dma_start(slot_y[bass.ds(i * 2 * CAP, 2 * CAP), :], yst).then_inc(y_stored, 16)

                act.wait_ge(scattered, 16 * 2 * TILES * (l + 1))
                load_rows(0)
                pair(0, True, False)
                with act.Fori(1, PAIRS - 1) as i:
                    pair(i, False, False)
                pair(PAIRS - 1, False, True)
                act.wait_ge(y_stored, 16 * PAIRS * (l + 1))
                n_over = act.value_load(tables[l][0:1, NOV:NOV + 1], min_val=0, max_val=NOV)
                with act.If(n_over > 0):
                    with act.Fori(0, NOV) as j:
                        with act.If(n_over > j):
                            act.dma_start(xg[0:CAP, :], slot_rows(slot_x, NE + j)).then_inc(over_in[l], 16)
                            act.wait_ge(over_step[l], over_count(j, PRODUCTS))
                            nc.scalar.activation(sg[0:CAP], ps[0:CAP, 2, :], ACT.Silu).then_inc(over_step[l], 1)
                            act.wait_ge(over_step[l], over_count(j, ROWS))
                            nc.scalar.activation(yst[0:CAP, :], ps[0:CAP, 5:7, :].rearrange("p a b -> p (a b)"),
                                                 ACT.Copy).then_inc(over_step[l], 1)
                            act.wait_ge(over_step[l], over_count(j, OUT))
                            act.dma_start(slot_rows(slot_y, NE + j), yst[0:CAP, :]).then_inc(over_stored[l], 16)
                            act.wait_ge(over_stored[l], 16 * j + 16)
                            act.sem_inc(over_seen, 1)
                        with act.Else():
                            act.nop()
                    act.nop()
                with act.Else():
                    act.nop()
                act.sem_inc(y_all_stored[l], 1)

            act.wait_ge(wo_done, 2 * TILES)
            for g in range(NG):
                act.dma_start(poolw[:, g], a["pool_w"][0, g].rearrange("(k p) c -> p k c", p=P)).then_inc(poolw_in, 16)
            experts(0)
            for t in range(TILES):
                m = 2 * TILES + t
                roots(t, m)
            for t in range(TILES):
                n = rows_of(t)
                act.wait_ge(mix_done, t + 1)
                if t:
                    act.wait_ge(pool_done, t)
                nc.scalar.activation(mixT[:, :, 0:n],
                                     ps[:, 0:2, :].rearrange("p b (k c) -> p (b k) c", k=4)[:, :, 0:n],
                                     ACT.Copy).then_inc(mixT_ready, 1)
                if t == NT - 1:
                    act.dma_start(p_prompt[0, 0], hall[P - KEEP:P, t, :]).then_inc(stored, 16)
                if t == NT:
                    act.dma_start(p_sample[0].rearrange("b t d -> (b t) d"), hall[0:NB, t, :]).then_inc(stored, 16)
            act.wait_ge(x_added, 3 * TILES)
            act.dma_start(gain[1], a["norm_ffn"][1:2, :].partition_broadcast(P).rearrange("p a d -> p (a d)")).then_inc(router_in, 16)
            act.dma_start(gain[0], a["norm_final"].rearrange("(a d) -> a d", a=1).partition_broadcast(P).rearrange("p a d -> p (a d)")).then_inc(router_in, 16)
            act.wait_ge(stored, 16 * 3)
            act.sem_inc(y_final, 1)
            experts(1)
            for t in range(TILES):
                m = 4 * TILES + t
                roots(t, m)
                act.wait_ge(y_final, t + 2)
                dst = y_prompt.rearrange("b (t p) d -> p (b t) d", p=P)[:, t, :] if t < NT else y_sample.rearrange("b t d -> (b t) d")
                act.dma_start(dst, x[0:rows_of(t), t, :]).then_inc(stored, 16)
            act.wait_ge(stored, 16 * (3 + TILES))
            act.wait_ge(vs_stored, 16)
            for i in range(2):
                act.wait_ge(ktok_stored[i], 16 * len(range(i, TILES, 2)))
            act.wait_ge(state_stored, 16 * HEADS)
            act.wait_ge(snew_stored, 16)

        @block.vector
        def _(dve):
            link = chained(dve, dve_chain)
            V = nc.vector

            def norm(x_of, h_of, gain_of, count, before=None, after=None):
                def squares(t):
                    n = rows_of(t)
                    if before:
                        before(t)
                    link(V.tensor_tensor_reduce(junk_of[0][0:n], x_of(t), x_of(t), 1.0, 0.0, ALU.mult, ALU.add,
                                                ssq[0:n, t:t + 1]))
                    V.tensor_scalar(ssq[0:n, t:t + 1], ssq[0:n, t:t + 1], 1.0 / D, EPS, ALU.mult, ALU.add).then_inc(meansq, 1)

                def scaled(t):
                    n = rows_of(t)
                    dve.wait_ge(root, count + t + 1)
                    link(V.reciprocal(rms[0:n, t:t + 1], rms[0:n, t:t + 1]))
                    if after:
                        after(t)
                    return V.scalar_tensor_tensor(h_of(t), x_of(t), rms[0:n, t:t + 1], gain_of[0:n], ALU.mult, ALU.mult)
                return squares, scaled

            junk_of = [junk]
            squares, scaled = norm(
                lambda t: xin[t][0:rows_of(t)], lambda t: hrow[0:rows_of(t)], gain0, 0,
                before=lambda t: dve.wait_ge(x_in[t], 16),
                after=lambda t: dve.wait_ge(h_turned, t) if t else dve.wait_ge(gain_in, 16))
            squares(0)
            for t in range(TILES):
                if t + 1 < TILES:
                    if t + 1 < TILES:
                        squares(t + 1)
                scaled(t).then_inc(h_ready, 1)
            dve.wait_ge(rel_in, 32)
            V.memset(relx[BUCKETS:BUCKETS + 1, :], 1.0).then_inc(rel_ready, 1)
            dve.wait_ge(rel_ready, 1)
            V.tensor_copy(relrep[0:BUCKETS + 1], wide(relx[0:BUCKETS + 1, :], [BUCKETS + 1, NB, HEADS], 1)).then_inc(rel_ready, 1)
            dve.wait_ge(brow_done, 1)
            V.tensor_copy(brow[0:HEADS], ps[0:HEADS, 6:8, :].rearrange("p a b -> p (a b)")[:, 0:ROWW]).then_inc(brow_ready, 1)
            dve.wait_ge(lb_in, 32)
            link(V.tensor_tensor(lbs, lbl[:, 0, :], lbl[:, 1, :], ALU.max))
            V.tensor_tensor(lbl, lbl, wide(lbs, [P, 2, HEADS], 1), ALU.subtract).then_inc(lbl_ready, 1)

            def logits(n):
                h, i = n // NT, n % NT
                w = (i + 1) * P
                dve.wait_ge(logit_done, n + 1)
                if n >= 2:
                    dve.wait_ge(prob_turned, n - 1)
                if n == 0:
                    dve.wait_ge(toep_in, 16)
                link(V.scalar_tensor_tensor(prob[n % 2][:, 0:w], ps[:, n % 2, 0:w], SCALE, toep[:, h, SEQ - w:SEQ], ALU.mult, ALU.add))
                V.tensor_reduce(astat[:, n:n + 1], prob[n % 2][:, 0:w], AX.X, ALU.max, negate=True).then_inc(logit_ready, 1)

            def normed(n):
                w = (n % NT + 1) * P
                dve.wait_ge(prob_ready, n + 1)
                link(V.reciprocal(astat[:, 32 + n:33 + n], astat[:, 16 + n:17 + n]))
                V.tensor_scalar(prob[n % 2][:, 0:w], prob[n % 2][:, 0:w], astat[:, 32 + n:33 + n], None, ALU.mult).then_inc(prob_normed, 1)

            def out_heads(n):
                h, i = n // NT, n % NT
                dve.wait_ge(att_done, n + 1)
                V.tensor_copy(catT[:, h, i * P:(i + 1) * P], ps[:, 4 + n % 2, 0:P]).then_inc(att_out, 1)

            logits(0)
            for n in range(HEADS * NT):
                if n + 1 < HEADS * NT:
                    logits(n + 1)
                normed(n)
                if n:
                    out_heads(n - 1)
            out_heads(HEADS * NT - 1)
            dve.wait_ge(att_out, HEADS * NT)
            V.tensor_tensor(qkself.rearrange("p b h -> p h b"), qT[:, :, SEQ:TOK], kT[:, :, SEQ:TOK], ALU.mult).then_inc(qkself_ready, 1)
            dve.wait_ge(dbias_done, 1)
            link(V.tensor_copy(dbias[0:32], ps[0:32, 7, 0:NDEC]))
            dve.wait_ge(dscore_done, 1)
            V.tensor_copy(dscT.rearrange("p t b h -> p (t b h)"), ps[:, 4, 0:64]).then_inc(dscT_ready, 1)
            dve.wait_ge(dlog_done, 1)
            link(V.scalar_tensor_tensor(dlog[0:32], ps[0:32, 5, 0:NDEC], SCALE, dbias[0:32], ALU.mult, ALU.add))
            V.tensor_reduce(dstat[0:32, 0:1], dlog[0:32], AX.X, ALU.max, negate=True).then_inc(dlog_ready, 1)
            dve.wait_ge(dprob_exp, 1)
            link(V.reciprocal(dstat[0:32, 2:3], dstat[0:32, 1:2]))
            link(V.tensor_scalar(dprob[0:32], dprob[0:32], dstat[0:32, 2:3], None, ALU.mult))
            V.tensor_scalar(diag[0:32], ident[0:32, 0:32], dprob[0:32, NDEC - 1:NDEC], None, ALU.mult).then_inc(dprob_ready, 1)
            dve.wait_ge(dprob_turned, 1)
            V.tensor_copy(dprobT.rearrange("p t c -> p (t c)"), ps[:, 6, 0:64]).then_inc(dprobT_ready, 1)
            dve.wait_ge(datt_done, 1)
            V.tensor_copy(catT[:, 0:HEADS, SEQ:TOK], ps[:, 7, 0:32].rearrange("p (b h) -> p h b", b=NB)).then_inc(att_out, 1)

            dve.wait_ge(lb_exp, 1)
            link(V.tensor_tensor(lbs, lbl[:, 0, :], lbl[:, 1, :], ALU.add))
            link(V.reciprocal(lbs, lbs))
            link(V.tensor_tensor(lb, lbl[:, 0, :], lbs, ALU.mult))
            link(V.tensor_scalar(oml, lb, -1.0, 1.0, ALU.mult, ALU.add))
            dve.wait_ge(att_out, HEADS * NT + 1)
            dve.wait_ge(masks_in, 16)

            def blocks(ap, n):
                return ap.rearrange("p (b n) -> p b n", n=n)

            def operands(h):
                q_ = qbT[:, h, 0:SEQ]
                f_ = fT[:, h, 0:SEQ]
                s = h % 2
                V.tensor_scalar(fT[:, h, :], fT[:, h, :], oml[:, h:h + 1], lb[:, h:h + 1], ALU.mult, ALU.add).then_inc(f_ready, 1)
                dve.wait_ge(logf_ready, h + 1)
                link(V.tensor_tensor_scan(lcum, reset, ldif, 0.0, ALU.mult, ALU.add))
                link(V.tensor_scalar(f_, f_, -1.0, 1.0, ALU.mult, ALU.add))
                if h >= 2:
                    dve.wait_ge(o_done, NT * (h - 1))

                def differ(n, at_):
                    V.tensor_tensor(blocks(ldif, n), blocks(lcum, n),
                                    blocks(lcum, n)[:, :, at_:at_ + 1].broadcast_to([P, SEQ // n, n]), ALU.subtract).then_inc(dif_ready, 1)

                def exped(step):
                    dve.wait_ge(exp_ready, 6 * h + step + 1)

                for j, n in enumerate(LEVELS[:-1]):
                    differ(n, n // 2 - 1)
                    exped(j)
                    w_, e_ = blocks(wl[s][j], n), blocks(lexp, n)
                    V.tensor_tensor(w_[:, :, n // 2:], blocks(q_, n)[:, :, n // 2:], e_[:, :, n // 2:], ALU.mult)
                    link(V.tensor_tensor(w_[:, :, :n // 2], blocks(f_, n)[:, :, :n // 2], e_[:, :, :n // 2], ALU.mult))
                differ(16, 7)
                exped(3)
                link(V.tensor_tensor(q16[s], q_, lexp, ALU.mult))
                link(V.tensor_tensor(k16[s], f_, ldif, ALU.mult))
                dve.sem_inc(dif_ready, 1)
                exped(4)
                link(V.tensor_tensor(qc[s], q_, lexp, ALU.mult))
                link(V.tensor_copy(hstat[:, 64 + 4 * h:68 + 4 * h].unsqueeze(2), blocks(lexp, P)[:, :, P - 1:P]))
                differ(P, P - 1)
                exped(5)
                V.tensor_tensor(kdT[s], f_, lexp, ALU.mult).then_inc(ops_ready, 1)
                dve.wait_ge(ops_ready, h + 1)

            operands(0)
            for h in range(HEADS):
                if h + 1 < HEADS:
                    operands(h + 1)
                for t in range(NT):
                    m = NT * h + t
                    dve.wait_ge(lvl_done, m + 1)
                    if m >= 2:
                        dve.wait_ge(o_done, m - 1)
                    V.scalar_tensor_tensor(smask[m % 2].rearrange("p a b -> p (a b)"), ps[:, m % 2, :], 3e38,
                                           masks.rearrange("p a b -> p (a b)"), ALU.min, ALU.mult).then_inc(smask_ready, 1)
                    dve.wait_ge(o_done, m + 1)
                    new = ps[:, 6 + m % 2, 0:P]
                    if t == 0:
                        V.tensor_copy(state[:, h, :], new).then_inc(state_ready, 1)
                    else:
                        dve.wait_ge(state_ready, m)
                        V.scalar_tensor_tensor(state[:, h, :], state[:, h, :], hstat[:, 64 + 4 * h + t:65 + 4 * h + t], new,
                                               ALU.mult, ALU.add).then_inc(state_ready, 1)
            dve.wait_ge(gn_in, 16)
            dve.wait_ge(o_out, HEADS * NT)
            for t in range(NT):
                dve.wait_ge(ohead_sq, t + 1)
                link(V.tensor_reduce(hstat[:, 8 * t:8 * t + 4], sq, AX.X, ALU.add))
                V.tensor_scalar(hstat[:, 8 * t:8 * t + 4], hstat[:, 8 * t:8 * t + 4], 1.0 / DH, EPS, ALU.mult, ALU.add).then_inc(ohead_ms, 1)
                dve.wait_ge(ohead_root, t + 1)
                r_ = hstat[:, 8 * t + 4:8 * t + 8]
                link(V.reciprocal(r_, r_))
                if t:
                    dve.wait_ge(og_turned, t)
                o_ = ib[:, t, :].rearrange("p (h v) -> p h v", h=HEADS)
                link(V.tensor_tensor(ostage, o_, wide(r_, [P, HEADS, DH], 2), ALU.mult))
                link(V.tensor_tensor(ostage, ostage, wide(gnb, [P, HEADS, DH], 1), ALU.mult))
                V.tensor_tensor(ostage.rearrange("p h v -> p (h v)"), ostage.rearrange("p h v -> p (h v)"), gb[:, t, :],
                                ALU.mult).then_inc(og_ready, 1)
            dve.wait_ge(state_in, 16)
            fs = fT[:, :, SEQ:TOK]
            ks = sstat[:, 64:96].rearrange("p (h b) -> p h b", h=HEADS)
            link(V.tensor_scalar(ks, fs, -1.0, 1.0, ALU.mult, ALU.add))
            for b in range(NB):
                if b:
                    dve.wait_ge(vb_done, b)
                V.tensor_scalar(vonly[0:NB], ib[0:NB, NT, :], ident[0:NB, b:b + 1], None, ALU.mult).then_inc(vonly_ready, 1)
                dve.wait_ge(vb_done, b + 1)
                link(V.tensor_tensor(tmp_kv, ps[:, b % 2, :].rearrange("p (h v) -> p h v", h=HEADS),
                                     ks[:, :, b:b + 1].broadcast_to([P, HEADS, DH]), ALU.mult))
                link(V.tensor_tensor(stv[:, b], stv[:, b], fs[:, :, b:b + 1].broadcast_to([P, HEADS, DH]), ALU.mult))
                V.tensor_tensor(stv[:, b], stv[:, b], tmp_kv, ALU.add).then_inc(snew_ready, 1)
                dve.wait_ge(snew_ready, b + 1)
            dve.wait_ge(os_done, 1)
            link(V.tensor_copy(osT.rearrange("p h b -> p (h b)"), ps[:, 6, 0:32]))
            V.tensor_tensor(osq, osT.rearrange("p h b -> p (h b)"), osT.rearrange("p h b -> p (h b)"), ALU.mult).then_inc(osq_ready, 1)
            link(V.tensor_copy(gsT.rearrange("p h b -> p (h b)"), ps[:, 6, 32:64]))
            dve.wait_ge(oss_done, 1)
            V.tensor_scalar(sstat[:, 0:32], ps[:, 7, 0:32], 1.0 / DH, EPS, ALU.mult, ALU.add).then_inc(oms_ready, 1)
            dve.wait_ge(oroot, 1)
            link(V.reciprocal(sstat[:, 32:64], sstat[:, 32:64]))
            dve.wait_ge(gn_in, 32)
            link(V.scalar_tensor_tensor(osT.rearrange("p h b -> p (h b)"), osT.rearrange("p h b -> p (h b)"), gncol[:, 0:1],
                                        sstat[:, 32:64], ALU.mult, ALU.mult))
            V.tensor_tensor(catT[:, HEADS:, SEQ:TOK], osT, gsT, ALU.mult).then_inc(cat_ready, 1)
            dve.wait_ge(cat_ready, 1)
            dve.wait_ge(og_out, NT)
            dve.wait_ge(state_stored, 16 * HEADS)
            dve.wait_ge(stored, 16)
            dve.wait_ge(vs_stored, 16)
            for i in range(2):
                dve.wait_ge(ktok_stored[i], 16 * len(range(i, TILES, 2)))
            dve.sem_inc(mixers_done, 1)
            for t in range(TILES):
                n = rows_of(t)
                dve.wait_ge(wo_done, 2 * (t + 1))
                if t == 0:
                    dve.wait_ge(xres_in, 16 * TILES)
                b = 4 + 2 * (t % 2)
                V.tensor_tensor(x[0:n, t, :], x[0:n, t, :], ps[0:n, b:b + 2, :].rearrange("p a b -> p (a b)"), ALU.add).then_inc(x_added, 1)

            def experts(l):
                squares, scaled = norm(lambda t: x[0:rows_of(t), t, :], lambda t: hall[0:rows_of(t), t, :], gain[1],
                                       TILES * (1 if l == 0 else 3))
                junk_of[0] = spare
                link(V.memset(lg, 0.0))
                link(V.memset(g8, NEG))
                if l == 0:
                    dve.wait_ge(router_in, 16 * 9)
                    dve.wait_ge(pool_in, 16 * 4)
                else:
                    dve.wait_ge(router_in, 16 * 11)
                    dve.wait_ge(y_final, 1)

                def logit(t):
                    n = rows_of(t)
                    dve.wait_ge(rlog_done, TILES * l + t + 1)
                    link(V.tensor_tensor(lg[0:n, t, :], ps[0:n, 4 + t % 2, 0:NG + NE], rbias[0:n, l, :], ALU.add))

                dve.wait_ge(x_added, TILES * (1 if l == 0 else 3))
                squares(0)
                for t in range(TILES):
                    if t + 1 < TILES:
                        squares(t + 1)
                    scaled(t).then_inc(hn_ready, 1)
                    if t:
                        logit(t - 1)
                logit(NT)
                link(V.tensor_copy(g8[:, :, 0:NG], lg[:, :, 0:NG]))
                for t in range(TILES):
                    link(V.max(gm8[:, t, :], g8[:, t, :]))
                    link(V.max_index(gi8[:, t, :], gm8[:, t, :], g8[:, t, :]))
                link(V.tensor_copy(gsel.unsqueeze(2), gi8[:, :, 0:1]))
                link(V.tensor_tensor(g4, wide(iota[:, 0:NG], [P, TILES, NG], 1), wide(gsel, [P, TILES, NG], 2), ALU.is_equal))
                for t in range(TILES):
                    link(V.tensor_tensor(sel[:, t], lg[:, t, NG:].rearrange("p (g e) -> p g e", g=NG),
                                         wide(g4[:, t, :], [P, NG, EPG], 2), ALU.mult))
                for t in range(TILES):
                    link(V.tensor_reduce(e8[:, t, :], sel[:, t].rearrange("p g e -> p e g"), AX.X, ALU.add))
                for t in range(TILES):
                    link(V.max(em8[:, t, :], e8[:, t, :]))
                    link(V.max_index(ei8[:, t, :], em8[:, t, :], e8[:, t, :]))
                link(V.tensor_tensor(dexp[:, :, 0:NG], lg[:, :, 0:NG], gm8[:, :, 0:1].broadcast_to([P, TILES, NG]), ALU.subtract))
                V.tensor_tensor(dexp[:, :, NG:NG + 1], em8[:, :, 1:2], em8[:, :, 0:1], ALU.subtract).then_inc(dexp_ready, 1)
                link(V.tensor_copy(eid, ei8[:, :, 0:2]))
                link(V.scalar_tensor_tensor(eid, wide(gsel, [P, TILES, 2], 2), float(EPG), eid, ALU.mult, ALU.add))
                for t in range(TILES):
                    link(V.tensor_tensor(oh[:, t], wide(iota, [P, 2, NE], 1), wide(eid[:, t, :], [P, 2, NE], 2), ALU.is_equal))
                link(V.tensor_tensor(mem, oh[:, :, 0, :], oh[:, :, 1, :], ALU.add))
                V.tensor_tensor(mem, mem, wide(valid, [P, TILES, NE], 2), ALU.mult).then_inc(mem_ready, 1)
                dve.wait_ge(gexp_ready, l + 1)
                link(V.tensor_reduce(gden, dexp[:, :, 0:NG], AX.X, ALU.add))
                w_ = dexp[:, :, NG:NG + 1]
                link(V.tensor_scalar(gates[:, :, 1:2], w_, 1.0, None, ALU.add))
                link(V.tensor_tensor(gates[:, :, 1:2], gates[:, :, 1:2], gden.unsqueeze(2), ALU.mult))
                link(V.reciprocal(gates[:, :, 0:1], gates[:, :, 1:2]))
                link(V.tensor_tensor(gates[:, :, 1:2], gates[:, :, 0:1], w_, ALU.mult))
                dve.wait_ge(rank_done, l + 1)
                rank = ps[:, 6, 0:TILES * NE].rearrange("p (t e) -> p t e", e=NE)
                count = ps[:, 7, 0:NE]
                link(V.tensor_tensor(cmp, wide(count, [P, NE, THR], 2), wide(thr, [P, NE, THR], 1), ALU.is_gt))
                link(V.tensor_reduce(novx, cmp, AX.X, ALU.add))
                link(V.tensor_tensor_scan(ovend, ones32, novx, 0.0, ALU.mult, ALU.add))
                link(V.tensor_tensor(dbase, ovend, novx, ALU.subtract))
                link(V.tensor_scalar(dbase, dbase, float(CAP), float((NE - 1) * CAP), ALU.mult, ALU.add))
                link(V.tensor_tensor(dbase, dbase, ebase, ALU.subtract))
                link(V.tensor_scalar(over, rank, float(CAP), None, ALU.is_ge))
                link(V.tensor_tensor(over, over, wide(dbase, [P, TILES, NE], 1), ALU.mult))
                link(V.tensor_tensor(over, over, rank, ALU.add))
                link(V.tensor_tensor(over, over, wide(ebase, [P, TILES, NE], 1), ALU.add))
                for k in range(2):
                    link(V.tensor_tensor(ohs[:, :, k, :], oh[:, :, k, :], over, ALU.mult))
                link(V.tensor_reduce(slotf, ohs, AX.X, ALU.add))
                link(V.tensor_copy(slotu, slotf))
                link(V.tensor_tensor(ecmp, wide(ovend, [P, NOV, NE], 1), wide(small[:, 0:NOV], [P, NOV, NE], 2), ALU.is_le))
                link(V.tensor_reduce(ovf, ecmp, AX.X, ALU.add))
                link(V.tensor_scalar(ovf, ovf, float(NE - 1), None, ALU.min))
                link(V.tensor_copy(tables[l][:, 0:NOV], ovf))
                V.tensor_copy(tables[l][:, NOV:NOV + 1], ovend[:, NE - 1:NE]).then_inc(slots_ready, 1)

                def gated(i, first):
                    dve.wait_ge(silu_ready, PAIRS * l + i + 1)
                    if not first:
                        dve.wait_ge(hact_turned, PAIRS * l + i)
                    V.tensor_tensor(hact, sg, ps[:, 3, :], ALU.mult).then_inc(hact_ready, 1)
                    dve.wait_ge(hact_turned, PAIRS * l + i + 1)
                    if not first:
                        dve.wait_ge(y_done, PAIRS * l + i)
                    V.tensor_copy(hactT.rearrange("p k c -> p (k c)"), ps[:, 4, :]).then_inc(hactT_ready, 1)

                def columns(i, first):
                    dve.wait_ge(x_turned, PAIRS * l + i + 1)
                    if not first:
                        dve.wait_ge(h_done, PAIRS * l + i)
                    V.tensor_copy(xgT.rearrange("p k c -> p (k c)"), ps[:, 0:2, :].rearrange("p a b -> p (a b)")).then_inc(xT_ready, 1)

                columns(0, True)
                gated(0, True)
                columns(1, False)
                with dve.Fori(1, PAIRS - 1) as i:
                    gated(i, False)
                    columns(i + 1, False)
                gated(PAIRS - 1, False)
                n_over = dve.value_load(tables[l][0:1, NOV:NOV + 1], min_val=0, max_val=NOV)
                with dve.If(n_over > 0):
                    with dve.Fori(0, NOV) as j:
                        with dve.If(n_over > j):
                            dve.wait_ge(over_step[l], over_count(j, TURNED))
                            V.tensor_copy(xgT[:, :, 0:CAP], ps[:, 0, :].rearrange("p (k c) -> p k c", k=KC)).then_inc(over_step[l], 1)
                            dve.wait_ge(over_step[l], over_count(j, SILU))
                            V.tensor_tensor(hact[0:CAP], sg[0:CAP], ps[0:CAP, 3, :], ALU.mult).then_inc(over_step[l], 1)
                            dve.wait_ge(over_step[l], over_count(j, ACT_TURNED))
                            V.tensor_copy(hactT[:, :, 0:CAP], ps[:, 4, 0:FC * CAP].rearrange("p (k c) -> p k c", k=FC)).then_inc(over_step[l], 1)
                        with dve.Else():
                            dve.nop()
                    dve.nop()
                with dve.Else():
                    dve.nop()
                for t in range(TILES):
                    n = rows_of(t)
                    g = TILES * l + t
                    uses = len(range(t % 2, TILES, 2)) * l + t // 2 + 1
                    dve.wait_ge(gathered[t % 2], 32 * uses)
                    link(V.scalar_tensor_tensor(x[0:n, t, :], gat[2 * (t % 2)][0:n], gates[0:n, t, 0:1], x[0:n, t, :], ALU.mult, ALU.add))
                    V.scalar_tensor_tensor(x[0:n, t, :], gat[2 * (t % 2) + 1][0:n], gates[0:n, t, 1:2], x[0:n, t, :],
                                           ALU.mult, ALU.add).then_inc(gat_used, 1)
                dve.wait_ge(gat_used, TILES * (l + 1))

            experts(0)
            squares, scaled = norm(lambda t: x[0:rows_of(t), t, :], lambda t: hall[0:rows_of(t), t, :], gain[0], 2 * TILES)
            squares(0)
            for t in range(TILES):
                if t + 1 < TILES:
                    squares(t + 1)
                scaled(t).then_inc(x_added, 1)
            for t in range(TILES):
                n = rows_of(t)
                dve.wait_ge(pool_done, t + 1)
                b = 2 + 2 * (t % 2)
                link(V.tensor_tensor(spare[0:n], ps[0:n, b:b + 2, :].rearrange("p a b -> p (a b)"), pscale[0:n], ALU.mult))
                V.tensor_tensor(x[0:n, t, :], x[0:n, t, :], spare[0:n], ALU.add).then_inc(x_added, 1)
                dve.wait_ge(x_added, 2 * TILES + t + 1)
            experts(1)
            junk_of[0] = spare
            squares, scaled = norm(lambda t: x[0:rows_of(t), t, :], lambda t: x[0:rows_of(t), t, :], gain[0], 4 * TILES)
            squares(0)
            for t in range(TILES):
                if t + 1 < TILES:
                    squares(t + 1)
                scaled(t).then_inc(y_final, 1)

        @block.tensor
        def _(pe):
            T = nc.tensor
            pe.wait_ge(consts_in, 32)
            for t in range(TILES):
                n = rows_of(t)
                pe.wait_ge(h_ready, t + 1)
                if t >= 2:
                    pe.wait_ge(hT_ready, t - 1)
                for k in range(KC):
                    last = T.transpose(ps[:, 2 * (t % 2) + k // 4, (k % 4) * P:(k % 4) * P + n], hrow[0:n, k * P:(k + 1) * P], ident[0:n, 0:n])
                last.then_inc(h_turned, 1)
            pe.wait_ge(rel_ready, 2)
            for j, (lo, hi) in enumerate(((0, 512), (512, ROWW))):
                last = T.matmul(ps[0:HEADS, 6 + j, 0:hi - lo], relx[0:BUCKETS + 1, :], onehot[0:BUCKETS + 1, lo:hi], start=True, stop=True)
            last.then_inc(brow_done, 1)
            pe.wait_ge(hT_ready, TILES)
            unit = 0
            for c in range(7):
                slot = c % RING
                pe.wait_ge(w_in[c], 16)
                for m in range(HEADS if c in (0, 1, 3, 4) else TILES):
                    if unit >= 2:
                        pe.wait_ge(unit_out, unit - 1)
                    for k in range(KC):
                        if c in (0, 1, 3, 4):
                            w_ = w1v[:, slot, k, m * P:(m + 1) * P]
                            last = T.matmul(ps[:, unit % 2, :], w_, hT[:, k, 0:SEQ], start=(k == 0), stop=(k == KC - 1))
                            last = T.matmul(ps[:, 2 + unit % 2, 0:NB], w_, hT[:, k, SEQ:TOK], start=(k == 0), stop=(k == KC - 1))
                        else:
                            n = rows_of(m)
                            last = T.matmul(ps[0:n, unit % 2, :], hT[:, k, m * P:m * P + n], w1v[:, slot, k, :],
                                            start=(k == 0), stop=(k == KC - 1))
                    last.then_inc(unit_done, 1)
                    unit += 1
            units = unit
            for t in range(TILES):
                n = rows_of(t)
                if t == 0:
                    pe.wait_ge(unit_out, units)
                if t >= 2:
                    pe.wait_ge(ktok_ready, t - 1)
                for h in range(HEADS):
                    last = T.transpose(ps[0:n, 4 + t % 2, h * P:(h + 1) * P], kT[:, h, t * P:t * P + n], ident)
                last.then_inc(kt_turned, 1)
            pe.wait_ge(ktok_ready, TILES)

            def scores(n):
                h, i = n // NT, n % NT
                if n >= 2:
                    pe.wait_ge(logit_ready, n - 1)
                T.matmul(ps[:, n % 2, 0:(i + 1) * P], qT[:, h, i * P:(i + 1) * P], kT[:, h, 0:(i + 1) * P],
                         start=True, stop=True).then_inc(logit_done, 1)

            scores(0)
            for n in range(HEADS * NT):
                h, i = n // NT, n % NT
                if n + 1 < HEADS * NT:
                    scores(n + 1)
                pe.wait_ge(prob_normed, n + 1)
                if n >= 2:
                    pe.wait_ge(probT_ready, n - 1)
                for j in range(i + 1):
                    last = T.transpose(ps[:, 2 + n % 2, j * P:(j + 1) * P], prob[n % 2][:, j * P:(j + 1) * P], ident)
                last.then_inc(prob_turned, 1)
                pe.wait_ge(probT_ready, n + 1)
                if n >= 2:
                    pe.wait_ge(att_out, n - 1)
                for j in range(i + 1):
                    last = T.matmul(ps[:, 4 + n % 2, 0:P], vtok[:, j, h * DH:(h + 1) * DH], probT[n % 2][:, j, :],
                                    start=(j == 0), stop=(j == i))
                last.then_inc(att_done, 1)
            pe.wait_ge(att_out, HEADS * NT)
            T.matmul(ps[0:32, 7, 0:NDEC], relrep[0:BUCKETS + 1].rearrange("p b h -> p (b h)"), onehot[0:BUCKETS + 1, ROWW:],
                     start=True, stop=True).then_inc(dbias_done, 1)

            def key_scores(b):
                pe.wait_ge(keyT_ready, b + 1)
                for t in range(2):
                    for h in range(HEADS):
                        c = t * 32 + b * HEADS + h
                        last = T.matmul(ps[:, 4, c:c + 1], keyT[b % 2][:, HEADS * t + h, :], qT[:, h, SEQ + b:SEQ + b + 1],
                                        start=True, stop=True)
                last.then_inc(dscore_done if b == NB - 1 else dscore_part, 1)

            for b in range(NB):
                if b % 2 == 0:
                    pe.wait_ge(kv_in[b // 2], 16 * 12)
                if b >= 2:
                    pe.wait_ge(keyT_ready, b - 1)
                for t in range(2):
                    for h in range(HEADS):
                        last = T.transpose(ps[:, 2 * (b % 2) + t, h * P:(h + 1) * P],
                                           kvv[:, (7 + b // 2) % RING, b % 2, 0, t, h * DH:(h + 1) * DH], ident)
                last.then_inc(key_turned, 1)
                if b:
                    key_scores(b - 1)
            key_scores(NB - 1)
            pe.wait_ge(dscT_ready, 1)
            for t in range(2):
                T.transpose(ps[0:32, 5, t * P:(t + 1) * P], dscT[:, t].rearrange("p b h -> p (b h)"), ident)
            pe.wait_ge(qkself_ready, 1)
            T.matmul(ps[0:32, 5, NDEC - 1:NDEC], qkself.rearrange("p b h -> p (b h)"), ones[:, 0:1], start=True, stop=True).then_inc(dlog_done, 1)
            pe.wait_ge(dprob_ready, 1)
            for t in range(2):
                last = T.transpose(ps[:, 6, t * 32:(t + 1) * 32], dprob[0:32, t * P:(t + 1) * P], ident[0:32, 0:32])
            last.then_inc(dprob_turned, 1)
            pe.wait_ge(dprobT_ready, 1)
            pe.wait_ge(vrow_in, 16)
            T.matmul(ps[:, 7, 0:32], vrow[0:32], diag[0:32], start=True, stop=False, skip_group_check=True)
            for b in range(NB):
                for h in range(HEADS):
                    c = b * HEADS + h
                    for t in range(2):
                        last = T.matmul(ps[:, 7, c:c + 1], kvv[:, (7 + b // 2) % RING, b % 2, 1, t, h * DH:(h + 1) * DH],
                                        dprobT[:, t, c:c + 1], start=False, stop=(t == 1), skip_group_check=True)
                if b % 2:
                    last.then_inc(kv_used if b < NB - 1 else datt_done, 1)
            pe.wait_ge(datt_done, 1)
            pe.sem_inc(kv_used, 1)

            pe.wait_ge(att_out, HEADS * NT + 1)
            for h in range(HEADS):
                pe.wait_ge(ops_ready, h + 1)
                s = h % 2
                for t in range(NT):
                    m = NT * h + t
                    cols = slice(t * P, (t + 1) * P)
                    if m >= 2:
                        pe.wait_ge(smask_ready, m - 1)
                    for j in range(3):
                        T.matmul(ps[:, m % 2, j * P:(j + 1) * P], wl[s][j][:, cols], wl[s][j][:, cols], start=True, stop=True)
                    T.matmul(ps[:, m % 2, 3 * P:4 * P], k16[s][:, cols], q16[s][:, cols], start=True, stop=True).then_inc(lvl_done, 1)
                    if m >= 2:
                        pe.wait_ge(kdtok_ready, m - 1)
                    T.transpose(ps[:, 2 + m % 2, 0:P], kdT[s][:, cols], ident).then_inc(kd_turned, 1)
                    v_ = ib[:, t, h * DH:(h + 1) * DH]
                    pe.wait_ge(smask_ready, m + 1)
                    if m >= 2:
                        pe.wait_ge(o_out, m - 1)
                    if t:
                        pe.wait_ge(state_ready, m)
                        T.matmul(ps[:, 4 + m % 2, 0:P], qc[s][:, cols], state[:, h, :], start=True, stop=False)
                    for j in range(4):
                        T.matmul(ps[:, 4 + m % 2, 0:P], smask[m % 2][:, j, :], v_, start=(t == 0 and j == 0), stop=(j == 3))
                    pe.wait_ge(kdtok_ready, m + 1)
                    if m >= 2:
                        pe.wait_ge(state_ready, m - 1)
                    T.matmul(ps[:, 6 + m % 2, 0:P], kdtok[m % 2], v_, start=True, stop=True).then_inc(o_done, 1)
            for t in range(NT):
                pe.wait_ge(og_ready, t + 1)
                if t >= 2:
                    pe.wait_ge(og_out, t - 1)
                for h in range(HEADS):
                    last = T.transpose(ps[:, 4 + t % 2, h * P:(h + 1) * P], ostage[:, h, :], ident)
                last.then_inc(og_turned, 1)
            for b in range(NB):
                pe.wait_ge(vonly_ready, b + 1)
                if b >= 2:
                    pe.wait_ge(snew_ready, b - 1)
                T.matmul(ps[:, b % 2, :], ones[0:NB, :], vonly[0:NB], start=True, stop=True).then_inc(vb_done, 1)
            pe.wait_ge(snew_ready, NB)
            for h in range(HEADS):
                T.transpose(ps[:, 6, 32 + h * NB:32 + (h + 1) * NB], gb[0:NB, NT, h * DH:(h + 1) * DH], ident[0:NB, 0:NB])
            for b in range(NB):
                for h in range(HEADS):
                    last = T.matmul(ps[:, 6, h * NB + b:h * NB + b + 1], stv[:, b, h, :], qbT[:, h, SEQ + b:SEQ + b + 1],
                                    start=True, stop=True)
            last.then_inc(os_done, 1)
            pe.wait_ge(osq_ready, 1)
            T.matmul(ps[:, 7, 0:32], ones, osq, start=True, stop=True).then_inc(oss_done, 1)
            pe.wait_ge(cat_ready, 1)
            pe.wait_ge(og_out, NT)
            for t in range(TILES):
                n = rows_of(t)
                if t >= 2:
                    pe.wait_ge(x_added, t - 1)
                for c in range(2):
                    pe.wait_ge(wout_in[c], 16)
                    for k in range(KC):
                        last = T.matmul(ps[0:n, 4 + 2 * (t % 2) + c, :], catT[:, k, t * P:t * P + n], w1v[:, (12 + c) % RING, k, :],
                                        start=(k == 0), stop=(k == KC - 1))
                    last.then_inc(wo_done, 1)

            def products(j, halves):
                for k in range(KC):
                    for half in halves:
                        r_ = slice(half * CAP, (half + 1) * CAP)
                        last = T.matmul(ps[r_, 2 + j, :], xgT[:, k, r_], w1v[:, piece_slot(half, j), k, :],
                                        start=(k == 0), stop=(k == KC - 1))
                return last

            def results(halves):
                for c in range(2):
                    for k in range(FC):
                        for half in halves:
                            r_ = slice(half * CAP, (half + 1) * CAP)
                            last = T.matmul(ps[r_, 5 + c, :], hactT[:, k, r_], w2v[:, piece_slot(half, 2), k, c * 512:(c + 1) * 512],
                                            start=(k == 0), stop=(k == FC - 1))
                return last

            def experts(l):
                pe.wait_ge(router_in, 16 * 9)
                for t in range(TILES):
                    n = rows_of(t)
                    g = TILES * l + t
                    pe.wait_ge(hn_ready, g + 1)
                    if t >= 2:
                        pe.wait_ge(htile_ready, g - 1)
                    for k in range(KC):
                        last = T.transpose(ps[:, 2 * (t % 2) + k // 4, (k % 4) * P:(k % 4) * P + n], hall[0:n, t, k * P:(k + 1) * P],
                                           ident[0:n, 0:n])
                    last.then_inc(hn_turned, 1)
                    pe.wait_ge(htile_ready, g + 1)
                    for k in range(KC):
                        last = T.matmul(ps[0:n, 4 + t % 2, 0:NG + NE], htile[:, k, 0:n], wr[:, l, k, :], start=(k == 0), stop=(k == KC - 1))
                    last.then_inc(rlog_done, 1)
                pe.wait_ge(mem_ready, l + 1)
                for t in range(TILES):
                    out = ps[:, 6, t * NE:(t + 1) * NE]
                    T.matmul(out, tri, mem[:, t, :], start=True, stop=(t == 0))
                    for s in range(t):
                        T.matmul(out, ones, mem[:, s, :], start=False, stop=(s == t - 1))
                for t in range(TILES):
                    last = T.matmul(ps[:, 7, 0:NE], ones, mem[:, t, :], start=(t == 0), stop=(t == NT))
                last.then_inc(rank_done, 1)
                pe.wait_ge(slots_ready, l + 1)

                def turn(i, first):
                    pe.wait_ge(xg_in, 16 * PAIRS * l + 16 * i + 16)
                    if not first:
                        pe.wait_ge(xT_ready, PAIRS * l + i)
                    for k in range(KC):
                        last = T.transpose(ps[:, k // 4, (k % 4) * P:(k % 4 + 1) * P], xg[:, k * P:(k + 1) * P], ident)
                    last.then_inc(x_turned, 1)

                def pair(i, first, last):
                    pe.wait_ge(xT_ready, PAIRS * l + i + 1)
                    if not first:
                        pe.wait_ge(hact_ready, PAIRS * l + i)
                    for j in range(2):
                        for half in range(2):
                            pe.wait_ge(wt_in[piece_slot(half, j)], 16 * PAIRS * l + 16 * i + 16)
                        products(j, (0, 1)).then_inc((w1_used, h_done)[j], 1)
                    if not last:
                        turn(i + 1, False)
                    pe.wait_ge(hact_ready, PAIRS * l + i + 1)
                    if not first:
                        pe.wait_ge(hactT_ready, PAIRS * l + i)
                    for k in range(FC):
                        t_ = T.transpose(ps[:, 4, k * P:(k + 1) * P], hact[:, k * P:(k + 1) * P], ident)
                    t_.then_inc(hact_turned, 1)
                    for half in range(2):
                        pe.wait_ge(wt_in[piece_slot(half, 2)], 16 * PAIRS * l + 16 * i + 16)
                    pe.wait_ge(hactT_ready, PAIRS * l + i + 1)
                    if not first:
                        pe.wait_ge(y_out, PAIRS * l + i)
                    results((0, 1)).then_inc(y_done, 1)

                turn(0, True)
                pair(0, True, False)
                with pe.Fori(1, PAIRS - 1) as i:
                    pair(i, False, False)
                pair(PAIRS - 1, False, True)
                pe.wait_ge(y_out, PAIRS * (l + 1))
                n_over = pe.value_load(tables[l][0:1, NOV:NOV + 1], min_val=0, max_val=NOV)
                with pe.If(n_over > 0):
                    with pe.Fori(0, NOV) as j:
                        with pe.If(n_over > j):
                            pe.wait_ge(over_in[l], 64 * j + 64)
                            pe.sem_inc(over_seen, 1)
                            for k in range(KC):
                                last = T.transpose(ps[:, 0, k * CAP:(k + 1) * CAP], xg[0:CAP, k * P:(k + 1) * P], ident[0:CAP, 0:CAP])
                            last.then_inc(over_step[l], 1)
                            pe.wait_ge(over_step[l], over_count(j, COLUMNS))
                            products(0, (0,))
                            products(1, (0,)).then_inc(over_step[l], 1)
                            pe.wait_ge(over_step[l], over_count(j, GATED))
                            pe.sem_inc(over_seen, 1)
                            for k in range(FC):
                                last = T.transpose(ps[:, 4, k * CAP:(k + 1) * CAP], hact[0:CAP, k * P:(k + 1) * P], ident[0:CAP, 0:CAP])
                            last.then_inc(over_step[l], 1)
                            pe.wait_ge(over_step[l], over_count(j, ACT_COLUMNS))
                            results((0,)).then_inc(over_step[l], 1)
                        with pe.Else():
                            pe.nop()
                    pe.nop()
                with pe.Else():
                    pe.nop()
                pe.nop()

            experts(0)
            pe.wait_ge(poolw_in, 16 * NG)
            pe.wait_ge(pool_in, 16 * 4)
            for t in range(TILES):
                n = rows_of(t)
                pe.wait_ge(x_added, TILES + t + 1)
                if t:
                    pe.wait_ge(mixT_ready, t)
                for k in range(KC):
                    g = k // 2
                    out = ps[:, k // 4, (k % 4) * P:(k % 4) * P + n]
                    cols = slice(k * P, (k + 1) * P)
                    if t < NT:
                        last = T.matmul(out, hall[:, t, cols], poolc[:, 0 if t == 0 else 1, g, :], start=True, stop=(t == 0))
                        if t:
                            last = T.matmul(out, hall[:, t - 1, cols], poolc[:, 2, g, :], start=False, stop=True)
                    else:
                        T.matmul(out, prev[0:NB * KEEP, cols], poolstate[0:NB * KEEP, 0, g, :], start=True, stop=False)
                        last = T.matmul(out, hall[0:NB, t, cols], poolstate[0:NB, 1, g, :], start=False, stop=True)
                last.then_inc(mix_done, 1)
                pe.wait_ge(mixT_ready, t + 1)
                if t >= 2:
                    pe.wait_ge(x_added, 2 * TILES + t - 1)
                for g in range(NG):
                    for k in range(2):
                        last = T.matmul(ps[0:n, 2 + 2 * (t % 2) + g // 2, (g % 2) * 256:(g % 2 + 1) * 256], mixT[:, 2 * g + k, 0:n],
                                        poolw[:, g, k, :], start=(k == 0), stop=(k == 1))
                last.then_inc(pool_done, 1)
            experts(1)


_INS = ["x_prompt", "x_sample", "cache_win_k", "cache_win_v", "state_hgrn", "state_pool", "rel_bias", "norm_mix",
        "norm_ffn", "norm_final", "w_in", "w_out", "hgrn_lb", "hgrn_gnorm", "pool_w", "pool_scale", "moe_wg_group",
        "moe_bg_group", "moe_wg_exp", "moe_bg_exp", "moe_w1", "moe_w3", "moe_w2"]
_OUTS = [(1, SEQ, D), (NB, 1, D), (1, 1, SEQ, HEADS, DH), (1, 1, SEQ, HEADS, DH), (1, 1, HEADS, DH, DH), (1, 1, KEEP, D),
         (1, NB, 1, HEADS, DH), (1, NB, 1, HEADS, DH), (1, NB, HEADS, DH, DH), (1, NB, 1, D)]


def kernel(**inputs):
    import numpy as _np
    import concourse.bacc as _bacc
    from concourse import mybir as _mybir
    from concourse.bass_utils import run_bass_kernel_spmd as _run

    nc = _bacc.Bacc("TRN2", target_bir_lowering=False, num_devices=1)
    arrays, a, consts = {}, {}, {}
    for name in _INS:
        v = _np.ascontiguousarray(inputs[name])
        arrays[f"in_{name}"] = v
        a[name] = nc.dram_tensor(f"in_{name}", v.shape, _mybir.dt.from_np(v.dtype), kind="ExternalInput").ap()
    for name, v in shape_constants().items():
        arrays[name] = v
        consts[name] = nc.dram_tensor(name, v.shape, _mybir.dt.from_np(v.dtype), kind="ExternalInput").ap()
    outs = [nc.dram_tensor(f"out_{i}", s, _mybir.dt.float32, kind="ExternalOutput").ap() for i, s in enumerate(_OUTS)]
    build(nc, a, outs, consts)
    r = _run(nc, [arrays], core_ids=[0])
    return tuple(r.results[0][f"out_{i}"] for i in range(len(_OUTS)))
```

```python
from contextlib import ExitStack

import numpy as np

import concourse.bass as bass
from concourse import mybir

ALU = mybir.AluOpType
ACT = mybir.ActivationFunctionType
F32 = mybir.dt.float32
I32 = mybir.dt.int32
U32 = mybir.dt.uint32
AX = mybir.AxisListType

P = 128
D = 1024
KC = D // P
SEQ = 512
NT = SEQ // P
NB = 8
TILES = NT + 1
TOK = SEQ + NB
HEADS = 4
DH = 128
AW = HEADS * DH
NPROJ = 7 * AW
PAST = 1024
NG = 4
EPG = 8
NE = 32
FE = 512
FC = FE // P
CAP = 64
NOV = 2 * TOK // (CAP + 1)
SLOTS = (NE + NOV) * CAP
THR = (TOK + CAP - 1) // CAP
EPS = 1e-6
SCALE = DH ** -0.5
PIECE = 4096
RING = 6
NEG = -1e30
BRANCHES = ((128, 1), (512, 4), (2048, 16))
BUCKETS = 32
MAXD = 2048
WINDOWS = (2, 4, 8, 16)
KEEP = 15
LEVELS = (128, 64, 32, 16)
ROWW = 640
NDEC = 257


def rows_of(t):
    return P if t < NT else NB


def shape_constants():
    def bucket(d):
        big = 16 + np.floor(np.log(np.maximum(d, 1) / 16) / np.log(MAXD / 16) * 16).astype(np.int32)
        return np.where(d < 16, d, np.minimum(big, BUCKETS - 1))

    def columns(dist):
        dist = np.asarray(dist)
        ok = dist >= 0
        d = np.where(ok, dist, 0)
        mult = sum(((d % s == 0) & (d <= w) & ok).astype(np.int32) for w, s in BRANCHES)
        out = np.zeros((BUCKETS + 1, len(d)), np.float32)
        out[bucket(d), np.arange(len(d))] = mult > 0
        out[BUCKETS] = np.where(mult > 0, np.log(np.maximum(mult, 1)), NEG)
        return out

    prompt = columns(SEQ - 1 - np.arange(ROWW))
    p = np.arange(P)
    near = P - p
    far = np.where(p < 96, 512 - 4 * p, 1024 - 16 * (p - 96))
    decode = columns(np.concatenate([near, far, [0]]))
    onehot = np.concatenate([prompt, decode], 1)

    s, t = np.arange(P)[:, None], np.arange(P)[None, :]
    levels = []
    for n in LEVELS[:-1]:
        levels.append((s // n == t // n) & (s % n < n // 2) & (t % n >= n // 2))
    levels.append((s // 16 == t // 16) & (s <= t))
    reset = np.broadcast_to((np.arange(SEQ) % P != 0).astype(np.float32), (P, SEQ))
    one = lambda a: np.broadcast_to(np.asarray(a, np.float32), (P, len(a)))
    valid = np.stack([(p < rows_of(k)) for k in range(TILES)], 1)
    square = np.concatenate([np.eye(P), np.ones((P, P)), s < t], 1)
    small = np.concatenate([one(np.arange(NE)), one(np.arange(NE) * CAP), one((np.arange(THR) + 1) * CAP), valid,
                            np.ones((P, NE))], 1)
    masks = np.concatenate(levels + [reset], 1)

    pool = np.zeros((P, 3, len(WINDOWS), P), np.float32)
    for g, w in enumerate(WINDOWS):
        own = ((s <= t) & (t - s < w)).astype(np.float32)
        before = (P + t - s < w).astype(np.float32)
        pool[:, 0, g] = own / np.minimum(w, t + 1) - np.eye(P)
        pool[:, 1, g] = own / w - np.eye(P)
        pool[:, 2, g] = before / w
    state = np.zeros((P, 2, len(WINDOWS), NB), np.float32)
    for g, w in enumerate(WINDOWS):
        for b in range(NB):
            state[b * KEEP + KEEP - (w - 1):(b + 1) * KEEP, 0, g, b] = 1 / w
            state[b, 1, g, b] = 1 / w - 1
    pools = np.concatenate([pool.reshape(P, -1), state.reshape(P, -1)], 1)
    return {k: np.ascontiguousarray(v, dtype=np.float32) for k, v in
            (("c_onehot", onehot), ("c_square", square), ("c_small", small), ("c_masks", masks), ("c_pool", pools))}


def build(nc, a, outs, consts):
    (y_prompt, y_sample, k_prompt, v_prompt, s_prompt, p_prompt, k_sample, v_sample, s_sample, p_sample) = outs
    slot_x = nc.dram_tensor("slot_x", (SLOTS, D), F32, kind="Internal").ap()
    slot_y = nc.dram_tensor("slot_y", (SLOTS, D), F32, kind="Internal").ap()
    bias_rows = nc.dram_tensor("bias_rows", (HEADS, P, ROWW), F32, kind="Internal").ap()

    with ExitStack() as ctx:
        ring = ctx.enter_context(nc.sbuf_tensor("ring", [P, RING, PIECE], F32))
        ARENA = 28600
        arena = ctx.enter_context(nc.sbuf_tensor("arena", [P, ARENA], F32))
        ps = ctx.enter_context(nc.psum_tensor("ps", [P, 8, 512], F32))

        def sem(name):
            return ctx.enter_context(nc.semaphore(name))

        def at(lo, *shape):
            n = int(np.prod(shape))
            assert lo + n <= ARENA, (lo, shape)
            v = arena[:, lo:lo + n]
            if len(shape) == 1:
                return v
            names = "abcd"[:len(shape)]
            return v.rearrange(f"p ({' '.join(names)}) -> p {' '.join(names)}",
                               **{k: s for k, s in zip(names, shape)})

        def wide(ap, shape, axis):
            return ap.unsqueeze(axis).broadcast_to(shape)

        hT = at(0, KC, TOK)
        catT = at(0, KC, TOK)
        qT = at(4160, HEADS, TOK)
        kT = at(6240, HEADS, TOK)
        vtok = at(8320, TILES, AW)
        qbT = at(10880, HEADS, TOK)
        fT = at(12960, HEADS, TOK)
        ib = at(15040, TILES, AW)
        gb = at(17600, TILES, AW)
        xin = [at(4160 + 1024 * t, D) for t in range(TILES)]
        hrow = at(22208, D)
        gain0 = at(23232, D)
        junk = at(24256, D)
        toep = at(20160, HEADS, SEQ)
        prob = [at(22208 + 512 * i, SEQ) for i in range(2)]
        probT = [at(23232 + 512 * i, NT, P) for i in range(2)]
        relx = at(25280, HEADS)
        relrep = at(25288, NB, HEADS)
        onehot = at(25320, ROWW + NDEC)
        brow = at(26220, ROWW)
        astat = at(26862, 96)
        dscT = at(22208, 2, NB, HEADS)
        dlog = at(22272, NDEC)
        dprob = at(22532, NDEC)
        dbias = at(22792, NDEC)
        qkself = at(23052, NB, HEADS)
        diag = at(23084, 32)
        vrow = at(23116, DH)
        dprobT = at(23244, 2, 32)
        dstat = at(23310, 8)
        wl = [[ring[:, 1 + i, 512 * j:512 * (j + 1)] for j in range(3)] for i in range(2)]
        q16 = [ring[:, 1 + i, 1536:2048] for i in range(2)]
        k16 = [ring[:, 1 + i, 2048:2560] for i in range(2)]
        qc = [ring[:, 1 + i, 2560:3072] for i in range(2)]
        kdT = [ring[:, 1 + i, 3072:3584] for i in range(2)]
        lcum = at(22208, SEQ)
        ldif = at(22720, SEQ)
        lexp = at(23232, SEQ)
        kdtok = at(23744, P)
        smask = at(23872, 4, P)
        state = at(24384, HEADS, DH)
        sq = at(24256, HEADS, DH)
        ostage = at(24768, HEADS, DH)
        hstat = at(26220, 160)
        gnb = at(26380, DH)
        ktok = [qbT[:, i, 0:SEQ] for i in range(2)]
        keyT = [fT[:, 2 * i:2 * i + 2, 0:SEQ] for i in range(2)]
        vonly = [at(26970 + 512 * i, AW) for i in range(2)]
        tmp_kv = qbT[:, 2, 0:SEQ].rearrange("p (h v) -> p h v", h=HEADS)
        osq = qbT[:, 3, 0:32]
        osT = qbT[:, 3, 32:64].rearrange("p (h b) -> p h b", h=HEADS)
        gsT = qbT[:, 3, 64:96].rearrange("p (h b) -> p h b", h=HEADS)
        gncol = qbT[:, 3, 96:97]
        sstat = qbT[:, 3, 128:256]
        masks = at(26970, 4, P)
        reset = at(27482, SEQ)
        zero = gb[:, 0:2, :].rearrange("p a b -> p (a b)")
        x = at(4160, TILES, D)
        hall = at(9280, TILES, D)
        xg = at(9280, D)
        yst = at(10304, D)
        gat = [at(9280 + 1024 * i, D) for i in range(4)]
        htile = at(14400, KC, P)
        wr = at(15424, 2, KC, NG + NE)
        rbias = at(16000, 2, NG + NE)
        xgT = at(16072, KC, 2 * CAP)
        sg = at(17096, FE)
        hact = at(17608, FE)
        hactT = at(26900, FC, 2 * CAP)
        gain = [at(18120 + 1024 * i, D) for i in range(2)]
        R = 20168
        lg = at(R, TILES, NG + NE)
        g8 = at(R + 180, TILES, 8)
        gm8 = at(R + 220, TILES, 8)
        e8 = at(R + 260, TILES, 8)
        em8 = at(R + 300, TILES, 8)
        gi8 = at(R + 340, TILES, 8).bitcast(U32)
        ei8 = at(R + 380, TILES, 8).bitcast(U32)
        gsel = at(R + 420, TILES)
        g4 = at(R + 425, TILES, NG)
        eid = at(R + 445, TILES, 2)
        dexp = at(R + 455, TILES, 5)
        gden = at(R + 480, TILES)
        sel = at(R + 485, TILES, NG, EPG)
        oh = at(R + 645, TILES, 2, NE)
        mem = at(R + 965, TILES, NE)
        over = at(R + 1125, TILES, NE)
        ohs = at(R + 1285, TILES, 2, NE)
        novx = at(R + 1605, NE)
        ovend = at(R + 1637, NE)
        dbase = at(R + 1669, NE)
        ovf = at(R + 1701, NOV)
        cmp = at(R + 1725, NE, THR)
        assert THR * NE <= 320 and NOV <= 24
        poolc = at(22216, 3, len(WINDOWS), P)
        poolstate = at(22216 + 1536, 2, len(WINDOWS), NB)
        prev = at(23816, D)
        mixT = at(24840, KC, P)
        pscale = at(25864, D)
        poolw = at(0, NG, 2, 256)
        spare = at(26900, D)
        ecmp = at(2048, NOV, NE)
        C = 28000
        ident = at(C, P)
        ones = at(C + 128, P)
        tri = at(C + 256, P)
        small = at(C + 384, 2 * NE + THR + TILES + NE)
        iota = small[:, 0:NE]
        ebase = small[:, NE:2 * NE]
        thr = small[:, 2 * NE:2 * NE + THR]
        valid = small[:, 2 * NE + THR:2 * NE + THR + TILES]
        ones32 = small[:, 2 * NE + THR + TILES:]
        M = C + 384 + 3 * NE + THR + TILES
        ssq = at(M, TILES)
        rms = at(M + 5, TILES)
        gates = at(M + 10, TILES, 2)
        slotu = at(M + 20, TILES, 2).bitcast(U32)
        slotf = at(M + 30, TILES, 2)
        tables = [at(lo, NOV + 1).bitcast(I32) for lo in (M + 40, M + 85)]
        lbl = at(M + 65, 2, HEADS)
        lb = at(M + 73, HEADS)
        oml = at(M + 77, HEADS)
        lbs = at(M + 81, HEADS)
        assert M + 85 + NOV + 1 <= ARENA and NOV + 1 <= 25

        consts_in = sem("consts_in")
        masks_in = sem("masks_in")
        x_in = [sem(f"x_in{i}") for i in range(TILES)]
        gain_in = sem("gain_in")
        meansq = sem("meansq")
        root = sem("root")
        h_ready = sem("h_ready")
        h_turned = sem("h_turned")
        hT_ready = sem("hT_ready")
        w_in = [sem(f"w_in{i}") for i in range(7)]
        kv_in = [sem(f"kv_in{i}") for i in range(4)]
        kv_used = sem("kv_used")
        state_in = sem("state_in")
        wout_in = [sem(f"wout_in{i}") for i in range(2)]
        unit_done = sem("unit_done")
        unit_out = sem("unit_out")
        kt_turned = sem("kt_turned")
        ktok_ready = sem("ktok_ready")
        ktok_stored = [sem(f"ktok_stored{i}") for i in range(2)]
        stored = sem("stored")
        rel_in = sem("rel_in")
        rel_ready = sem("rel_ready")
        brow_done = sem("brow_done")
        brow_ready = sem("brow_ready")
        brow_stored = sem("brow_stored")
        toep_in = sem("toep_in")
        logit_done = sem("logit_done")
        logit_ready = sem("logit_ready")
        prob_ready = sem("prob_ready")
        prob_normed = sem("prob_normed")
        prob_turned = sem("prob_turned")
        probT_ready = sem("probT_ready")
        att_done = sem("att_done")
        att_out = sem("att_out")
        dbias_done = sem("dbias_done")
        key_turned = sem("key_turned")
        keyT_ready = sem("keyT_ready")
        dscore_done = sem("dscore_done")
        dscore_part = sem("dscore_part")
        dscT_ready = sem("dscT_ready")
        dlog_done = sem("dlog_done")
        qkself_ready = sem("qkself_ready")
        dlog_ready = sem("dlog_ready")
        dprob_exp = sem("dprob_exp")
        dprob_ready = sem("dprob_ready")
        dprob_turned = sem("dprob_turned")
        dprobT_ready = sem("dprobT_ready")
        vrow_in = sem("vrow_in")
        datt_done = sem("datt_done")
        vs_stored = sem("vs_stored")
        zeros_ready = sem("zeros_ready")
        slots_cleared = sem("slots_cleared")
        lb_in = sem("lb_in")
        lb_exp = sem("lb_exp")
        lbl_ready = sem("lbl_ready")
        f_ready = sem("f_ready")
        logf_ready = sem("logf_ready")
        dif_ready = sem("dif_ready")
        exp_ready = sem("exp_ready")
        ops_ready = sem("ops_ready")
        lvl_done = sem("lvl_done")
        smask_ready = sem("smask_ready")
        kd_turned = sem("kd_turned")
        kdtok_ready = sem("kdtok_ready")
        o_done = sem("o_done")
        o_out = sem("o_out")
        state_ready = sem("state_ready")
        state_stored = sem("state_stored")
        gn_in = sem("gn_in")
        ohead_sq = sem("ohead_sq")
        ohead_ms = sem("ohead_ms")
        ohead_root = sem("ohead_root")
        og_ready = sem("og_ready")
        og_turned = sem("og_turned")
        og_out = sem("og_out")
        vonly_ready = sem("vonly_ready")
        vb_done = sem("vb_done")
        snew_ready = sem("snew_ready")
        snew_stored = sem("snew_stored")
        os_done = sem("os_done")
        osq_ready = sem("osq_ready")
        oss_done = sem("oss_done")
        oms_ready = sem("oms_ready")
        oroot = sem("oroot")
        cat_ready = sem("cat_ready")
        mixers_done = sem("mixers_done")
        xres_in = sem("xres_in")
        wo_done = sem("wo_done")
        x_added = sem("x_added")
        router_in = sem("router_in")
        act_chain = sem("act_chain")
        dve_chain = sem("dve_chain")
        hn_ready = sem("hn_ready")
        hn_turned = sem("hn_turned")
        htile_ready = sem("htile_ready")
        rlog_done = sem("rlog_done")
        dexp_ready = sem("dexp_ready")
        gexp_ready = sem("gexp_ready")
        mem_ready = sem("mem_ready")
        rank_done = sem("rank_done")
        slots_ready = sem("slots_ready")
        scattered = sem("scattered")
        gathered = [sem(f"gathered{i}") for i in range(2)]
        gat_used = sem("gat_used")
        y_all_stored = [sem(f"y_all_stored{i}") for i in range(2)]
        pool_in = sem("pool_in")
        poolw_in = sem("poolw_in")
        mix_done = sem("mix_done")
        mixT_ready = sem("mixT_ready")
        pool_done = sem("pool_done")
        y_final = sem("y_final")

        wt_in = [sem(f"wt_in{i}") for i in range(RING)]
        w1_used = sem("w1_used")
        xg_in = sem("xg_in")
        x_turned = sem("x_turned")
        xT_ready = sem("xT_ready")
        h_done = sem("h_done")
        silu_ready = sem("silu_ready")
        hact_ready = sem("hact_ready")
        hact_turned = sem("hact_turned")
        hactT_ready = sem("hactT_ready")
        y_done = sem("y_done")
        y_out = sem("y_out")
        y_stored = sem("y_stored")
        PAIRS = NE // 2
        over_in = [sem(f"over_in{l}") for l in range(2)]
        over_step = [sem(f"over_step{l}") for l in range(2)]
        over_stored = [sem(f"over_stored{l}") for l in range(2)]
        over_seen = sem("over_seen")
        TURNED, COLUMNS, PRODUCTS, SILU, GATED, ACT_TURNED, ACT_COLUMNS, ROWS, OUT = range(1, 10)

        def over_count(j, step):
            return 9 * j + step

        ORDER = (3, 4, 5, 0, 1, 2, 6)
        QB, FB, IB, QA, KA, VA, GB = range(7)
        WOUT_SLOT = 2
        STATE_SLOT = 1
        KV_SLOT = 3
        TURNED_PARTS = (QB, FB, QA, KA)
        FIRST = 4

        UNITS = [4, 8, 13, 17, 21, 26, 31]

        def piece_slot(half, j):
            return (FIRST + 2 * j + half) % RING

        w1v = ring[:, :, :].rearrange("p s (k f) -> p s k f", k=KC)
        w2v = ring[:, :, :].rearrange("p s (k d) -> p s k d", k=FC)
        kvv = ring[:, :, :].rearrange("p s (b w t c) -> p s b w t c", b=2, w=2, t=2)
        stv = ring[:, STATE_SLOT, :].rearrange("p (b h v) -> p b h v", b=NB, h=HEADS)

        xp = a["x_prompt"].rearrange("b (t p) d -> p (b t) d", p=P)
        xs = a["x_sample"].rearrange("b t d -> (b t) d")

        def x_rows(t):
            return xp[:, t, :] if t < NT else xs

        def gate_rows(name, layer, e):
            return a[name][layer, bass.ds(e, 1), :, :].rearrange("a (k p) f -> p (a k) f", p=P)

        def slot_rows(tensor, block):
            return tensor[bass.ds(block * CAP, CAP), :]

        def chained(eng, signal):
            n = [0]

            def link(instruction):
                n[0] += 1
                instruction.then_inc(signal, 1)
                eng.wait_ge(signal, n[0])
            return link

        block = ctx.enter_context(nc.Block())

        @block.sync
        def _(sp):
            for t in range(TILES):
                sp.dma_start(xin[t][0:rows_of(t)], x_rows(t)).then_inc(x_in[t], 16)
            for c in range(7):
                if c == RING:
                    sp.wait_ge(unit_done, UNITS[0])
                col = ORDER[c] * AW
                sp.dma_start(w1v[:, c % RING], a["w_in"][0, :, col:col + AW].rearrange(
                    "(k p) f -> p k f", p=P)).then_inc(w_in[c], 16)
            for c in range(4):
                sp.wait_ge(unit_done, UNITS[KV_SLOT + c])
                for b in range(2):
                    for w, name in enumerate(("cache_win_k", "cache_win_v")):
                        src = a[name][0, 2 * c + b].rearrange("r h d -> r (h d)")
                        dst = kvv[:, (KV_SLOT + c) % RING, b, w]
                        for to, of in ((dst[:, 0, :], src[PAST - P:PAST, :]),
                                       (dst[0:96, 1, :], src[512:893:4, :]),
                                       (dst[96:P, 1, :], src[0:497:16, :])):
                            sp.dma_start(to, of).then_inc(kv_in[c], 16)
            sp.wait_ge(o_done, HEADS * NT)
            sp.dma_start(stv[:, :, :, :], a["state_hgrn"][0].rearrange("b h k v -> k b h v")).then_inc(state_in, 16)
            for c in range(2):
                if c == 1:
                    sp.wait_ge(kv_used, 1)
                sp.dma_start(w1v[:, WOUT_SLOT + c], a["w_out"][0, :, c * 512:(c + 1) * 512].rearrange(
                    "(k p) f -> p k f", p=P)).then_inc(wout_in[c], 16)

            def load(l, e, half, j, before):
                if before is not None:
                    sp.wait_ge((w1_used, h_done, y_done)[j], before)
                s = piece_slot(half, j)
                name = ("moe_w1", "moe_w3", "moe_w2")[j]
                sp.dma_start(w2v[:, s] if j == 2 else w1v[:, s], gate_rows(name, l, e)).then_inc(wt_in[s], 16)

            for l in range(2):
                for j in range(3):
                    for half in range(2):
                        if l == 0 and (half, j) == (0, 0):
                            sp.wait_ge(kv_used, 4)
                        if l == 0 and (half, j) == (1, 1):
                            sp.wait_ge(snew_stored, 16)
                        if l == 0 and (half, j) == (0, 2):
                            sp.wait_ge(wo_done, 2 * TILES)
                        load(l, half, half, j, None if l == 0 else PAIRS)
                with sp.Fori(1, PAIRS) as i:
                    for j in range(3):
                        for half in range(2):
                            load(l, 2 * i + half, half, j, PAIRS * l + i)
                sp.wait_ge(slots_ready, l + 1)
                n_over = sp.value_load(tables[l][0:1, NOV:NOV + 1], min_val=0, max_val=NOV)
                with sp.If(n_over > 0):
                    sp.wait_ge(y_done, PAIRS * (l + 1))
                    with sp.Fori(0, NOV) as j:
                        with sp.If(n_over > j):
                            e = sp.value_load(tables[l][0:1, bass.ds(j, 1)], min_val=0, max_val=NE - 1)
                            for k, name in enumerate(("moe_w1", "moe_w3", "moe_w2")):
                                s = piece_slot(0, k)
                                dst = w2v[:, s] if k == 2 else w1v[:, s]
                                sp.dma_start(dst, gate_rows(name, l, e)).then_inc(over_in[l], 16)
                            sp.wait_ge(over_step[l], over_count(j, ROWS))
                            sp.sem_inc(over_seen, 1)
                        with sp.Else():
                            sp.nop()
                    sp.nop()
                with sp.Else():
                    sp.nop()
                sp.nop()

        @block.gpsimd
        def _(pool):
            nc.gpsimd.memset(zero, 0.0).then_inc(zeros_ready, 1)
            pool.dma_start(at(26970, 4 * P + SEQ), consts["c_masks"]).then_inc(masks_in, 16)
            pool.wait_ge(brow_ready, 1)
            pool.dma_start(bias_rows, wide(brow[0:HEADS], [HEADS, P, ROWW], 1)).then_inc(brow_stored, 16)
            pool.wait_ge(brow_stored, 16)
            pool.dma_start(toep, bass.AP(bias_rows.tensor, P - 1, [[ROWW - 1, P], [P * ROWW, HEADS], [1, SEQ]])).then_inc(toep_in, 16)
            pool.wait_ge(zeros_ready, 1)
            pool.wait_ge(unit_done, UNITS[QB])
            for table, lo in ((slot_x, 0), (slot_y, NE * CAP)):
                rows = table[lo:SLOTS, :].rearrange("(p j) d -> p j d", p=P)
                pool.dma_start(rows, wide(zero, [P, rows.shape[1], D], 1)).then_inc(slots_cleared, 16)
            for l in range(2):
                pool.wait_ge(slots_ready, l + 1)
                for t in range(TILES):
                    for k in range(2):
                        n = rows_of(t)
                        pool.indirect_dma_start(
                            out=slot_x[:, :], out_offset=bass.IndirectOffsetOnAxis(ap=slotu[0:n, t, k:k + 1], axis=0),
                            in_=hall[0:n, t, :], in_offset=None).then_inc(scattered, 16)
                pool.wait_ge(y_all_stored[l], 1)
                for t in range(TILES):
                    for k in range(2):
                        n = rows_of(t)
                        g = TILES * l + t
                        if t >= 2:
                            pool.wait_ge(gat_used, g - 1)
                        pool.indirect_dma_start(
                            out=gat[2 * (t % 2) + k][0:n, :], out_offset=None, in_=slot_y[:, :],
                            in_offset=bass.IndirectOffsetOnAxis(ap=slotu[0:n, t, k:k + 1], axis=0),
                        ).then_inc(gathered[t % 2], 16)

        @block.scalar
        def _(act):
            link = chained(act, act_chain)
            act.dma_start(gain0, a["norm_mix"][0:1, :].partition_broadcast(P).rearrange("p a d -> p (a d)")).then_inc(gain_in, 16)
            act.dma_start(at(C, 384), consts["c_square"]).then_inc(consts_in, 16)
            act.dma_start(small, consts["c_small"]).then_inc(consts_in, 16)
            with nc.allow_non_contiguous_dma(reason="1024 words of the gates' lower bound, once"):
                for j in range(2):
                    act.dma_start(lbl[:, j, :], a["hgrn_lb"][j].rearrange("(h k) -> k h", k=P)).then_inc(lb_in, 16)
            act.dma_start(onehot[0:BUCKETS + 1], consts["c_onehot"]).then_inc(rel_in, 16)
            act.dma_start(relx[0:BUCKETS, :], a["rel_bias"]).then_inc(rel_in, 16)
            def roots(t, m):
                act.wait_ge(meansq, m + 1)
                nc.scalar.activation(rms[0:rows_of(t), t:t + 1], ssq[0:rows_of(t), t:t + 1], ACT.Sqrt).then_inc(root, 1)

            for t in range(TILES):
                n = rows_of(t)
                roots(t, t)
                act.wait_ge(h_turned, t + 1)
                b = 2 * (t % 2)
                nc.scalar.activation(hT[:, :, t * P:t * P + n],
                                     ps[:, b:b + 2, :].rearrange("p b (k c) -> p (b k) c", k=4)[:, :, 0:n],
                                     ACT.Copy).then_inc(hT_ready, 1)

            act.wait_ge(lbl_ready, 1)
            nc.scalar.activation(lbl, lbl, ACT.Exp).then_inc(lb_exp, 1)
            act.wait_ge(brow_stored, 16)
            act.dma_start(gnb, a["hgrn_gnorm"][0:1, :].partition_broadcast(P).rearrange("p a d -> p (a d)")).then_inc(gn_in, 16)

            def evacuate(unit):
                c = next(c for c in range(7) if unit < UNITS[c])
                m = unit - (UNITS[c - 1] if c else 0)
                act.wait_ge(unit_done, unit + 1)
                if c in TURNED_PARTS:
                    dst, fn = {QA: (qT, ACT.Copy), KA: (kT, ACT.Copy), QB: (qbT, ACT.Silu), FB: (fT, ACT.Sigmoid)}[c]
                    nc.scalar.activation(dst[:, m, 0:SEQ], ps[:, unit % 2, :], fn)
                    nc.scalar.activation(dst[:, m, SEQ:TOK], ps[:, 2, 0:NB], fn).then_inc(unit_out, 1)
                else:
                    dst, fn = {VA: (vtok, ACT.Copy), IB: (ib, ACT.Copy), GB: (gb, ACT.Silu)}[c]
                    n = rows_of(m)
                    if c == GB and m == 0:
                        act.wait_ge(slots_cleared, 32)
                    nc.scalar.activation(dst[0:n, m, :], ps[0:n, unit % 2, :], fn).then_inc(unit_out, 1)
                if unit == UNITS[VA] - 1:
                    act.wait_ge(unit_out, unit + 1)
                    act.dma_start(v_prompt.rearrange("a b (t p) h d -> p (a b t) (h d)", p=P), vtok[:, 0:NT, :]).then_inc(stored, 16)
                    act.dma_start(v_sample.rearrange("a b t h d -> (a b t) (h d)"), vtok[0:NB, NT, :]).then_inc(vs_stored, 16)

            def decays(h, part):
                if part == 0:
                    act.wait_ge(f_ready, h + 1)
                    nc.scalar.activation(ldif, fT[:, h, 0:SEQ], ACT.Ln).then_inc(logf_ready, 1)
                for step in ((0,), (1, 2), (3,), (4, 5))[part]:
                    act.wait_ge(dif_ready, 6 * h + step + 1)
                    if step < 3:
                        link(nc.scalar.activation(lexp, ldif, ACT.Abs))
                        nc.scalar.activation(lexp, lexp, ACT.Exp, scale=-1.0).then_inc(exp_ready, 1)
                    elif step == 3:
                        link(nc.scalar.activation(lexp, ldif, ACT.Exp))
                        nc.scalar.activation(ldif, ldif, ACT.Exp, scale=-1.0).then_inc(exp_ready, 1)
                    elif step == 4:
                        nc.scalar.activation(lexp, lcum, ACT.Exp).then_inc(exp_ready, 1)
                    else:
                        nc.scalar.activation(lexp, ldif, ACT.Exp, scale=-1.0).then_inc(exp_ready, 1)

            for unit in range(UNITS[IB]):
                evacuate(unit)
                if UNITS[FB] <= unit < UNITS[FB] + 4:
                    decays(0, unit - UNITS[FB])
            for unit in range(UNITS[IB], UNITS[GB]):
                m = unit - UNITS[IB]
                h, t = m // NT, m % NT
                if m < HEADS * NT:
                    act.wait_ge(kd_turned, m + 1)
                    nc.scalar.activation(kdtok, ps[:, 4, 0:P], ACT.Copy).then_inc(kdtok_ready, 1)
                    if m and t == 0:
                        act.wait_ge(state_ready, m)
                        act.dma_start(s_prompt[0, 0, h - 1], state[:, h - 1, :]).then_inc(state_stored, 16)
                    if h + 1 < HEADS:
                        decays(h + 1, t)
                evacuate(unit)
                if m < HEADS * NT:
                    act.wait_ge(o_done, m + 1)
                    nc.scalar.activation(ib[:, t, h * DH:(h + 1) * DH], ps[:, 5, 0:P], ACT.Copy).then_inc(o_out, 1)
                k = unit - UNITS[VA]
                if k >= 0:
                    n = rows_of(k)
                    act.wait_ge(kt_turned, k + 1)
                    if k == 0:
                        act.wait_ge(ops_ready, HEADS)
                    if k >= 2:
                        act.wait_ge(ktok_stored[k % 2], 16 * (k // 2))
                    nc.scalar.activation(ktok[k % 2][0:n, :], ps[0:n, 7, :], ACT.Copy).then_inc(ktok_ready, 1)
                    act.wait_ge(ktok_ready, k + 1)
                    dst = (k_prompt.rearrange("a b (t p) h d -> p (a b t) (h d)", p=P)[:, k, :] if k < NT
                           else k_sample.rearrange("a b t h d -> (a b t) (h d)"))
                    act.dma_start(dst, ktok[k % 2][0:n, :]).then_inc(ktok_stored[k % 2], 16)
            act.wait_ge(state_ready, HEADS * NT)
            act.dma_start(s_prompt[0, 0, HEADS - 1], state[:, HEADS - 1, :]).then_inc(state_stored, 16)

            def exponentials(n):
                w = (n % NT + 1) * P
                act.wait_ge(logit_ready, n + 1)
                nc.scalar.activation(prob[n % 2][:, 0:w], prob[n % 2][:, 0:w], ACT.Exp,
                                     bias=astat[:, n:n + 1], accum_out=astat[:, 16 + n:17 + n]).then_inc(prob_ready, 1)

            exponentials(0)
            for n in range(HEADS * NT):
                i = n % NT
                w = (i + 1) * P
                if n + 1 < HEADS * NT:
                    exponentials(n + 1)
                act.wait_ge(prob_turned, n + 1)
                nc.scalar.activation(probT[n % 2][:, 0:i + 1, :],
                                     ps[:, 2 + n % 2, 0:w].rearrange("p (a b) -> p a b", b=P), ACT.Copy).then_inc(probT_ready, 1)
                if n < NB:
                    act.wait_ge(key_turned, n + 1)
                    nc.scalar.activation(keyT[n % 2], ps[:, 6:8, :], ACT.Copy).then_inc(keyT_ready, 1)
                else:
                    t = n - NB
                    if t == 0:
                        act.wait_ge(state_stored, 16 * HEADS)
                    if 2 <= t < NT + 2:
                        act.wait_ge(og_turned, t - 1)
                        nc.scalar.activation(catT[:, HEADS:2 * HEADS, (t - 2) * P:(t - 1) * P],
                                             ps[:, 7, :].rearrange("p (h c) -> p h c", h=HEADS), ACT.Copy).then_inc(og_out, 1)
                    if 1 <= t < NT + 1:
                        act.wait_ge(ohead_ms, t)
                        nc.scalar.activation(hstat[:, 8 * t - 4:8 * t], hstat[:, 8 * t - 8:8 * t - 4], ACT.Sqrt).then_inc(ohead_root, 1)
                    if t < NT:
                        nc.scalar.activation(sq.rearrange("p a b -> p (a b)"), ib[:, t, :], ACT.Square).then_inc(ohead_sq, 1)
            act.wait_ge(vs_stored, 16)
            act.wait_ge(att_out, HEADS * NT)
            act.dma_start(vrow[0:32], v_sample.rearrange("a b t h d -> (a b t h) d")).then_inc(vrow_in, 16)
            act.dma_start(gncol, a["hgrn_gnorm"][0].rearrange("(k a) -> k a", a=1)).then_inc(gn_in, 16)
            act.wait_ge(snew_ready, NB)
            act.dma_start(s_sample[0].rearrange("b h k v -> k b h v"), stv[:, :, :, :]).then_inc(snew_stored, 16)
            act.wait_ge(dlog_ready, 1)
            nc.scalar.activation(dprob[0:32], dlog[0:32], ACT.Exp, bias=dstat[0:32, 0:1],
                                 accum_out=dstat[0:32, 1:2]).then_inc(dprob_exp, 1)
            act.wait_ge(oms_ready, 1)
            nc.scalar.activation(sstat[:, 32:64], sstat[:, 0:32], ACT.Sqrt).then_inc(oroot, 1)

            act.wait_ge(mixers_done, 1)
            for t in range(TILES):
                act.dma_start(x[0:rows_of(t), t, :], x_rows(t)).then_inc(xres_in, 16)
            act.dma_start(gain[1], a["norm_ffn"][0:1, :].partition_broadcast(P).rearrange("p a d -> p (a d)")).then_inc(router_in, 16)
            for l in range(2):
                act.dma_start(wr[:, l, :, 0:NG], a["moe_wg_group"][l].rearrange("(k p) g -> p k g", p=P)).then_inc(router_in, 16)
                act.dma_start(wr[:, l, :, NG:], a["moe_wg_exp"][l].rearrange("(k p) g -> p k g", p=P)).then_inc(router_in, 16)
                act.dma_start(rbias[:, l, 0:NG], a["moe_bg_group"][l:l + 1, :].partition_broadcast(P).rearrange("p a d -> p (a d)")).then_inc(router_in, 16)
                act.dma_start(rbias[:, l, NG:], a["moe_bg_exp"][l:l + 1, :].partition_broadcast(P).rearrange("p a d -> p (a d)")).then_inc(router_in, 16)
            act.dma_start(at(22216, 1536 + 64), consts["c_pool"]).then_inc(pool_in, 16)
            act.dma_start(prev[0:NB * KEEP], a["state_pool"][0].rearrange("b r d -> (b r) d")).then_inc(pool_in, 16)
            act.dma_start(pscale, a["pool_scale"].partition_broadcast(P).rearrange("p a d -> p (a d)")).then_inc(pool_in, 16)
            act.dma_start(gain[0], a["norm_mix"][1:2, :].partition_broadcast(P).rearrange("p a d -> p (a d)")).then_inc(pool_in, 16)

            def experts(l):
                for t in range(TILES):
                    m = TILES * (1 if l == 0 else 3) + t
                    g = TILES * l + t
                    roots(t, m)
                    n = rows_of(t)
                    act.wait_ge(hn_turned, g + 1)
                    if g:
                        act.wait_ge(rlog_done, g)
                    b = 2 * (t % 2)
                    nc.scalar.activation(htile[:, :, 0:n],
                                         ps[:, b:b + 2, :].rearrange("p b (k c) -> p (b k) c", k=4)[:, :, 0:n],
                                         ACT.Copy).then_inc(htile_ready, 1)
                act.wait_ge(dexp_ready, l + 1)
                nc.scalar.activation(dexp, dexp, ACT.Exp).then_inc(gexp_ready, 1)
                def load_rows(i):
                    act.dma_start(xg, slot_x[bass.ds(i * 2 * CAP, 2 * CAP), :]).then_inc(xg_in, 16)

                def pair(i, first, last):
                    if not last:
                        act.wait_ge(x_turned, PAIRS * l + i + 1)
                        load_rows(i + 1)
                    act.wait_ge(h_done, PAIRS * l + i + 1)
                    nc.scalar.activation(sg, ps[:, 2, :], ACT.Silu).then_inc(silu_ready, 1)
                    act.wait_ge(y_done, PAIRS * l + i + 1)
                    if not first:
                        act.wait_ge(y_stored, 16 * PAIRS * l + 16 * i)
                    nc.scalar.activation(yst, ps[:, 5:7, :].rearrange("p a b -> p (a b)"), ACT.Copy).then_inc(y_out, 1)
                    act.wait_ge(y_out, PAIRS * l + i + 1)
                    act.dma_start(slot_y[bass.ds(i * 2 * CAP, 2 * CAP), :], yst).then_inc(y_stored, 16)

                act.wait_ge(scattered, 16 * 2 * TILES * (l + 1))
                load_rows(0)
                pair(0, True, False)
                with act.Fori(1, PAIRS - 1) as i:
                    pair(i, False, False)
                pair(PAIRS - 1, False, True)
                act.wait_ge(y_stored, 16 * PAIRS * (l + 1))
                n_over = act.value_load(tables[l][0:1, NOV:NOV + 1], min_val=0, max_val=NOV)
                with act.If(n_over > 0):
                    with act.Fori(0, NOV) as j:
                        with act.If(n_over > j):
                            act.dma_start(xg[0:CAP, :], slot_rows(slot_x, NE + j)).then_inc(over_in[l], 16)
                            act.wait_ge(over_step[l], over_count(j, PRODUCTS))
                            nc.scalar.activation(sg[0:CAP], ps[0:CAP, 2, :], ACT.Silu).then_inc(over_step[l], 1)
                            act.wait_ge(over_step[l], over_count(j, ROWS))
                            nc.scalar.activation(yst[0:CAP, :], ps[0:CAP, 5:7, :].rearrange("p a b -> p (a b)"),
                                                 ACT.Copy).then_inc(over_step[l], 1)
                            act.wait_ge(over_step[l], over_count(j, OUT))
                            act.dma_start(slot_rows(slot_y, NE + j), yst[0:CAP, :]).then_inc(over_stored[l], 16)
                            act.wait_ge(over_stored[l], 16 * j + 16)
                            act.sem_inc(over_seen, 1)
                        with act.Else():
                            act.nop()
                    act.nop()
                with act.Else():
                    act.nop()
                act.sem_inc(y_all_stored[l], 1)

            act.wait_ge(wo_done, 2 * TILES)
            for g in range(NG):
                act.dma_start(poolw[:, g], a["pool_w"][0, g].rearrange("(k p) c -> p k c", p=P)).then_inc(poolw_in, 16)
            experts(0)
            for t in range(TILES):
                m = 2 * TILES + t
                roots(t, m)
            for t in range(TILES):
                n = rows_of(t)
                act.wait_ge(mix_done, t + 1)
                if t:
                    act.wait_ge(pool_done, t)
                nc.scalar.activation(mixT[:, :, 0:n],
                                     ps[:, 0:2, :].rearrange("p b (k c) -> p (b k) c", k=4)[:, :, 0:n],
                                     ACT.Copy).then_inc(mixT_ready, 1)
                if t == NT - 1:
                    act.dma_start(p_prompt[0, 0], hall[P - KEEP:P, t, :]).then_inc(stored, 16)
                if t == NT:
                    act.dma_start(p_sample[0].rearrange("b t d -> (b t) d"), hall[0:NB, t, :]).then_inc(stored, 16)
            act.wait_ge(x_added, 3 * TILES)
            act.dma_start(gain[1], a["norm_ffn"][1:2, :].partition_broadcast(P).rearrange("p a d -> p (a d)")).then_inc(router_in, 16)
            act.dma_start(gain[0], a["norm_final"].rearrange("(a d) -> a d", a=1).partition_broadcast(P).rearrange("p a d -> p (a d)")).then_inc(router_in, 16)
            act.wait_ge(stored, 16 * 3)
            act.sem_inc(y_final, 1)
            experts(1)
            for t in range(TILES):
                m = 4 * TILES + t
                roots(t, m)
                act.wait_ge(y_final, t + 2)
                dst = y_prompt.rearrange("b (t p) d -> p (b t) d", p=P)[:, t, :] if t < NT else y_sample.rearrange("b t d -> (b t) d")
                act.dma_start(dst, x[0:rows_of(t), t, :]).then_inc(stored, 16)
            act.wait_ge(stored, 16 * (3 + TILES))
            act.wait_ge(vs_stored, 16)
            for i in range(2):
                act.wait_ge(ktok_stored[i], 16 * len(range(i, TILES, 2)))
            act.wait_ge(state_stored, 16 * HEADS)
            act.wait_ge(snew_stored, 16)

        @block.vector
        def _(dve):
            link = chained(dve, dve_chain)
            V = nc.vector

            def norm(x_of, h_of, gain_of, count, before=None, after=None):
                def squares(t):
                    n = rows_of(t)
                    if before:
                        before(t)
                    link(V.tensor_tensor_reduce(junk_of[0][0:n], x_of(t), x_of(t), 1.0, 0.0, ALU.mult, ALU.add,
                                                ssq[0:n, t:t + 1]))
                    V.tensor_scalar(ssq[0:n, t:t + 1], ssq[0:n, t:t + 1], 1.0 / D, EPS, ALU.mult, ALU.add).then_inc(meansq, 1)

                def scaled(t):
                    n = rows_of(t)
                    dve.wait_ge(root, count + t + 1)
                    link(V.reciprocal(rms[0:n, t:t + 1], rms[0:n, t:t + 1]))
                    if after:
                        after(t)
                    return V.scalar_tensor_tensor(h_of(t), x_of(t), rms[0:n, t:t + 1], gain_of[0:n], ALU.mult, ALU.mult)
                return squares, scaled

            junk_of = [junk]
            squares, scaled = norm(
                lambda t: xin[t][0:rows_of(t)], lambda t: hrow[0:rows_of(t)], gain0, 0,
                before=lambda t: dve.wait_ge(x_in[t], 16),
                after=lambda t: dve.wait_ge(h_turned, t) if t else dve.wait_ge(gain_in, 16))
            squares(0)
            for t in range(TILES):
                if t + 1 < TILES:
                    if t + 1 < TILES:
                        squares(t + 1)
                scaled(t).then_inc(h_ready, 1)
            dve.wait_ge(rel_in, 32)
            V.memset(relx[BUCKETS:BUCKETS + 1, :], 1.0).then_inc(rel_ready, 1)
            dve.wait_ge(rel_ready, 1)
            V.tensor_copy(relrep[0:BUCKETS + 1], wide(relx[0:BUCKETS + 1, :], [BUCKETS + 1, NB, HEADS], 1)).then_inc(rel_ready, 1)
            dve.wait_ge(brow_done, 1)
            V.tensor_copy(brow[0:HEADS], ps[0:HEADS, 6:8, :].rearrange("p a b -> p (a b)")[:, 0:ROWW]).then_inc(brow_ready, 1)
            dve.wait_ge(lb_in, 32)
            link(V.tensor_tensor(lbs, lbl[:, 0, :], lbl[:, 1, :], ALU.max))
            V.tensor_tensor(lbl, lbl, wide(lbs, [P, 2, HEADS], 1), ALU.subtract).then_inc(lbl_ready, 1)

            dve.wait_ge(lb_exp, 1)
            link(V.tensor_tensor(lbs, lbl[:, 0, :], lbl[:, 1, :], ALU.add))
            link(V.reciprocal(lbs, lbs))
            link(V.tensor_tensor(lb, lbl[:, 0, :], lbs, ALU.mult))
            link(V.tensor_scalar(oml, lb, -1.0, 1.0, ALU.mult, ALU.add))
            dve.wait_ge(masks_in, 16)
            dve.wait_ge(brow_stored, 16)
            dve.wait_ge(unit_out, UNITS[FB])

            def blocks(ap, n):
                return ap.rearrange("p (b n) -> p b n", n=n)

            def operands(h, part):
                q_ = qbT[:, h, 0:SEQ]
                f_ = fT[:, h, 0:SEQ]
                s = h % 2

                def differ(n, at_):
                    V.tensor_tensor(blocks(ldif, n), blocks(lcum, n),
                                    blocks(lcum, n)[:, :, at_:at_ + 1].broadcast_to([P, SEQ // n, n]), ALU.subtract).then_inc(dif_ready, 1)

                def exped(step):
                    dve.wait_ge(exp_ready, 6 * h + step + 1)

                def level(j):
                    n = LEVELS[j]
                    differ(n, n // 2 - 1)
                    exped(j)
                    w_, e_ = blocks(wl[s][j], n), blocks(lexp, n)
                    V.tensor_tensor(w_[:, :, n // 2:], blocks(q_, n)[:, :, n // 2:], e_[:, :, n // 2:], ALU.mult)
                    link(V.tensor_tensor(w_[:, :, :n // 2], blocks(f_, n)[:, :, :n // 2], e_[:, :, :n // 2], ALU.mult))

                if part == 0:
                    V.tensor_scalar(fT[:, h, :], fT[:, h, :], oml[:, h:h + 1], lb[:, h:h + 1], ALU.mult, ALU.add).then_inc(f_ready, 1)
                    dve.wait_ge(logf_ready, h + 1)
                    link(V.tensor_tensor_scan(lcum, reset, ldif, 0.0, ALU.mult, ALU.add))
                    link(V.tensor_scalar(f_, f_, -1.0, 1.0, ALU.mult, ALU.add))
                    if h >= 2:
                        dve.wait_ge(o_done, NT * (h - 1))
                    level(0)
                elif part == 1:
                    level(1)
                    level(2)
                elif part == 2:
                    differ(16, 7)
                    exped(3)
                    link(V.tensor_tensor(q16[s], q_, lexp, ALU.mult))
                    link(V.tensor_tensor(k16[s], f_, ldif, ALU.mult))
                else:
                    dve.sem_inc(dif_ready, 1)
                    exped(4)
                    link(V.tensor_tensor(qc[s], q_, lexp, ALU.mult))
                    link(V.tensor_copy(hstat[:, 64 + 4 * h:68 + 4 * h].unsqueeze(2), blocks(lexp, P)[:, :, P - 1:P]))
                    differ(P, P - 1)
                    exped(5)
                    V.tensor_tensor(kdT[s], f_, lexp, ALU.mult).then_inc(ops_ready, 1)
                    dve.wait_ge(ops_ready, h + 1)

            for part in range(4):
                operands(0, part)
            for h in range(HEADS):
                for t in range(NT):
                    m = NT * h + t
                    dve.wait_ge(lvl_done, m + 1)
                    V.scalar_tensor_tensor(smask.rearrange("p a b -> p (a b)"), ps[:, 3, :], 3e38,
                                           masks.rearrange("p a b -> p (a b)"), ALU.min, ALU.mult).then_inc(smask_ready, 1)
                    if h + 1 < HEADS:
                        if m == 0:
                            dve.wait_ge(unit_done, UNITS[IB])
                        operands(h + 1, t)
                    dve.wait_ge(o_done, m + 1)
                    new = ps[:, 6, 0:P]
                    if t == 0:
                        V.tensor_copy(state[:, h, :], new).then_inc(state_ready, 1)
                    else:
                        dve.wait_ge(state_ready, m)
                        V.scalar_tensor_tensor(state[:, h, :], state[:, h, :], hstat[:, 64 + 4 * h + t:65 + 4 * h + t], new,
                                               ALU.mult, ALU.add).then_inc(state_ready, 1)
            def logits(n):
                h, i = n // NT, n % NT
                w = (i + 1) * P
                dve.wait_ge(logit_done, n + 1)
                if n >= 2:
                    dve.wait_ge(prob_turned, n - 1)
                if n == 0:
                    dve.wait_ge(toep_in, 16)
                link(V.scalar_tensor_tensor(prob[n % 2][:, 0:w], ps[:, n % 2, 0:w], SCALE, toep[:, h, SEQ - w:SEQ], ALU.mult, ALU.add))
                V.tensor_reduce(astat[:, n:n + 1], prob[n % 2][:, 0:w], AX.X, ALU.max, negate=True).then_inc(logit_ready, 1)

            def normed(n):
                w = (n % NT + 1) * P
                dve.wait_ge(prob_ready, n + 1)
                link(V.reciprocal(astat[:, 32 + n:33 + n], astat[:, 16 + n:17 + n]))
                V.tensor_scalar(prob[n % 2][:, 0:w], prob[n % 2][:, 0:w], astat[:, 32 + n:33 + n], None, ALU.mult).then_inc(prob_normed, 1)

            def out_heads(n):
                h, i = n // NT, n % NT
                dve.wait_ge(att_done, n + 1)
                V.tensor_copy(catT[:, h, i * P:(i + 1) * P], ps[:, 4, 0:P]).then_inc(att_out, 1)

            def head_squares(t):
                dve.wait_ge(ohead_sq, t + 1)
                link(V.tensor_reduce(hstat[:, 8 * t:8 * t + 4], sq, AX.X, ALU.add))
                V.tensor_scalar(hstat[:, 8 * t:8 * t + 4], hstat[:, 8 * t:8 * t + 4], 1.0 / DH, EPS, ALU.mult, ALU.add).then_inc(ohead_ms, 1)

            def head_scaled(t):
                dve.wait_ge(ohead_root, t + 1)
                r_ = hstat[:, 8 * t + 4:8 * t + 8]
                link(V.reciprocal(r_, r_))
                if t:
                    dve.wait_ge(og_turned, t)
                o_ = ib[:, t, :].rearrange("p (h v) -> p h v", h=HEADS)
                link(V.tensor_tensor(ostage, o_, wide(r_, [P, HEADS, DH], 2), ALU.mult))
                link(V.tensor_tensor(ostage, ostage, wide(gnb, [P, HEADS, DH], 1), ALU.mult))
                V.tensor_tensor(ostage.rearrange("p h v -> p (h v)"), ostage.rearrange("p h v -> p (h v)"), gb[:, t, :],
                                ALU.mult).then_inc(og_ready, 1)

            fs = fT[:, :, SEQ:TOK]
            ks = sstat[:, 64:96].rearrange("p (h b) -> p h b", h=HEADS)

            def value_of(b):
                if b >= 2:
                    dve.wait_ge(vb_done, b - 1)
                V.tensor_scalar(vonly[b % 2][0:NB], ib[0:NB, NT, :], ident[0:NB, b:b + 1], None, ALU.mult).then_inc(vonly_ready, 1)

            def sample_state(b):
                if b == 0:
                    dve.wait_ge(state_in, 16)
                V.tensor_tensor(stv[:, b], stv[:, b], fs[:, :, b:b + 1].broadcast_to([P, HEADS, DH]), ALU.mult)
                dve.wait_ge(vb_done, b + 1)
                link(V.tensor_tensor(tmp_kv, ps[:, 6, :].rearrange("p (h v) -> p h v", h=HEADS),
                                     ks[:, :, b:b + 1].broadcast_to([P, HEADS, DH]), ALU.mult))
                V.tensor_tensor(stv[:, b], stv[:, b], tmp_kv, ALU.add).then_inc(snew_ready, 1)
                dve.wait_ge(snew_ready, b + 1)

            link(V.tensor_scalar(ks, fs, -1.0, 1.0, ALU.mult, ALU.add))
            dve.wait_ge(unit_out, UNITS[GB])
            logits(0)
            for n in range(HEADS * NT):
                if n + 1 < HEADS * NT:
                    logits(n + 1)
                normed(n)
                if n:
                    out_heads(n - 1)
                t = n - NB
                if t == -1:
                    dve.wait_ge(gn_in, 16)
                    value_of(0)
                if t >= 0:
                    if t < NT:
                        head_squares(t)
                    if 1 <= t < NT + 1:
                        head_scaled(t - 1)
                    if t + 1 < NB:
                        value_of(t + 1)
                    sample_state(t)
            out_heads(HEADS * NT - 1)
            dve.wait_ge(att_out, HEADS * NT)
            V.tensor_tensor(qkself.rearrange("p b h -> p h b"), qT[:, :, SEQ:TOK], kT[:, :, SEQ:TOK], ALU.mult).then_inc(qkself_ready, 1)
            dve.wait_ge(dbias_done, 1)
            link(V.tensor_copy(dbias[0:32], ps[0:32, 7, 0:NDEC]))
            dve.wait_ge(dscore_done, 1)
            V.tensor_copy(dscT.rearrange("p t b h -> p (t b h)"), ps[:, 5, 0:64]).then_inc(dscT_ready, 1)
            dve.wait_ge(dlog_done, 1)
            link(V.scalar_tensor_tensor(dlog[0:32], ps[0:32, 4, 0:NDEC], SCALE, dbias[0:32], ALU.mult, ALU.add))
            V.tensor_reduce(dstat[0:32, 0:1], dlog[0:32], AX.X, ALU.max, negate=True).then_inc(dlog_ready, 1)
            dve.wait_ge(dprob_exp, 1)
            link(V.reciprocal(dstat[0:32, 2:3], dstat[0:32, 1:2]))
            link(V.tensor_scalar(dprob[0:32], dprob[0:32], dstat[0:32, 2:3], None, ALU.mult))
            V.tensor_scalar(diag[0:32], ident[0:32, 0:32], dprob[0:32, NDEC - 1:NDEC], None, ALU.mult).then_inc(dprob_ready, 1)
            dve.wait_ge(dprob_turned, 1)
            V.tensor_copy(dprobT.rearrange("p t c -> p (t c)"), ps[:, 6, 0:64]).then_inc(dprobT_ready, 1)
            dve.wait_ge(datt_done, 1)
            V.tensor_copy(catT[:, 0:HEADS, SEQ:TOK], ps[:, 7, 0:32].rearrange("p (b h) -> p h b", b=NB)).then_inc(att_out, 1)

            dve.wait_ge(os_done, 1)
            link(V.tensor_copy(osT.rearrange("p h b -> p (h b)"), ps[:, 0, 0:32]))
            V.tensor_tensor(osq, osT.rearrange("p h b -> p (h b)"), osT.rearrange("p h b -> p (h b)"), ALU.mult).then_inc(osq_ready, 1)
            link(V.tensor_copy(gsT.rearrange("p h b -> p (h b)"), ps[:, 0, 32:64]))
            dve.wait_ge(oss_done, 1)
            V.tensor_scalar(sstat[:, 0:32], ps[:, 1, 0:32], 1.0 / DH, EPS, ALU.mult, ALU.add).then_inc(oms_ready, 1)
            dve.wait_ge(oroot, 1)
            link(V.reciprocal(sstat[:, 32:64], sstat[:, 32:64]))
            dve.wait_ge(gn_in, 32)
            link(V.scalar_tensor_tensor(osT.rearrange("p h b -> p (h b)"), osT.rearrange("p h b -> p (h b)"), gncol[:, 0:1],
                                        sstat[:, 32:64], ALU.mult, ALU.mult))
            V.tensor_tensor(catT[:, HEADS:, SEQ:TOK], osT, gsT, ALU.mult).then_inc(cat_ready, 1)
            dve.wait_ge(cat_ready, 1)
            dve.wait_ge(og_out, NT)
            dve.wait_ge(state_stored, 16 * HEADS)
            dve.wait_ge(stored, 16)
            dve.wait_ge(vs_stored, 16)
            for i in range(2):
                dve.wait_ge(ktok_stored[i], 16 * len(range(i, TILES, 2)))
            dve.sem_inc(mixers_done, 1)
            for t in range(TILES):
                n = rows_of(t)
                dve.wait_ge(wo_done, 2 * (t + 1))
                if t == 0:
                    dve.wait_ge(xres_in, 16 * TILES)
                b = 4 + 2 * (t % 2)
                V.tensor_tensor(x[0:n, t, :], x[0:n, t, :], ps[0:n, b:b + 2, :].rearrange("p a b -> p (a b)"), ALU.add).then_inc(x_added, 1)

            def experts(l):
                squares, scaled = norm(lambda t: x[0:rows_of(t), t, :], lambda t: hall[0:rows_of(t), t, :], gain[1],
                                       TILES * (1 if l == 0 else 3))
                junk_of[0] = spare
                link(V.memset(lg, 0.0))
                link(V.memset(g8, NEG))
                if l == 0:
                    dve.wait_ge(router_in, 16 * 9)
                    dve.wait_ge(pool_in, 16 * 4)
                else:
                    dve.wait_ge(router_in, 16 * 11)
                    dve.wait_ge(y_final, 1)

                def logit(t):
                    n = rows_of(t)
                    dve.wait_ge(rlog_done, TILES * l + t + 1)
                    link(V.tensor_tensor(lg[0:n, t, :], ps[0:n, 4 + t % 2, 0:NG + NE], rbias[0:n, l, :], ALU.add))

                dve.wait_ge(x_added, TILES * (1 if l == 0 else 3))
                squares(0)
                for t in range(TILES):
                    if t + 1 < TILES:
                        squares(t + 1)
                    scaled(t).then_inc(hn_ready, 1)
                    if t:
                        logit(t - 1)
                logit(NT)
                link(V.tensor_copy(g8[:, :, 0:NG], lg[:, :, 0:NG]))
                for t in range(TILES):
                    link(V.max(gm8[:, t, :], g8[:, t, :]))
                    link(V.max_index(gi8[:, t, :], gm8[:, t, :], g8[:, t, :]))
                link(V.tensor_copy(gsel.unsqueeze(2), gi8[:, :, 0:1]))
                link(V.tensor_tensor(g4, wide(iota[:, 0:NG], [P, TILES, NG], 1), wide(gsel, [P, TILES, NG], 2), ALU.is_equal))
                for t in range(TILES):
                    link(V.tensor_tensor(sel[:, t], lg[:, t, NG:].rearrange("p (g e) -> p g e", g=NG),
                                         wide(g4[:, t, :], [P, NG, EPG], 2), ALU.mult))
                for t in range(TILES):
                    link(V.tensor_reduce(e8[:, t, :], sel[:, t].rearrange("p g e -> p e g"), AX.X, ALU.add))
                for t in range(TILES):
                    link(V.max(em8[:, t, :], e8[:, t, :]))
                    link(V.max_index(ei8[:, t, :], em8[:, t, :], e8[:, t, :]))
                link(V.tensor_tensor(dexp[:, :, 0:NG], lg[:, :, 0:NG], gm8[:, :, 0:1].broadcast_to([P, TILES, NG]), ALU.subtract))
                V.tensor_tensor(dexp[:, :, NG:NG + 1], em8[:, :, 1:2], em8[:, :, 0:1], ALU.subtract).then_inc(dexp_ready, 1)
                link(V.tensor_copy(eid, ei8[:, :, 0:2]))
                link(V.scalar_tensor_tensor(eid, wide(gsel, [P, TILES, 2], 2), float(EPG), eid, ALU.mult, ALU.add))
                for t in range(TILES):
                    link(V.tensor_tensor(oh[:, t], wide(iota, [P, 2, NE], 1), wide(eid[:, t, :], [P, 2, NE], 2), ALU.is_equal))
                link(V.tensor_tensor(mem, oh[:, :, 0, :], oh[:, :, 1, :], ALU.add))
                V.tensor_tensor(mem, mem, wide(valid, [P, TILES, NE], 2), ALU.mult).then_inc(mem_ready, 1)
                dve.wait_ge(gexp_ready, l + 1)
                link(V.tensor_reduce(gden, dexp[:, :, 0:NG], AX.X, ALU.add))
                w_ = dexp[:, :, NG:NG + 1]
                link(V.tensor_scalar(gates[:, :, 1:2], w_, 1.0, None, ALU.add))
                link(V.tensor_tensor(gates[:, :, 1:2], gates[:, :, 1:2], gden.unsqueeze(2), ALU.mult))
                link(V.reciprocal(gates[:, :, 0:1], gates[:, :, 1:2]))
                link(V.tensor_tensor(gates[:, :, 1:2], gates[:, :, 0:1], w_, ALU.mult))
                dve.wait_ge(rank_done, l + 1)
                rank = ps[:, 6, 0:TILES * NE].rearrange("p (t e) -> p t e", e=NE)
                count = ps[:, 7, 0:NE]
                link(V.tensor_tensor(cmp, wide(count, [P, NE, THR], 2), wide(thr, [P, NE, THR], 1), ALU.is_gt))
                link(V.tensor_reduce(novx, cmp, AX.X, ALU.add))
                link(V.tensor_tensor_scan(ovend, ones32, novx, 0.0, ALU.mult, ALU.add))
                link(V.tensor_tensor(dbase, ovend, novx, ALU.subtract))
                link(V.tensor_scalar(dbase, dbase, float(CAP), float((NE - 1) * CAP), ALU.mult, ALU.add))
                link(V.tensor_tensor(dbase, dbase, ebase, ALU.subtract))
                link(V.tensor_scalar(over, rank, float(CAP), None, ALU.is_ge))
                link(V.tensor_tensor(over, over, wide(dbase, [P, TILES, NE], 1), ALU.mult))
                link(V.tensor_tensor(over, over, rank, ALU.add))
                link(V.tensor_tensor(over, over, wide(ebase, [P, TILES, NE], 1), ALU.add))
                for k in range(2):
                    link(V.tensor_tensor(ohs[:, :, k, :], oh[:, :, k, :], over, ALU.mult))
                link(V.tensor_reduce(slotf, ohs, AX.X, ALU.add))
                link(V.tensor_copy(slotu, slotf))
                link(V.tensor_tensor(ecmp, wide(ovend, [P, NOV, NE], 1), wide(small[:, 0:NOV], [P, NOV, NE], 2), ALU.is_le))
                link(V.tensor_reduce(ovf, ecmp, AX.X, ALU.add))
                link(V.tensor_scalar(ovf, ovf, float(NE - 1), None, ALU.min))
                link(V.tensor_copy(tables[l][:, 0:NOV], ovf))
                V.tensor_copy(tables[l][:, NOV:NOV + 1], ovend[:, NE - 1:NE]).then_inc(slots_ready, 1)

                def gated(i, first):
                    dve.wait_ge(silu_ready, PAIRS * l + i + 1)
                    if not first:
                        dve.wait_ge(hact_turned, PAIRS * l + i)
                    V.tensor_tensor(hact, sg, ps[:, 3, :], ALU.mult).then_inc(hact_ready, 1)
                    dve.wait_ge(hact_turned, PAIRS * l + i + 1)
                    if not first:
                        dve.wait_ge(y_done, PAIRS * l + i)
                    V.tensor_copy(hactT.rearrange("p k c -> p (k c)"), ps[:, 4, :]).then_inc(hactT_ready, 1)

                def columns(i, first):
                    dve.wait_ge(x_turned, PAIRS * l + i + 1)
                    if not first:
                        dve.wait_ge(h_done, PAIRS * l + i)
                    V.tensor_copy(xgT.rearrange("p k c -> p (k c)"), ps[:, 0:2, :].rearrange("p a b -> p (a b)")).then_inc(xT_ready, 1)

                columns(0, True)
                gated(0, True)
                columns(1, False)
                with dve.Fori(1, PAIRS - 1) as i:
                    gated(i, False)
                    columns(i + 1, False)
                gated(PAIRS - 1, False)
                n_over = dve.value_load(tables[l][0:1, NOV:NOV + 1], min_val=0, max_val=NOV)
                with dve.If(n_over > 0):
                    with dve.Fori(0, NOV) as j:
                        with dve.If(n_over > j):
                            dve.wait_ge(over_step[l], over_count(j, TURNED))
                            V.tensor_copy(xgT[:, :, 0:CAP], ps[:, 0, :].rearrange("p (k c) -> p k c", k=KC)).then_inc(over_step[l], 1)
                            dve.wait_ge(over_step[l], over_count(j, SILU))
                            V.tensor_tensor(hact[0:CAP], sg[0:CAP], ps[0:CAP, 3, :], ALU.mult).then_inc(over_step[l], 1)
                            dve.wait_ge(over_step[l], over_count(j, ACT_TURNED))
                            V.tensor_copy(hactT[:, :, 0:CAP], ps[:, 4, 0:FC * CAP].rearrange("p (k c) -> p k c", k=FC)).then_inc(over_step[l], 1)
                        with dve.Else():
                            dve.nop()
                    dve.nop()
                with dve.Else():
                    dve.nop()
                for t in range(TILES):
                    n = rows_of(t)
                    g = TILES * l + t
                    uses = len(range(t % 2, TILES, 2)) * l + t // 2 + 1
                    dve.wait_ge(gathered[t % 2], 32 * uses)
                    link(V.scalar_tensor_tensor(x[0:n, t, :], gat[2 * (t % 2)][0:n], gates[0:n, t, 0:1], x[0:n, t, :], ALU.mult, ALU.add))
                    V.scalar_tensor_tensor(x[0:n, t, :], gat[2 * (t % 2) + 1][0:n], gates[0:n, t, 1:2], x[0:n, t, :],
                                           ALU.mult, ALU.add).then_inc(gat_used, 1)
                dve.wait_ge(gat_used, TILES * (l + 1))

            experts(0)
            squares, scaled = norm(lambda t: x[0:rows_of(t), t, :], lambda t: hall[0:rows_of(t), t, :], gain[0], 2 * TILES)
            squares(0)
            for t in range(TILES):
                if t + 1 < TILES:
                    squares(t + 1)
                scaled(t).then_inc(x_added, 1)
            for t in range(TILES):
                n = rows_of(t)
                dve.wait_ge(pool_done, t + 1)
                b = 2 + 2 * (t % 2)
                link(V.tensor_tensor(spare[0:n], ps[0:n, b:b + 2, :].rearrange("p a b -> p (a b)"), pscale[0:n], ALU.mult))
                V.tensor_tensor(x[0:n, t, :], x[0:n, t, :], spare[0:n], ALU.add).then_inc(x_added, 1)
                dve.wait_ge(x_added, 2 * TILES + t + 1)
            experts(1)
            junk_of[0] = spare
            squares, scaled = norm(lambda t: x[0:rows_of(t), t, :], lambda t: x[0:rows_of(t), t, :], gain[0], 4 * TILES)
            squares(0)
            for t in range(TILES):
                if t + 1 < TILES:
                    squares(t + 1)
                scaled(t).then_inc(y_final, 1)

        @block.tensor
        def _(pe):
            T = nc.tensor
            pe.wait_ge(consts_in, 32)
            for t in range(TILES):
                n = rows_of(t)
                pe.wait_ge(h_ready, t + 1)
                if t >= 2:
                    pe.wait_ge(hT_ready, t - 1)
                for k in range(KC):
                    last = T.transpose(ps[:, 2 * (t % 2) + k // 4, (k % 4) * P:(k % 4) * P + n], hrow[0:n, k * P:(k + 1) * P], ident[0:n, 0:n])
                last.then_inc(h_turned, 1)
            pe.wait_ge(rel_ready, 2)
            for j, (lo, hi) in enumerate(((0, 512), (512, ROWW))):
                last = T.matmul(ps[0:HEADS, 6 + j, 0:hi - lo], relx[0:BUCKETS + 1, :], onehot[0:BUCKETS + 1, lo:hi], start=True, stop=True)
            last.then_inc(brow_done, 1)
            pe.wait_ge(hT_ready, TILES)
            def project(unit):
                c = next(c for c in range(7) if unit < UNITS[c])
                m = unit - (UNITS[c - 1] if c else 0)
                slot = c % RING
                pe.wait_ge(w_in[c], 16)
                if unit >= 2:
                    pe.wait_ge(unit_out, unit - 1)
                if c in TURNED_PARTS:
                    w_ = w1v[:, slot, :, m * P:(m + 1) * P]
                    for k in range(KC):
                        T.matmul(ps[:, unit % 2, :], w_[:, k], hT[:, k, 0:SEQ], start=(k == 0), stop=(k == KC - 1))
                    if unit:
                        pe.wait_ge(unit_out, unit)
                    for k in range(KC):
                        last = T.matmul(ps[:, 2, 0:NB], w_[:, k], hT[:, k, SEQ:TOK], start=(k == 0), stop=(k == KC - 1))
                else:
                    n = rows_of(m)
                    for k in range(KC):
                        last = T.matmul(ps[0:n, unit % 2, :], hT[:, k, m * P:m * P + n], w1v[:, slot, k, :],
                                        start=(k == 0), stop=(k == KC - 1))
                last.then_inc(unit_done, 1)

            def levels(m):
                h, t = m // NT, m % NT
                s, cols = h % 2, slice(t * P, (t + 1) * P)
                pe.wait_ge(ops_ready, h + 1)
                for j in range(3):
                    T.matmul(ps[:, 3, j * P:(j + 1) * P], wl[s][j][:, cols], wl[s][j][:, cols], start=True, stop=True)
                T.matmul(ps[:, 3, 3 * P:4 * P], k16[s][:, cols], q16[s][:, cols], start=True, stop=True).then_inc(lvl_done, 1)
                T.transpose(ps[:, 4, 0:P], kdT[s][:, cols], ident).then_inc(kd_turned, 1)

            def outputs(m):
                h, t = m // NT, m % NT
                s, cols = h % 2, slice(t * P, (t + 1) * P)
                v_ = ib[:, t, h * DH:(h + 1) * DH]
                pe.wait_ge(smask_ready, m + 1)
                if m:
                    pe.wait_ge(o_out, m)
                    pe.wait_ge(state_ready, m)
                if t:
                    T.matmul(ps[:, 5, 0:P], qc[s][:, cols], state[:, h, :], start=True, stop=False)
                for j in range(4):
                    T.matmul(ps[:, 5, 0:P], smask[:, j, :], v_, start=(t == 0 and j == 0), stop=(j == 3))
                pe.wait_ge(kdtok_ready, m + 1)
                T.matmul(ps[:, 6, 0:P], kdtok, v_, start=True, stop=True).then_inc(o_done, 1)

            for unit in range(UNITS[IB]):
                project(unit)
            for unit in range(UNITS[IB], UNITS[GB]):
                m = unit - UNITS[IB]
                if m < HEADS * NT:
                    levels(m)
                project(unit)
                if m < HEADS * NT:
                    outputs(m)
                k = unit - UNITS[VA]
                if k >= 0:
                    n = rows_of(k)
                    pe.wait_ge(unit_out, UNITS[KA])
                    if k:
                        pe.wait_ge(ktok_ready, k)
                    for h in range(HEADS):
                        last = T.transpose(ps[0:n, 7, h * P:(h + 1) * P], kT[:, h, k * P:k * P + n], ident)
                    last.then_inc(kt_turned, 1)
            pe.wait_ge(unit_out, UNITS[GB])
            pe.wait_ge(ktok_ready, TILES)
            pe.wait_ge(o_out, HEADS * NT)
            pe.wait_ge(state_ready, HEADS * NT)

            def scores(n):
                h, i = n // NT, n % NT
                if n >= 2:
                    pe.wait_ge(logit_ready, n - 1)
                T.matmul(ps[:, n % 2, 0:(i + 1) * P], qT[:, h, i * P:(i + 1) * P], kT[:, h, 0:(i + 1) * P],
                         start=True, stop=True).then_inc(logit_done, 1)

            def key_scores(b):
                pe.wait_ge(keyT_ready, b + 1)
                for t in range(2):
                    for h in range(HEADS):
                        c = t * 32 + b * HEADS + h
                        last = T.matmul(ps[:, 5, c:c + 1], keyT[b % 2][:, t, h * P:(h + 1) * P], qT[:, h, SEQ + b:SEQ + b + 1],
                                        start=True, stop=True)
                last.then_inc(dscore_done if b == NB - 1 else dscore_part, 1)

            def keys(b):
                if b % 2 == 0:
                    pe.wait_ge(kv_in[b // 2], 16 * 12)
                if b:
                    pe.wait_ge(keyT_ready, b)
                for t in range(2):
                    for h in range(HEADS):
                        last = T.transpose(ps[:, 6 + t, h * P:(h + 1) * P],
                                           kvv[:, (KV_SLOT + b // 2) % RING, b % 2, 0, t, h * DH:(h + 1) * DH], ident)
                last.then_inc(key_turned, 1)

            def gated_heads(t):
                pe.wait_ge(og_ready, t + 1)
                if t:
                    pe.wait_ge(og_out, t)
                for h in range(HEADS):
                    last = T.transpose(ps[:, 7, h * P:(h + 1) * P], ostage[:, h, :], ident)
                last.then_inc(og_turned, 1)

            def spread_value(b):
                pe.wait_ge(vonly_ready, b + 1)
                if b:
                    pe.wait_ge(snew_ready, b)
                T.matmul(ps[:, 6, :], ones[0:NB, :], vonly[b % 2][0:NB], start=True, stop=True).then_inc(vb_done, 1)

            scores(0)
            for n in range(HEADS * NT):
                h, i = n // NT, n % NT
                if n + 1 < HEADS * NT:
                    scores(n + 1)
                if 0 < n <= NB:
                    key_scores(n - 1)
                pe.wait_ge(prob_normed, n + 1)
                if n >= 2:
                    pe.wait_ge(probT_ready, n - 1)
                for j in range(i + 1):
                    last = T.transpose(ps[:, 2 + n % 2, j * P:(j + 1) * P], prob[n % 2][:, j * P:(j + 1) * P], ident)
                last.then_inc(prob_turned, 1)
                if n < NB:
                    keys(n)
                else:
                    t = n - NB
                    spread_value(t)
                    if 2 <= t < NT + 2:
                        gated_heads(t - 2)
                pe.wait_ge(probT_ready, n + 1)
                if n:
                    pe.wait_ge(att_out, n)
                for j in range(i + 1):
                    last = T.matmul(ps[:, 4, 0:P], vtok[:, j, h * DH:(h + 1) * DH], probT[n % 2][:, j, :],
                                    start=(j == 0), stop=(j == i))
                last.then_inc(att_done, 1)
            pe.wait_ge(att_out, HEADS * NT)
            pe.wait_ge(og_out, NT)
            T.matmul(ps[0:32, 7, 0:NDEC], relrep[0:BUCKETS + 1].rearrange("p b h -> p (b h)"), onehot[0:BUCKETS + 1, ROWW:],
                     start=True, stop=True).then_inc(dbias_done, 1)
            pe.wait_ge(snew_ready, NB)
            for h in range(HEADS):
                T.transpose(ps[:, 0, 32 + h * NB:32 + (h + 1) * NB], gb[0:NB, NT, h * DH:(h + 1) * DH], ident[0:NB, 0:NB])
            for b in range(NB):
                for h in range(HEADS):
                    last = T.matmul(ps[:, 0, h * NB + b:h * NB + b + 1], stv[:, b, h, :], qbT[:, h, SEQ + b:SEQ + b + 1],
                                    start=True, stop=True)
            last.then_inc(os_done, 1)
            pe.wait_ge(dscT_ready, 1)
            for t in range(2):
                T.transpose(ps[0:32, 4, t * P:(t + 1) * P], dscT[:, t].rearrange("p b h -> p (b h)"), ident)
            pe.wait_ge(qkself_ready, 1)
            T.matmul(ps[0:32, 4, NDEC - 1:NDEC], qkself.rearrange("p b h -> p (b h)"), ones[:, 0:1], start=True, stop=True).then_inc(dlog_done, 1)
            pe.wait_ge(dprob_ready, 1)
            for t in range(2):
                last = T.transpose(ps[:, 6, t * 32:(t + 1) * 32], dprob[0:32, t * P:(t + 1) * P], ident[0:32, 0:32])
            last.then_inc(dprob_turned, 1)
            pe.wait_ge(dprobT_ready, 1)
            pe.wait_ge(vrow_in, 16)
            T.matmul(ps[:, 7, 0:32], vrow[0:32], diag[0:32], start=True, stop=False, skip_group_check=True)
            for b in range(NB):
                for h in range(HEADS):
                    c = b * HEADS + h
                    for t in range(2):
                        last = T.matmul(ps[:, 7, c:c + 1], kvv[:, (KV_SLOT + b // 2) % RING, b % 2, 1, t, h * DH:(h + 1) * DH],
                                        dprobT[:, t, c:c + 1], start=False, stop=(t == 1), skip_group_check=True)
                if b % 2:
                    last.then_inc(kv_used if b < NB - 1 else datt_done, 1)
            pe.wait_ge(datt_done, 1)
            pe.sem_inc(kv_used, 1)

            pe.wait_ge(osq_ready, 1)
            T.matmul(ps[:, 1, 0:32], ones, osq, start=True, stop=True).then_inc(oss_done, 1)
            pe.wait_ge(cat_ready, 1)
            pe.wait_ge(og_out, NT)
            for t in range(TILES):
                n = rows_of(t)
                if t >= 2:
                    pe.wait_ge(x_added, t - 1)
                for c in range(2):
                    pe.wait_ge(wout_in[c], 16)
                    for k in range(KC):
                        last = T.matmul(ps[0:n, 4 + 2 * (t % 2) + c, :], catT[:, k, t * P:t * P + n], w1v[:, WOUT_SLOT + c, k, :],
                                        start=(k == 0), stop=(k == KC - 1))
                    last.then_inc(wo_done, 1)

            def products(j, halves):
                for k in range(KC):
                    for half in halves:
                        r_ = slice(half * CAP, (half + 1) * CAP)
                        last = T.matmul(ps[r_, 2 + j, :], xgT[:, k, r_], w1v[:, piece_slot(half, j), k, :],
                                        start=(k == 0), stop=(k == KC - 1))
                return last

            def results(halves):
                for c in range(2):
                    for k in range(FC):
                        for half in halves:
                            r_ = slice(half * CAP, (half + 1) * CAP)
                            last = T.matmul(ps[r_, 5 + c, :], hactT[:, k, r_], w2v[:, piece_slot(half, 2), k, c * 512:(c + 1) * 512],
                                            start=(k == 0), stop=(k == FC - 1))
                return last

            def experts(l):
                pe.wait_ge(router_in, 16 * 9)
                for t in range(TILES):
                    n = rows_of(t)
                    g = TILES * l + t
                    pe.wait_ge(hn_ready, g + 1)
                    if t >= 2:
                        pe.wait_ge(htile_ready, g - 1)
                    for k in range(KC):
                        last = T.transpose(ps[:, 2 * (t % 2) + k // 4, (k % 4) * P:(k % 4) * P + n], hall[0:n, t, k * P:(k + 1) * P],
                                           ident[0:n, 0:n])
                    last.then_inc(hn_turned, 1)
                    pe.wait_ge(htile_ready, g + 1)
                    for k in range(KC):
                        last = T.matmul(ps[0:n, 4 + t % 2, 0:NG + NE], htile[:, k, 0:n], wr[:, l, k, :], start=(k == 0), stop=(k == KC - 1))
                    last.then_inc(rlog_done, 1)
                pe.wait_ge(mem_ready, l + 1)
                for t in range(TILES):
                    out = ps[:, 6, t * NE:(t + 1) * NE]
                    T.matmul(out, tri, mem[:, t, :], start=True, stop=(t == 0))
                    for s in range(t):
                        T.matmul(out, ones, mem[:, s, :], start=False, stop=(s == t - 1))
                for t in range(TILES):
                    last = T.matmul(ps[:, 7, 0:NE], ones, mem[:, t, :], start=(t == 0), stop=(t == NT))
                last.then_inc(rank_done, 1)
                pe.wait_ge(slots_ready, l + 1)

                def turn(i, first):
                    pe.wait_ge(xg_in, 16 * PAIRS * l + 16 * i + 16)
                    if not first:
                        pe.wait_ge(xT_ready, PAIRS * l + i)
                    for k in range(KC):
                        last = T.transpose(ps[:, k // 4, (k % 4) * P:(k % 4 + 1) * P], xg[:, k * P:(k + 1) * P], ident)
                    last.then_inc(x_turned, 1)

                def pair(i, first, last):
                    pe.wait_ge(xT_ready, PAIRS * l + i + 1)
                    if not first:
                        pe.wait_ge(hact_ready, PAIRS * l + i)
                    for j in range(2):
                        for half in range(2):
                            pe.wait_ge(wt_in[piece_slot(half, j)], 16 * PAIRS * l + 16 * i + 16)
                        products(j, (0, 1)).then_inc((w1_used, h_done)[j], 1)
                    if not last:
                        turn(i + 1, False)
                    pe.wait_ge(hact_ready, PAIRS * l + i + 1)
                    if not first:
                        pe.wait_ge(hactT_ready, PAIRS * l + i)
                    for k in range(FC):
                        t_ = T.transpose(ps[:, 4, k * P:(k + 1) * P], hact[:, k * P:(k + 1) * P], ident)
                    t_.then_inc(hact_turned, 1)
                    for half in range(2):
                        pe.wait_ge(wt_in[piece_slot(half, 2)], 16 * PAIRS * l + 16 * i + 16)
                    pe.wait_ge(hactT_ready, PAIRS * l + i + 1)
                    if not first:
                        pe.wait_ge(y_out, PAIRS * l + i)
                    results((0, 1)).then_inc(y_done, 1)

                turn(0, True)
                pair(0, True, False)
                with pe.Fori(1, PAIRS - 1) as i:
                    pair(i, False, False)
                pair(PAIRS - 1, False, True)
                pe.wait_ge(y_out, PAIRS * (l + 1))
                n_over = pe.value_load(tables[l][0:1, NOV:NOV + 1], min_val=0, max_val=NOV)
                with pe.If(n_over > 0):
                    with pe.Fori(0, NOV) as j:
                        with pe.If(n_over > j):
                            pe.wait_ge(over_in[l], 64 * j + 64)
                            pe.sem_inc(over_seen, 1)
                            for k in range(KC):
                                last = T.transpose(ps[:, 0, k * CAP:(k + 1) * CAP], xg[0:CAP, k * P:(k + 1) * P], ident[0:CAP, 0:CAP])
                            last.then_inc(over_step[l], 1)
                            pe.wait_ge(over_step[l], over_count(j, COLUMNS))
                            products(0, (0,))
                            products(1, (0,)).then_inc(over_step[l], 1)
                            pe.wait_ge(over_step[l], over_count(j, GATED))
                            pe.sem_inc(over_seen, 1)
                            for k in range(FC):
                                last = T.transpose(ps[:, 4, k * CAP:(k + 1) * CAP], hact[0:CAP, k * P:(k + 1) * P], ident[0:CAP, 0:CAP])
                            last.then_inc(over_step[l], 1)
                            pe.wait_ge(over_step[l], over_count(j, ACT_COLUMNS))
                            results((0,)).then_inc(over_step[l], 1)
                        with pe.Else():
                            pe.nop()
                    pe.nop()
                with pe.Else():
                    pe.nop()
                pe.nop()

            experts(0)
            pe.wait_ge(poolw_in, 16 * NG)
            pe.wait_ge(pool_in, 16 * 4)
            for t in range(TILES):
                n = rows_of(t)
                pe.wait_ge(x_added, TILES + t + 1)
                if t:
                    pe.wait_ge(mixT_ready, t)
                for k in range(KC):
                    g = k // 2
                    out = ps[:, k // 4, (k % 4) * P:(k % 4) * P + n]
                    cols = slice(k * P, (k + 1) * P)
                    if t < NT:
                        last = T.matmul(out, hall[:, t, cols], poolc[:, 0 if t == 0 else 1, g, :], start=True, stop=(t == 0))
                        if t:
                            last = T.matmul(out, hall[:, t - 1, cols], poolc[:, 2, g, :], start=False, stop=True)
                    else:
                        T.matmul(out, prev[0:NB * KEEP, cols], poolstate[0:NB * KEEP, 0, g, :], start=True, stop=False)
                        last = T.matmul(out, hall[0:NB, t, cols], poolstate[0:NB, 1, g, :], start=False, stop=True)
                last.then_inc(mix_done, 1)
                pe.wait_ge(mixT_ready, t + 1)
                if t >= 2:
                    pe.wait_ge(x_added, 2 * TILES + t - 1)
                for g in range(NG):
                    for k in range(2):
                        last = T.matmul(ps[0:n, 2 + 2 * (t % 2) + g // 2, (g % 2) * 256:(g % 2 + 1) * 256], mixT[:, 2 * g + k, 0:n],
                                        poolw[:, g, k, :], start=(k == 0), stop=(k == 1))
                last.then_inc(pool_done, 1)
            experts(1)


_INS = ["x_prompt", "x_sample", "cache_win_k", "cache_win_v", "state_hgrn", "state_pool", "rel_bias", "norm_mix",
        "norm_ffn", "norm_final", "w_in", "w_out", "hgrn_lb", "hgrn_gnorm", "pool_w", "pool_scale", "moe_wg_group",
        "moe_bg_group", "moe_wg_exp", "moe_bg_exp", "moe_w1", "moe_w3", "moe_w2"]
_OUTS = [(1, SEQ, D), (NB, 1, D), (1, 1, SEQ, HEADS, DH), (1, 1, SEQ, HEADS, DH), (1, 1, HEADS, DH, DH), (1, 1, KEEP, D),
         (1, NB, 1, HEADS, DH), (1, NB, 1, HEADS, DH), (1, NB, HEADS, DH, DH), (1, NB, 1, D)]


def kernel(**inputs):
    import numpy as _np
    import concourse.bacc as _bacc
    from concourse import mybir as _mybir
    from concourse.bass_utils import run_bass_kernel_spmd as _run

    nc = _bacc.Bacc("TRN2", target_bir_lowering=False, num_devices=1)
    arrays, a, consts = {}, {}, {}
    for name in _INS:
        v = _np.ascontiguousarray(inputs[name])
        arrays[f"in_{name}"] = v
        a[name] = nc.dram_tensor(f"in_{name}", v.shape, _mybir.dt.from_np(v.dtype), kind="ExternalInput").ap()
    for name, v in shape_constants().items():
        arrays[name] = v
        consts[name] = nc.dram_tensor(name, v.shape, _mybir.dt.from_np(v.dtype), kind="ExternalInput").ap()
    outs = [nc.dram_tensor(f"out_{i}", s, _mybir.dt.float32, kind="ExternalOutput").ap() for i, s in enumerate(_OUTS)]
    build(nc, a, outs, consts)
    r = _run(nc, [arrays], core_ids=[0])
    return tuple(r.results[0][f"out_{i}"] for i in range(len(_OUTS)))
```

```python
from contextlib import ExitStack

import numpy as np

import concourse.bass as bass
from concourse import mybir

ALU = mybir.AluOpType
ACT = mybir.ActivationFunctionType
F32 = mybir.dt.float32
I32 = mybir.dt.int32
U32 = mybir.dt.uint32
AX = mybir.AxisListType

P = 128
D = 1024
KC = D // P
SEQ = 512
NT = SEQ // P
NB = 8
TILES = NT + 1
TOK = SEQ + NB
HEADS = 4
DH = 128
AW = HEADS * DH
NPROJ = 7 * AW
PAST = 1024
NG = 4
EPG = 8
NE = 32
FE = 512
FC = FE // P
CAP = 64
NOV = 2 * TOK // (CAP + 1)
SLOTS = (NE + NOV) * CAP
THR = (TOK + CAP - 1) // CAP
EPS = 1e-6
SCALE = DH ** -0.5
PIECE = 4096
RING = 6
NEG = -1e30
BRANCHES = ((128, 1), (512, 4), (2048, 16))
BUCKETS = 32
MAXD = 2048
WINDOWS = (2, 4, 8, 16)
KEEP = 15
LEVELS = (128, 64, 32, 16)
ROWW = 640
NDEC = 257


def rows_of(t):
    return P if t < NT else NB


def shape_constants():
    def bucket(d):
        big = 16 + np.floor(np.log(np.maximum(d, 1) / 16) / np.log(MAXD / 16) * 16).astype(np.int32)
        return np.where(d < 16, d, np.minimum(big, BUCKETS - 1))

    def columns(dist):
        dist = np.asarray(dist)
        ok = dist >= 0
        d = np.where(ok, dist, 0)
        mult = sum(((d % s == 0) & (d <= w) & ok).astype(np.int32) for w, s in BRANCHES)
        out = np.zeros((BUCKETS + 1, len(d)), np.float32)
        out[bucket(d), np.arange(len(d))] = mult > 0
        out[BUCKETS] = np.where(mult > 0, np.log(np.maximum(mult, 1)), NEG)
        return out

    prompt = columns(SEQ - 1 - np.arange(ROWW))
    p = np.arange(P)
    near = P - p
    far = np.where(p < 96, 512 - 4 * p, 1024 - 16 * (p - 96))
    decode = columns(np.concatenate([near, far, [0]]))
    onehot = np.concatenate([prompt, decode], 1)

    s, t = np.arange(P)[:, None], np.arange(P)[None, :]
    levels = []
    for n in LEVELS[:-1]:
        levels.append((s // n == t // n) & (s % n < n // 2) & (t % n >= n // 2))
    levels.append((s // 16 == t // 16) & (s <= t))
    reset = np.broadcast_to((np.arange(SEQ) % P != 0).astype(np.float32), (P, SEQ))
    one = lambda a: np.broadcast_to(np.asarray(a, np.float32), (P, len(a)))
    valid = np.stack([(p < rows_of(k)) for k in range(TILES)], 1)
    square = np.concatenate([np.eye(P), np.ones((P, P)), s < t], 1)
    small = np.concatenate([one(np.arange(NE)), one(np.arange(NE) * CAP), one((np.arange(THR) + 1) * CAP), valid,
                            np.ones((P, NE)), SLOTS + p[:, None]], 1)
    masks = np.concatenate(levels + [reset], 1)

    pool = np.zeros((P, 3, len(WINDOWS), P), np.float32)
    for g, w in enumerate(WINDOWS):
        own = ((s <= t) & (t - s < w)).astype(np.float32)
        before = (P + t - s < w).astype(np.float32)
        pool[:, 0, g] = own / np.minimum(w, t + 1) - np.eye(P)
        pool[:, 1, g] = own / w - np.eye(P)
        pool[:, 2, g] = before / w
    state = np.zeros((P, 2, len(WINDOWS), NB), np.float32)
    for g, w in enumerate(WINDOWS):
        for b in range(NB):
            state[b * KEEP + KEEP - (w - 1):(b + 1) * KEEP, 0, g, b] = 1 / w
            state[b, 1, g, b] = 1 / w - 1
    pools = np.concatenate([pool.reshape(P, -1), state.reshape(P, -1)], 1)
    return {k: np.ascontiguousarray(v, dtype=np.float32) for k, v in
            (("c_onehot", onehot), ("c_square", square), ("c_small", small), ("c_masks", masks), ("c_pool", pools))}


def build(nc, a, outs, consts):
    (y_prompt, y_sample, k_prompt, v_prompt, s_prompt, p_prompt, k_sample, v_sample, s_sample, p_sample) = outs
    slot_x = nc.dram_tensor("slot_x", (SLOTS + 2 * TILES * P, D), F32, kind="Internal").ap()
    slot_y = nc.dram_tensor("slot_y", (SLOTS, D), F32, kind="Internal").ap()
    bias_rows = nc.dram_tensor("bias_rows", (HEADS, P, ROWW), F32, kind="Internal").ap()

    with ExitStack() as ctx:
        ring = ctx.enter_context(nc.sbuf_tensor("ring", [P, RING, PIECE], F32))
        ARENA = 28600
        arena = ctx.enter_context(nc.sbuf_tensor("arena", [P, ARENA], F32))
        ps = ctx.enter_context(nc.psum_tensor("ps", [P, 8, 512], F32))

        def sem(name):
            return ctx.enter_context(nc.semaphore(name))

        def at(lo, *shape):
            n = int(np.prod(shape))
            assert lo + n <= ARENA, (lo, shape)
            v = arena[:, lo:lo + n]
            if len(shape) == 1:
                return v
            names = "abcd"[:len(shape)]
            return v.rearrange(f"p ({' '.join(names)}) -> p {' '.join(names)}",
                               **{k: s for k, s in zip(names, shape)})

        def wide(ap, shape, axis):
            return ap.unsqueeze(axis).broadcast_to(shape)

        hT = at(0, KC, TOK)
        catT = at(0, KC, TOK)
        qT = at(4160, HEADS, TOK)
        kT = at(6240, HEADS, TOK)
        vtok = at(8320, TILES, AW)
        qbT = at(10880, HEADS, TOK)
        fT = at(12960, HEADS, TOK)
        ib = at(15040, TILES, AW)
        gb = at(17600, TILES, AW)
        xin = [at(4160 + 1024 * t, D) for t in range(TILES)]
        hrow = at(22208, D)
        gain0 = at(23232, D)
        junk = at(24256, D)
        toep = at(20160, HEADS, SEQ)
        prob = [at(22208 + 512 * i, SEQ) for i in range(2)]
        probT = [at(23232 + 512 * i, NT, P) for i in range(2)]
        relx = at(25280, HEADS)
        relrep = at(25288, NB, HEADS)
        onehot = at(25320, ROWW + NDEC)
        brow = at(26220, ROWW)
        astat = at(26862, 96)
        dscT = at(22208, 2, NB, HEADS)
        dlog = at(22272, NDEC)
        dprob = at(22532, NDEC)
        dbias = at(22792, NDEC)
        qkself = at(23052, NB, HEADS)
        diag = at(23084, 32)
        vrow = at(23116, DH)
        dstat = at(23310, 8)
        pspread = at(23320, 2, NB * (4 * NB + HEADS))
        dheads = at(23896, HEADS * DH)
        wl = [[ring[:, 1 + i, 512 * j:512 * (j + 1)] for j in range(3)] for i in range(2)]
        q16 = [ring[:, 1 + i, 1536:2048] for i in range(2)]
        k16 = [ring[:, 1 + i, 2048:2560] for i in range(2)]
        qc = [ring[:, 1 + i, 2560:3072] for i in range(2)]
        kdT = [ring[:, 1 + i, 3072:3584] for i in range(2)]
        partial = [at(23872, AW), ring[:, 1, 3584:4096]]
        pick = at(24896, NB)
        partial_late = at(24840, 2, 512)
        pick_late = at(17096, NB)
        lcum = at(22208, SEQ)
        ldif = at(22720, SEQ)
        lexp = at(23232, SEQ)
        kdtok = at(23744, P)
        smask = at(23872, 4, P)
        state = at(24384, HEADS, DH)
        sq = at(24256, HEADS, DH)
        ostage = at(24768, HEADS, DH)
        hstat = at(26220, 160)
        gnb = at(26380, DH)
        ktok = [qbT[:, i, 0:SEQ] for i in range(2)]
        keyT = [fT[:, 2 * i:2 * i + 2, 0:SEQ] for i in range(2)]
        vonly = [at(26970 + 512 * i, AW) for i in range(2)]
        tmp_kv = [qbT[:, i, 0:SEQ].rearrange("p (h v) -> p h v", h=HEADS) for i in (2, 1)]
        osq = qbT[:, 3, 0:32]
        osT = qbT[:, 3, 32:64].rearrange("p (h b) -> p h b", h=HEADS)
        gsT = qbT[:, 3, 64:96].rearrange("p (h b) -> p h b", h=HEADS)
        gncol = qbT[:, 3, 96:97]
        sstat = qbT[:, 3, 128:256]
        masks = at(26970, 4, P)
        reset = at(27482, SEQ)
        zero = gb[:, 0:2, :].rearrange("p a b -> p (a b)")
        x = at(4160, TILES, D)
        hall = at(9280, TILES, D)
        xg = at(9280, D)
        yst = at(10304, D)
        gat = [at(lo, D) for lo in (3072, 25864, 16072, 17096)]
        htile = at(14400, KC, P)
        wr = at(15424, 2, KC, NG + NE)
        rbias = at(16000, 2, NG + NE)
        xgT = at(16072, KC, 2 * CAP)
        sg = at(17096, FE)
        hact = at(17608, FE)
        hactT = at(26900, FC, 2 * CAP)
        gain = [at(18120 + 1024 * i, D) for i in range(2)]
        R = 20168
        lg = at(R, TILES, NG + NE)
        g8 = at(R + 180, TILES, 8)
        gm8 = at(R + 220, TILES, 8)
        e8 = at(R + 260, TILES, 8)
        em8 = at(R + 300, TILES, 8)
        gi8 = at(R + 340, TILES, 8).bitcast(U32)
        ei8 = at(R + 380, TILES, 8).bitcast(U32)
        gsel = at(R + 420, TILES)
        g4 = at(R + 425, TILES, NG)
        eid = at(R + 445, TILES, 2)
        dexp = at(R + 455, TILES, 5)
        gden = at(R + 480, TILES)
        sel = at(R + 485, TILES, NG, EPG)
        oh = at(R + 645, TILES, 2, NE)
        mem = at(R + 965, TILES, NE)
        over = at(R + 1125, TILES, NE)
        ohs = at(3072, TILES, 2, NE)
        novx = at(R + 1605, NE)
        ovend = at(R + 1637, NE)
        dbase = at(R + 1669, NE)
        ovf = at(R + 1701, NOV)
        cmp = at(R + 1725, NE, THR)
        place = at(R + 1485, NE)
        spares = at(R + 1725 + THR * NE + 1, 2 * TILES)
        placed = at(R + 1517, 2, NE)
        firstf = at(R + 1581, 2)
        firstu = at(R + 1583, TILES, 2).bitcast(U32)
        assert THR * NE + 2 * TILES < 320 and NOV <= 24
        poolc = at(22216, 3, len(WINDOWS), P)
        poolstate = at(22216 + 1536, 2, len(WINDOWS), NB)
        prev = at(23816, D)
        mixT = at(24840, KC, P)
        pscale = at(25864, D)
        poolw = at(0, NG, 2, 256)
        spare = at(26900, D)
        ecmp = at(2048, NOV, NE)
        C = 28000
        ident = at(C, P)
        ones = at(C + 128, P)
        tri = at(C + 256, P)
        small = at(C + 384, 3 * NE + THR + TILES + 1)
        iota = small[:, 0:NE]
        ebase = small[:, NE:2 * NE]
        thr = small[:, 2 * NE:2 * NE + THR]
        valid = small[:, 2 * NE + THR:2 * NE + THR + TILES]
        ones32 = small[:, 2 * NE + THR + TILES:3 * NE + THR + TILES]
        spare_row = small[:, 3 * NE + THR + TILES:]
        M = C + 384 + 3 * NE + THR + TILES + 1
        rms = [at(M + 5 * i, TILES) for i in range(2)]
        eps = at(ARENA - 1, 1)
        gates = at(M + 10, TILES, 2)
        slotu = at(M + 20, TILES, 2).bitcast(U32)
        slotf = at(M + 30, TILES, 2)
        tables = [at(lo, NOV + 1).bitcast(I32) for lo in (M + 40, M + 85)]
        lbl = at(M + 65, 2, HEADS)
        lb = at(M + 73, HEADS)
        oml = at(M + 77, HEADS)
        lbs = at(M + 81, HEADS)
        assert M + 85 + NOV + 1 < ARENA and NOV + 1 <= 25

        consts_in = sem("consts_in")
        masks_in = sem("masks_in")
        x_in = [sem(f"x_in{i}") for i in range(TILES)]
        gain_in = sem("gain_in")
        eps_ready = sem("eps_ready")
        root = [sem(f"root{i}") for i in range(2)]
        h_ready = sem("h_ready")
        h_turned = sem("h_turned")
        hT_ready = sem("hT_ready")
        w_in = [sem(f"w_in{i}") for i in range(RING)]
        kv_in = [sem(f"kv_in{i}") for i in range(2)]
        kv_used = sem("kv_used")
        state_in = sem("state_in")
        wout_in = [sem(f"wout_in{i}") for i in range(2)]
        unit_done = sem("unit_done")
        unit_out = sem("unit_out")
        part_picked = sem("part_picked")
        part_out = sem("part_out")
        partial_clear = sem("partial_clear")
        kt_turned = sem("kt_turned")
        ktok_ready = sem("ktok_ready")
        ktok_stored = [sem(f"ktok_stored{i}") for i in range(2)]
        stored = sem("stored")
        rel_in = sem("rel_in")
        rel_ready = sem("rel_ready")
        brow_done = sem("brow_done")
        brow_ready = sem("brow_ready")
        bias_moved = sem("bias_moved")
        logit_done = sem("logit_done")
        logit_ready = sem("logit_ready")
        prob_ready = sem("prob_ready")
        prob_normed = sem("prob_normed")
        prob_turned = sem("prob_turned")
        probT_ready = sem("probT_ready")
        att_done = sem("att_done")
        att_out = sem("att_out")
        key_turned = sem("key_turned")
        keyT_ready = sem("keyT_ready")
        dscore_done = sem("dscore_done")
        dscT_ready = sem("dscT_ready")
        dheads_ready = sem("dheads_ready")
        qkself_ready = sem("qkself_ready")
        dlog_ready = sem("dlog_ready")
        dprob_exp = sem("dprob_exp")
        dprob_ready = sem("dprob_ready")
        dprobT_ready = sem("dprobT_ready")
        vrow_in = sem("vrow_in")
        vs_stored = sem("vs_stored")
        zeros_ready = sem("zeros_ready")
        slots_cleared = sem("slots_cleared")
        lb_in = sem("lb_in")
        lb_exp = sem("lb_exp")
        lbl_ready = sem("lbl_ready")
        f_ready = sem("f_ready")
        logf_ready = sem("logf_ready")
        dif_ready = sem("dif_ready")
        exp_ready = sem("exp_ready")
        ops_ready = sem("ops_ready")
        lvl_done = sem("lvl_done")
        smask_ready = sem("smask_ready")
        kd_turned = sem("kd_turned")
        kdtok_ready = sem("kdtok_ready")
        o_done = sem("o_done")
        o_out = sem("o_out")
        state_ready = sem("state_ready")
        state_stored = sem("state_stored")
        gn_in = sem("gn_in")
        ohead_sq = sem("ohead_sq")
        ohead_ms = sem("ohead_ms")
        ohead_root = sem("ohead_root")
        og_ready = sem("og_ready")
        og_turned = sem("og_turned")
        og_out = sem("og_out")
        vonly_ready = sem("vonly_ready")
        vb_done = sem("vb_done")
        snew_ready = sem("snew_ready")
        fs_ready = sem("fs_ready")
        fS_ready = sem("fS_ready")
        kv_ready = sem("kv_ready")
        snew_stored = sem("snew_stored")
        osq_ready = sem("osq_ready")
        oms_ready = sem("oms_ready")
        oroot = sem("oroot")
        cat_ready = sem("cat_ready")
        sample_step = sem("sample_step")
        BIASES, LOGITS, PROBS_TURNED, STATE_OUT, ATTENDED, SQUARES_SUMMED, HEADS_TURNED = range(1, 8)
        mixers_done = sem("mixers_done")
        xres_in = sem("xres_in")
        wo_done = sem("wo_done")
        x_added = sem("x_added")
        router_in = sem("router_in")
        act_chain = sem("act_chain")
        dve_chain = sem("dve_chain")
        hn_ready = sem("hn_ready")
        hn_turned = sem("hn_turned")
        htile_ready = sem("htile_ready")
        rlog_done = sem("rlog_done")
        lg_ready = sem("lg_ready")
        tables_ready = sem("tables_ready")
        pooled_in = sem("pooled_in")
        pooled_stored = sem("pooled_stored")
        gexp_ready = sem("gexp_ready")
        mem_ready = sem("mem_ready")
        rank_done = sem("rank_done")
        slots_ready = sem("slots_ready")
        first_ready = sem("first_ready")
        over_counted = sem("over_counted")
        rows_placed = sem("rows_placed")
        scattered = [sem(f"scattered{l}") for l in range(2)]
        gathered = [sem(f"gathered{i}") for i in range(2)]
        gat_used = sem("gat_used")
        y_all_stored = [sem(f"y_all_stored{i}") for i in range(2)]
        pool_in = sem("pool_in")
        mix_done = sem("mix_done")
        mixT_ready = sem("mixT_ready")
        pool_done = sem("pool_done")
        y_final = sem("y_final")

        wt_in = [sem(f"wt_in{i}") for i in range(RING)]
        w1_used = sem("w1_used")
        xg_in = sem("xg_in")
        x_turned = sem("x_turned")
        xT_ready = sem("xT_ready")
        h_done = sem("h_done")
        silu_ready = sem("silu_ready")
        hact_ready = sem("hact_ready")
        hact_turned = sem("hact_turned")
        hactT_ready = sem("hactT_ready")
        y_done = sem("y_done")
        y_out = sem("y_out")
        y_stored = sem("y_stored")
        PAIRS = NE // 2
        over_in = [sem(f"over_in{l}") for l in range(2)]
        over_step = [sem(f"over_step{l}") for l in range(2)]
        over_stored = [sem(f"over_stored{l}") for l in range(2)]
        over_seen = sem("over_seen")
        TURNED, COLUMNS, PRODUCTS, SILU, GATED, ACT_TURNED, ACT_COLUMNS, ROWS, OUT = range(1, 10)

        def over_count(j, step):
            return 9 * j + step

        ORDER = (3, 4, 5, 0, 1, 2, 6)
        QB, FB, IB, QA, KA, VA, GB = range(7)
        WOUT_SLOT = 2
        STATE_SLOT = 1
        KV_SLOT = 3
        TURNED_PARTS = (QB, FB, QA, KA)
        FIRST = 4

        UNITS = [TILES * (c + 1) for c in range(7)]

        def piece_slot(half, j):
            return (FIRST + 2 * j + half) % RING

        w1v = ring[:, :, :].rearrange("p s (k f) -> p s k f", k=KC)
        w2v = ring[:, :, :].rearrange("p s (k d) -> p s k d", k=FC)
        kvv = ring[:, :, :].rearrange("p s (b w t c) -> p s b w t c", b=2, w=2, t=2)
        stv = ring[:, STATE_SLOT, :].rearrange("p (b h v) -> p b h v", b=NB, h=HEADS)

        xp = a["x_prompt"].rearrange("b (t p) d -> p (b t) d", p=P)
        xs = a["x_sample"].rearrange("b t d -> (b t) d")

        def x_rows(t):
            return xp[:, t, :] if t < NT else xs

        def gate_rows(name, layer, e):
            return a[name][layer, bass.ds(e, 1), :, :].rearrange("a (k p) f -> p (a k) f", p=P)

        def slot_rows(tensor, block):
            return tensor[bass.ds(block * CAP, CAP), :]

        def chained(eng, signal):
            n = [0]

            def link(instruction):
                n[0] += 1
                instruction.then_inc(signal, 1)
                eng.wait_ge(signal, n[0])
            return link

        block = ctx.enter_context(nc.Block())

        @block.sync
        def _(sp):
            for t in range(TILES):
                sp.dma_start(xin[t][0:rows_of(t)], x_rows(t)).then_inc(x_in[t], 16)
            for c in range(7):
                if c == RING:
                    sp.wait_ge(unit_done, UNITS[0])
                col = ORDER[c] * AW
                sp.dma_start(w1v[:, c % RING], a["w_in"][0, :, col:col + AW].rearrange(
                    "(k p) f -> p k f", p=P)).then_inc(w_in[c % RING], 16)
            for c in range(4):
                sp.wait_ge(unit_done, UNITS[KV_SLOT + c])
                for b in range(2):
                    for w, name in enumerate(("cache_win_k", "cache_win_v")):
                        src = a[name][0, 2 * c + b].rearrange("r h d -> r (h d)")
                        dst = kvv[:, (KV_SLOT + c) % RING, b, w]
                        for to, of in ((dst[:, 0, :], src[PAST - P:PAST, :]),
                                       (dst[0:96, 1, :], src[512:893:4, :]),
                                       (dst[96:P, 1, :], src[0:497:16, :])):
                            sp.dma_start(to, of).then_inc(kv_in[c // 3], 16)
            sp.wait_ge(o_done, HEADS * NT)
            sp.wait_ge(part_picked, GB + 1)
            sp.dma_start(stv[:, :, :, :], a["state_hgrn"][0].rearrange("b h k v -> k b h v")).then_inc(state_in, 16)
            for c in range(2):
                if c == 1:
                    sp.wait_ge(kv_used, 1)
                sp.dma_start(w1v[:, WOUT_SLOT + c], a["w_out"][0, :, c * 512:(c + 1) * 512].rearrange(
                    "(k p) f -> p k f", p=P)).then_inc(wout_in[c], 16)

            def load(l, e, half, j, before):
                if before is not None:
                    sp.wait_ge((w1_used, h_done, y_done)[j], before)
                s = piece_slot(half, j)
                name = ("moe_w1", "moe_w3", "moe_w2")[j]
                sp.dma_start(w2v[:, s] if j == 2 else w1v[:, s], gate_rows(name, l, e)).then_inc(wt_in[s], 16)

            for l in range(2):
                for j in range(3):
                    for half in range(2):
                        if l == 0 and (half, j) == (0, 0):
                            sp.wait_ge(kv_used, 4)
                            sp.wait_ge(xres_in, 16 * TILES)
                            sp.wait_ge(router_in, 16 * 9)
                        if l == 0 and (half, j) == (1, 1):
                            sp.wait_ge(snew_stored, 16)
                        if l == 0 and (half, j) == (0, 2):
                            sp.wait_ge(wo_done, 2 * TILES)
                        if l == 1 and (half, j) == (0, 0):
                            sp.wait_ge(gat_used, TILES)
                        if l == 1 and (half, j) == (1, 1):
                            sp.wait_ge(pooled_stored, 32)
                        load(l, half, half, j, None if l == 0 else PAIRS)
                with sp.Fori(1, PAIRS) as i:
                    for j in range(3):
                        for half in range(2):
                            load(l, 2 * i + half, half, j, PAIRS * l + i)
                sp.wait_ge(tables_ready, l + 1)
                n_over = sp.value_load(tables[l][0:1, NOV:NOV + 1], min_val=0, max_val=NOV)
                with sp.If(n_over > 0):
                    sp.wait_ge(y_done, PAIRS * (l + 1))
                    with sp.Fori(0, NOV) as j:
                        with sp.If(n_over > j):
                            e = sp.value_load(tables[l][0:1, bass.ds(j, 1)], min_val=0, max_val=NE - 1)
                            for k, name in enumerate(("moe_w1", "moe_w3", "moe_w2")):
                                s = piece_slot(0, k)
                                dst = w2v[:, s] if k == 2 else w1v[:, s]
                                sp.dma_start(dst, gate_rows(name, l, e)).then_inc(over_in[l], 16)
                            sp.wait_ge(over_step[l], over_count(j, ROWS))
                            sp.sem_inc(over_seen, 1)
                        with sp.Else():
                            sp.nop()
                    sp.nop()
                with sp.Else():
                    sp.nop()
                sp.nop()

        @block.gpsimd
        def _(pool):
            nc.gpsimd.memset(zero, 0.0).then_inc(zeros_ready, 1)
            pool.dma_start(at(26970, 4 * P + SEQ), consts["c_masks"]).then_inc(masks_in, 16)
            pool.wait_ge(brow_ready, 1)
            pool.dma_start(bias_rows, wide(brow[0:HEADS], [HEADS, P, ROWW], 1)).then_inc(bias_moved, 16)
            pool.wait_ge(bias_moved, 16)
            pool.dma_start(toep, bass.AP(bias_rows.tensor, P - 1, [[ROWW - 1, P], [P * ROWW, HEADS], [1, SEQ]])).then_inc(bias_moved, 16)
            pool.wait_ge(zeros_ready, 1)
            pool.wait_ge(unit_done, UNITS[QB])
            for table, lo in ((slot_x, 0), (slot_y, NE * CAP)):
                rows = table[lo:SLOTS, :].rearrange("(p j) d -> p j d", p=P)
                pool.dma_start(rows, wide(zero, [P, rows.shape[1], D], 1)).then_inc(slots_cleared, 16)
            pool.wait_ge(fs_ready, 1)
            pool.wait_ge(state_in, 16)
            for b in range(NB):
                nc.gpsimd.tensor_tensor(stv[:, b], stv[:, b], fT[:, :, SEQ + b:SEQ + b + 1].broadcast_to([P, HEADS, DH]),
                                        ALU.mult).then_inc(fS_ready, 1)
            for b in range(NB):
                pool.wait_ge(fS_ready, b + 1)
                pool.wait_ge(kv_ready, b + 1)
                nc.gpsimd.tensor_tensor(stv[:, b], stv[:, b], tmp_kv[b % 2], ALU.add).then_inc(snew_ready, 1)
            for l in range(2):
                def scatter(slots, t, k, signal):
                    n = rows_of(t)
                    pool.indirect_dma_start(
                        out=slot_x[:, :], out_offset=bass.IndirectOffsetOnAxis(ap=slots[0:n, t, k:k + 1], axis=0),
                        in_=hall[0:n, t, :], in_offset=None).then_inc(signal, 16)

                for t in range(TILES):
                    pool.wait_ge(first_ready, TILES * l + t + 1)
                    for k in range(2):
                        scatter(firstu, t, k, scattered[l])
                pool.wait_ge(over_counted, l + 1)
                n_over = pool.value_load(tables[l][0:1, NOV:NOV + 1], min_val=0, max_val=NOV)
                pool.wait_ge(scattered[l], 16 * 2 * TILES)
                with pool.If(n_over > 0):
                    pool.wait_ge(slots_ready, l + 1)
                    for t in range(TILES):
                        for k in range(2):
                            scatter(slotu, t, k, scattered[l])
                    pool.wait_ge(scattered[l], 2 * 16 * 2 * TILES)
                with pool.Else():
                    pool.nop()
                pool.sem_inc(rows_placed, 1)
                pool.wait_ge(slots_ready, l + 1)
                pool.wait_ge(y_all_stored[l], 1)
                for t in range(TILES):
                    for k in range(2):
                        n = rows_of(t)
                        g = TILES * l + t
                        if t >= 2:
                            pool.wait_ge(gat_used, g - 1)
                        pool.indirect_dma_start(
                            out=gat[2 * (t % 2) + k][0:n, :], out_offset=None, in_=slot_y[:, :],
                            in_offset=bass.IndirectOffsetOnAxis(ap=slotu[0:n, t, k:k + 1], axis=0),
                        ).then_inc(gathered[t % 2], 16)

        @block.scalar
        def _(act):
            link = chained(act, act_chain)
            act.dma_start(gain0, a["norm_mix"][0:1, :].partition_broadcast(P).rearrange("p a d -> p (a d)")).then_inc(gain_in, 16)
            act.dma_start(at(C, 384), consts["c_square"]).then_inc(consts_in, 16)
            act.dma_start(small, consts["c_small"]).then_inc(consts_in, 16)
            with nc.allow_non_contiguous_dma(reason="1024 words of the gates' lower bound, once"):
                for j in range(2):
                    act.dma_start(lbl[:, j, :], a["hgrn_lb"][j].rearrange("(h k) -> k h", k=P)).then_inc(lb_in, 16)
            act.dma_start(onehot[0:BUCKETS + 1], consts["c_onehot"]).then_inc(rel_in, 16)
            act.dma_start(relx[0:BUCKETS, :], a["rel_bias"]).then_inc(rel_in, 16)
            def mean_root(i, t, x_, junk_):
                n = rows_of(t)
                r_ = rms[i % 2][0:n, t:t + 1]
                link(nc.scalar.activation(junk_[0:n], x_, ACT.Square, accum_out=r_))
                nc.scalar.activation(r_, r_, ACT.Sqrt, bias=eps[0:n], scale=1.0 / D).then_inc(root[i % 2], 1)

            act.wait_ge(eps_ready, 1)
            for t in range(TILES + 1):
                if t < TILES:
                    act.wait_ge(x_in[t], 16)
                    mean_root(0, t, xin[t][0:rows_of(t)], junk)
                if t:
                    n = rows_of(t - 1)
                    act.wait_ge(h_turned, t)
                    b = 2 * ((t - 1) % 2)
                    nc.scalar.activation(hT[:, :, (t - 1) * P:(t - 1) * P + n],
                                         ps[:, b:b + 2, :].rearrange("p b (k c) -> p (b k) c", k=4)[:, :, 0:n],
                                         ACT.Copy).then_inc(hT_ready, 1)

            act.wait_ge(lbl_ready, 1)
            nc.scalar.activation(lbl, lbl, ACT.Exp).then_inc(lb_exp, 1)

            PART = {QA: (qT, ACT.Copy), KA: (kT, ACT.Copy), QB: (qbT, ACT.Silu), FB: (fT, ACT.Sigmoid),
                    VA: (vtok, ACT.Copy), IB: (ib, ACT.Copy), GB: (gb, ACT.Silu)}

            def evacuate(unit):
                c = next(c for c in range(7) if unit < UNITS[c])
                m = unit - (UNITS[c - 1] if c else 0)
                act.wait_ge(unit_done, unit + 1)
                if m == NT:
                    sums = partial[c > IB]
                    act.wait_ge(partial_clear, 2 if c > IB else 1)
                    if c:
                        act.wait_ge(part_picked, c)
                    nc.scalar.activation(sums[0:32], ps[0:32, unit % 2, :], ACT.Copy)
                    nc.scalar.activation(sums[64:96], ps[64:96, unit % 2, :], ACT.Copy).then_inc(unit_out, 1)
                else:
                    dst, fn = PART[c]
                    if c == GB and m == 0:
                        act.wait_ge(slots_cleared, 32)
                    to = dst[:, m, 0:SEQ] if c in TURNED_PARTS else dst[:, m, :]
                    nc.scalar.activation(to, ps[:, unit % 2, :], fn).then_inc(unit_out, 1)

            def evacuate_picked(c):
                act.wait_ge(part_picked, c + 1)
                dst, fn = PART[c]
                if c in TURNED_PARTS:
                    nc.scalar.activation(dst[:, :, SEQ:TOK], ps[:, 2, 0:HEADS * NB].rearrange("p (h b) -> p h b", h=HEADS),
                                         fn).then_inc(part_out, 1)
                else:
                    nc.scalar.activation(dst[0:NB, NT, :], ps[0:NB, 2, :], fn).then_inc(part_out, 1)
                if c == VA:
                    act.wait_ge(part_out, c + 1)
                    act.dma_start(v_prompt.rearrange("a b (t p) h d -> p (a b t) (h d)", p=P), vtok[:, 0:NT, :]).then_inc(stored, 16)
                    act.dma_start(v_sample.rearrange("a b t h d -> (a b t) (h d)"), vtok[0:NB, NT, :]).then_inc(vs_stored, 16)

            def decays(h, part):
                if part == 0:
                    act.wait_ge(f_ready, h + 1)
                    nc.scalar.activation(ldif, fT[:, h, 0:SEQ], ACT.Ln).then_inc(logf_ready, 1)
                for step in ((0,), (1, 2), (3,), (4, 5))[part]:
                    act.wait_ge(dif_ready, 6 * h + step + 1)
                    if step < 3:
                        link(nc.scalar.activation(lexp, ldif, ACT.Abs))
                        nc.scalar.activation(lexp, lexp, ACT.Exp, scale=-1.0).then_inc(exp_ready, 1)
                    elif step == 3:
                        link(nc.scalar.activation(lexp, ldif, ACT.Exp))
                        nc.scalar.activation(ldif, ldif, ACT.Exp, scale=-1.0).then_inc(exp_ready, 1)
                    elif step == 4:
                        nc.scalar.activation(lexp, lcum, ACT.Exp).then_inc(exp_ready, 1)
                    else:
                        nc.scalar.activation(lexp, ldif, ACT.Exp, scale=-1.0).then_inc(exp_ready, 1)

            for unit in range(UNITS[IB]):
                evacuate(unit)
                if unit == UNITS[QB]:
                    act.wait_ge(bias_moved, 16)
                    act.dma_start(gnb, a["hgrn_gnorm"][0:1, :].partition_broadcast(P).rearrange("p a d -> p (a d)")).then_inc(gn_in, 16)
                if unit and unit % TILES == 0:
                    evacuate_picked(unit // TILES - 1)
                if UNITS[FB] <= unit < UNITS[FB] + 4:
                    decays(0, unit - UNITS[FB])
            for unit in range(UNITS[IB], UNITS[GB]):
                m = unit - UNITS[IB]
                h, t = m // NT, m % NT
                if m == 0:
                    evacuate_picked(IB)
                if m < HEADS * NT:
                    act.wait_ge(kd_turned, m + 1)
                    nc.scalar.activation(kdtok, ps[:, 4, 0:P], ACT.Copy).then_inc(kdtok_ready, 1)
                    if m and t == 0:
                        act.wait_ge(state_ready, m)
                        act.dma_start(s_prompt[0, 0, h - 1], state[:, h - 1, :]).then_inc(state_stored, 16)
                    if h + 1 < HEADS:
                        decays(h + 1, t)
                evacuate(unit)
                if m and m % TILES == 0:
                    evacuate_picked(unit // TILES - 1)
                if m < HEADS * NT:
                    act.wait_ge(o_done, m + 1)
                    nc.scalar.activation(ib[:, t, h * DH:(h + 1) * DH], ps[:, 5, 0:P], ACT.Copy).then_inc(o_out, 1)
                k = unit - UNITS[VA]
                if k >= 0:
                    n = rows_of(k)
                    act.wait_ge(kt_turned, k + 1)
                    if k == 0:
                        act.wait_ge(ops_ready, HEADS)
                    if k >= 2:
                        act.wait_ge(ktok_stored[k % 2], 16 * (k // 2))
                    nc.scalar.activation(ktok[k % 2][0:n, :], ps[0:n, 7, :], ACT.Copy).then_inc(ktok_ready, 1)
                    act.wait_ge(ktok_ready, k + 1)
                    dst = (k_prompt.rearrange("a b (t p) h d -> p (a b t) (h d)", p=P)[:, k, :] if k < NT
                           else k_sample.rearrange("a b t h d -> (a b t) (h d)"))
                    act.dma_start(dst, ktok[k % 2][0:n, :]).then_inc(ktok_stored[k % 2], 16)
            evacuate_picked(GB)
            act.wait_ge(state_ready, HEADS * NT)
            act.dma_start(s_prompt[0, 0, HEADS - 1], state[:, HEADS - 1, :]).then_inc(state_stored, 16)

            def exponentials(n):
                w = (n % NT + 1) * P
                act.wait_ge(logit_ready, n + 1)
                nc.scalar.activation(prob[n % 2][:, 0:w], prob[n % 2][:, 0:w], ACT.Exp,
                                     bias=astat[:, n:n + 1], accum_out=astat[:, 16 + n:17 + n]).then_inc(prob_ready, 1)

            exponentials(0)
            for n in range(HEADS * NT):
                i = n % NT
                w = (i + 1) * P
                if n + 1 < HEADS * NT:
                    exponentials(n + 1)
                act.wait_ge(prob_turned, n + 1)
                nc.scalar.activation(probT[n % 2][:, 0:i + 1, :],
                                     ps[:, 2 + n % 2, 0:w].rearrange("p (a b) -> p a b", b=P), ACT.Copy).then_inc(probT_ready, 1)
                if n < NB:
                    act.wait_ge(key_turned, n + 1)
                    nc.scalar.activation(keyT[n % 2], ps[:, 6:8, :], ACT.Copy).then_inc(keyT_ready, 1)
                t = n - 11
                if 0 <= t < NT:
                    act.wait_ge(og_turned, t + 1)
                    nc.scalar.activation(catT[:, HEADS:2 * HEADS, t * P:(t + 1) * P],
                                         ps[:, 7, :].rearrange("p (h c) -> p h c", h=HEADS), ACT.Copy).then_inc(og_out, 1)
                t = n - 8
                if 0 <= t < NT:
                    act.wait_ge(ohead_ms, t + 1)
                    nc.scalar.activation(hstat[:, 8 * t + 4:8 * t + 8], hstat[:, 8 * t:8 * t + 4], ACT.Sqrt).then_inc(ohead_root, 1)
                t = n - 6
                if 0 <= t < NT:
                    if t == 0:
                        act.wait_ge(state_stored, 16 * HEADS)
                    else:
                        act.wait_ge(ohead_ms, t)
                    nc.scalar.activation(sq.rearrange("p a b -> p (a b)"), ib[:, t, :], ACT.Square).then_inc(ohead_sq, 1)
            act.wait_ge(vs_stored, 16)
            act.wait_ge(att_out, HEADS * NT)
            act.wait_ge(qkself_ready, 1)
            act.wait_ge(stored, 16)
            for t in range(TILES):
                act.dma_start(x[0:rows_of(t), t, :], x_rows(t)).then_inc(xres_in, 16)
            act.dma_start(vrow[0:32], v_sample.rearrange("a b t h d -> (a b t h) d")).then_inc(vrow_in, 16)
            act.dma_start(gncol, a["hgrn_gnorm"][0].rearrange("(k a) -> k a", a=1)).then_inc(gn_in, 16)
            act.wait_ge(snew_ready, NB)
            act.dma_start(s_sample[0].rearrange("b h k v -> k b h v"), stv[:, :, :, :]).then_inc(snew_stored, 16)
            act.wait_ge(dlog_ready, 1)
            nc.scalar.activation(dprob[0:32], dlog[0:32], ACT.Exp, bias=dstat[0:32, 0:1],
                                 accum_out=dstat[0:32, 1:2]).then_inc(dprob_exp, 1)
            act.wait_ge(oms_ready, 1)
            nc.scalar.activation(sstat[:, 32:64], sstat[:, 0:32], ACT.Sqrt).then_inc(oroot, 1)

            act.wait_ge(mixers_done, 1)
            act.dma_start(gain[1], a["norm_ffn"][0:1, :].partition_broadcast(P).rearrange("p a d -> p (a d)")).then_inc(router_in, 16)
            for l in range(2):
                act.dma_start(wr[:, l, :, 0:NG], a["moe_wg_group"][l].rearrange("(k p) g -> p k g", p=P)).then_inc(router_in, 16)
                act.dma_start(wr[:, l, :, NG:], a["moe_wg_exp"][l].rearrange("(k p) g -> p k g", p=P)).then_inc(router_in, 16)
                act.dma_start(rbias[:, l, 0:NG], a["moe_bg_group"][l:l + 1, :].partition_broadcast(P).rearrange("p a d -> p (a d)")).then_inc(router_in, 16)
                act.dma_start(rbias[:, l, NG:], a["moe_bg_exp"][l:l + 1, :].partition_broadcast(P).rearrange("p a d -> p (a d)")).then_inc(router_in, 16)
            act.dma_start(at(22216, 1536 + 64), consts["c_pool"]).then_inc(pool_in, 16)
            act.dma_start(prev[0:NB * KEEP], a["state_pool"][0].rearrange("b r d -> (b r) d")).then_inc(pool_in, 16)
            act.dma_start(pscale, a["pool_scale"].partition_broadcast(P).rearrange("p a d -> p (a d)")).then_inc(pool_in, 16)
            act.dma_start(gain[0], a["norm_mix"][1:2, :].partition_broadcast(P).rearrange("p a d -> p (a d)")).then_inc(pool_in, 16)

            def experts(l):
                lag = 1 if l == 0 else 3
                for u in range(TILES + lag):
                    t = u
                    if l == 1:
                        if t < TILES:
                            act.wait_ge(gat_used, t + 1)
                            mean_root(2, t, x[0:rows_of(t), t, :], spare)
                        t = u - 1
                        if 0 <= t < TILES:
                            act.wait_ge(mix_done, t + 1)
                            if t:
                                act.wait_ge(pool_done, t)
                            nc.scalar.activation(mixT[:, :, 0:rows_of(t)],
                                                 ps[:, 0:2, :].rearrange("p b (k c) -> p (b k) c", k=4)[:, :, 0:rows_of(t)],
                                                 ACT.Copy).then_inc(mixT_ready, 1)
                            if t == NT - 1:
                                act.dma_start(p_prompt[0, 0], hall[P - KEEP:P, t, :]).then_inc(pooled_stored, 16)
                            if t == NT:
                                act.dma_start(p_sample[0].rearrange("b t d -> (b t) d"), hall[0:NB, t, :]).then_inc(pooled_stored, 16)
                                act.dma_start(gain[0], a["norm_final"].rearrange("(a d) -> a d", a=1).partition_broadcast(P).rearrange("p a d -> p (a d)")).then_inc(router_in, 16)
                        t = u - 2
                        if 0 <= t < TILES:
                            act.wait_ge(x_added, TILES + t + 1)
                            mean_root(3, t, x[0:rows_of(t), t, :], spare)
                    t = u - lag
                    if 0 <= t < TILES:
                        g = TILES * l + t
                        n = rows_of(t)
                        b = 6 * l
                        act.wait_ge(hn_turned, g + 1)
                        if g:
                            act.wait_ge(rlog_done, g)
                        nc.scalar.activation(htile[:, :, 0:n],
                                             ps[:, b:b + 2, :].rearrange("p b (k c) -> p (b k) c", k=4)[:, :, 0:n],
                                             ACT.Copy).then_inc(htile_ready, 1)
                    if l == 0 and u == NT:
                        act.wait_ge(wo_done, 2 * TILES)
                        act.wait_ge(partial_clear, 3)
                        nc.scalar.activation(partial_late[0:32], ps[0:32, 4:6, :], ACT.Copy)
                        nc.scalar.activation(partial_late[64:96], ps[64:96, 4:6, :], ACT.Copy).then_inc(part_out, 1)
                    if l == 0 and u < TILES:
                        act.wait_ge(x_added, u + 1)
                        mean_root(1, u, x[0:rows_of(u), u, :], spare)
                if l == 0:
                    act.wait_ge(hn_ready, TILES)
                    act.dma_start(gain[1], a["norm_ffn"][1:2, :].partition_broadcast(P).rearrange("p a d -> p (a d)")).then_inc(router_in, 16)
                    act.wait_ge(wo_done, 2 * TILES)
                    for g in range(NG):
                        act.dma_start(poolw[:, g], a["pool_w"][0, g].rearrange("(k p) c -> p k c", p=P)).then_inc(pool_in, 16)
                act.wait_ge(mem_ready, TILES * (l + 1))
                nc.scalar.activation(dexp, dexp, ACT.Exp).then_inc(gexp_ready, 1)
                def load_rows(i):
                    act.dma_start(xg, slot_x[bass.ds(i * 2 * CAP, 2 * CAP), :]).then_inc(xg_in, 16)

                def pair(i, first, last):
                    if not last:
                        act.wait_ge(x_turned, PAIRS * l + i + 1)
                        load_rows(i + 1)
                    act.wait_ge(h_done, PAIRS * l + i + 1)
                    nc.scalar.activation(sg, ps[:, 2, :], ACT.Silu).then_inc(silu_ready, 1)
                    act.wait_ge(y_done, PAIRS * l + i + 1)
                    if not first:
                        act.wait_ge(y_stored, 16 * PAIRS * l + 16 * i)
                    nc.scalar.activation(yst, ps[:, 5:7, :].rearrange("p a b -> p (a b)"), ACT.Copy).then_inc(y_out, 1)
                    act.wait_ge(y_out, PAIRS * l + i + 1)
                    act.dma_start(slot_y[bass.ds(i * 2 * CAP, 2 * CAP), :], yst).then_inc(y_stored, 16)

                act.wait_ge(rows_placed, l + 1)
                load_rows(0)
                pair(0, True, False)
                with act.Fori(1, PAIRS - 1) as i:
                    pair(i, False, False)
                pair(PAIRS - 1, False, True)
                act.wait_ge(y_stored, 16 * PAIRS * (l + 1))
                act.wait_ge(tables_ready, l + 1)
                n_over = act.value_load(tables[l][0:1, NOV:NOV + 1], min_val=0, max_val=NOV)
                with act.If(n_over > 0):
                    with act.Fori(0, NOV) as j:
                        with act.If(n_over > j):
                            act.dma_start(xg[0:CAP, :], slot_rows(slot_x, NE + j)).then_inc(over_in[l], 16)
                            act.wait_ge(over_step[l], over_count(j, PRODUCTS))
                            nc.scalar.activation(sg[0:CAP], ps[0:CAP, 2, :], ACT.Silu).then_inc(over_step[l], 1)
                            act.wait_ge(over_step[l], over_count(j, ROWS))
                            nc.scalar.activation(yst[0:CAP, :], ps[0:CAP, 5:7, :].rearrange("p a b -> p (a b)"),
                                                 ACT.Copy).then_inc(over_step[l], 1)
                            act.wait_ge(over_step[l], over_count(j, OUT))
                            act.dma_start(slot_rows(slot_y, NE + j), yst[0:CAP, :]).then_inc(over_stored[l], 16)
                            act.wait_ge(over_stored[l], 16 * j + 16)
                            act.sem_inc(over_seen, 1)
                        with act.Else():
                            act.nop()
                    act.nop()
                with act.Else():
                    act.nop()
                act.sem_inc(y_all_stored[l], 1)

            experts(0)
            experts(1)
            for u in range(TILES + 1):
                if u < TILES:
                    act.wait_ge(gat_used, TILES + u + 1)
                    mean_root(4, u, x[0:rows_of(u), u, :], spare)
                t = u - 1
                if t >= 0:
                    act.wait_ge(y_final, t + 1)
                    dst = y_prompt.rearrange("b (t p) d -> p (b t) d", p=P)[:, t, :] if t < NT else y_sample.rearrange("b t d -> (b t) d")
                    act.dma_start(dst, x[0:rows_of(t), t, :]).then_inc(stored, 16)
            act.wait_ge(stored, 16 * (1 + TILES))
            act.wait_ge(pooled_stored, 32)
            act.wait_ge(vs_stored, 16)
            for i in range(2):
                act.wait_ge(ktok_stored[i], 16 * len(range(i, TILES, 2)))
            act.wait_ge(state_stored, 16 * HEADS)
            act.wait_ge(snew_stored, 16)

        @block.vector
        def _(dve):
            link = chained(dve, dve_chain)
            V = nc.vector

            def normed_rows(i, t, x_, gain_, to):
                n = rows_of(t)
                r_ = rms[i % 2][0:n, t:t + 1]
                dve.wait_ge(root[i % 2], TILES * (i // 2) + t + 1)
                link(V.reciprocal(r_, r_))
                return V.scalar_tensor_tensor(to, x_, r_, gain_[0:n], ALU.mult, ALU.mult)

            V.memset(eps, EPS).then_inc(eps_ready, 1)
            dve.wait_ge(gain_in, 16)
            for t in range(TILES):
                if t:
                    dve.wait_ge(h_turned, t)
                dve.wait_ge(x_in[t], 16)
                normed_rows(0, t, xin[t][0:rows_of(t)], gain0, hrow[0:rows_of(t)]).then_inc(h_ready, 1)
            dve.wait_ge(h_ready, TILES)
            V.memset(partial[0], 0.0)
            V.tensor_tensor(pick, ident[:, 32 - NB:32], ident[:, 96 - NB:96], ALU.add).then_inc(partial_clear, 1)
            dve.wait_ge(rel_in, 32)
            V.memset(relx[BUCKETS:BUCKETS + 1, :], 1.0).then_inc(rel_ready, 1)
            dve.wait_ge(rel_ready, 1)
            V.tensor_copy(relrep[0:BUCKETS + 1], wide(relx[0:BUCKETS + 1, :], [BUCKETS + 1, NB, HEADS], 1)).then_inc(rel_ready, 1)
            dve.wait_ge(brow_done, 1)
            V.tensor_copy(brow[0:HEADS], ps[0:HEADS, 6:8, :].rearrange("p a b -> p (a b)")[:, 0:ROWW]).then_inc(brow_ready, 1)
            dve.wait_ge(lb_in, 32)
            link(V.tensor_tensor(lbs, lbl[:, 0, :], lbl[:, 1, :], ALU.max))
            V.tensor_tensor(lbl, lbl, wide(lbs, [P, 2, HEADS], 1), ALU.subtract).then_inc(lbl_ready, 1)

            dve.wait_ge(lb_exp, 1)
            link(V.tensor_tensor(lbs, lbl[:, 0, :], lbl[:, 1, :], ALU.add))
            link(V.reciprocal(lbs, lbs))
            link(V.tensor_tensor(lb, lbl[:, 0, :], lbs, ALU.mult))
            link(V.tensor_scalar(oml, lb, -1.0, 1.0, ALU.mult, ALU.add))
            dve.wait_ge(masks_in, 16)
            dve.wait_ge(bias_moved, 16)
            dve.wait_ge(part_out, FB + 1)
            V.memset(partial[1], 0.0).then_inc(partial_clear, 1)

            def blocks(ap, n):
                return ap.rearrange("p (b n) -> p b n", n=n)

            def operands(h, part):
                q_ = qbT[:, h, 0:SEQ]
                f_ = fT[:, h, 0:SEQ]
                s = h % 2

                def differ(n, at_):
                    V.tensor_tensor(blocks(ldif, n), blocks(lcum, n),
                                    blocks(lcum, n)[:, :, at_:at_ + 1].broadcast_to([P, SEQ // n, n]), ALU.subtract).then_inc(dif_ready, 1)

                def exped(step):
                    dve.wait_ge(exp_ready, 6 * h + step + 1)

                def level(j):
                    n = LEVELS[j]
                    differ(n, n // 2 - 1)
                    exped(j)
                    w_, e_ = blocks(wl[s][j], n), blocks(lexp, n)
                    V.tensor_tensor(w_[:, :, n // 2:], blocks(q_, n)[:, :, n // 2:], e_[:, :, n // 2:], ALU.mult)
                    link(V.tensor_tensor(w_[:, :, :n // 2], blocks(f_, n)[:, :, :n // 2], e_[:, :, :n // 2], ALU.mult))

                if part == 0:
                    V.tensor_scalar(fT[:, h, :], fT[:, h, :], oml[:, h:h + 1], lb[:, h:h + 1], ALU.mult, ALU.add).then_inc(f_ready, 1)
                    dve.wait_ge(logf_ready, h + 1)
                    link(V.tensor_tensor_scan(lcum, reset, ldif, 0.0, ALU.mult, ALU.add))
                    link(V.tensor_scalar(f_, f_, -1.0, 1.0, ALU.mult, ALU.add))
                    if h >= 2:
                        dve.wait_ge(o_done, NT * (h - 1))
                    level(0)
                elif part == 1:
                    level(1)
                    level(2)
                elif part == 2:
                    differ(16, 7)
                    exped(3)
                    link(V.tensor_tensor(q16[s], q_, lexp, ALU.mult))
                    link(V.tensor_tensor(k16[s], f_, ldif, ALU.mult))
                else:
                    dve.sem_inc(dif_ready, 1)
                    exped(4)
                    link(V.tensor_tensor(qc[s], q_, lexp, ALU.mult))
                    link(V.tensor_copy(hstat[:, 64 + 4 * h:68 + 4 * h].unsqueeze(2), blocks(lexp, P)[:, :, P - 1:P]))
                    differ(P, P - 1)
                    exped(5)
                    V.tensor_tensor(kdT[s], f_, lexp, ALU.mult).then_inc(ops_ready, 1)
                    dve.wait_ge(ops_ready, h + 1)

            for part in range(4):
                operands(0, part)
            for h in range(HEADS):
                for t in range(NT):
                    m = NT * h + t
                    dve.wait_ge(lvl_done, m + 1)
                    V.scalar_tensor_tensor(smask.rearrange("p a b -> p (a b)"), ps[:, 3, :], 3e38,
                                           masks.rearrange("p a b -> p (a b)"), ALU.min, ALU.mult).then_inc(smask_ready, 1)
                    if h + 1 < HEADS:
                        if m == 0:
                            dve.wait_ge(unit_done, UNITS[IB])
                        operands(h + 1, t)
                    dve.wait_ge(o_done, m + 1)
                    new = ps[:, 6, 0:P]
                    if t == 0:
                        V.tensor_copy(state[:, h, :], new).then_inc(state_ready, 1)
                    else:
                        dve.wait_ge(state_ready, m)
                        V.scalar_tensor_tensor(state[:, h, :], state[:, h, :], hstat[:, 64 + 4 * h + t:65 + 4 * h + t], new,
                                               ALU.mult, ALU.add).then_inc(state_ready, 1)
            def logits(n):
                h, i = n // NT, n % NT
                w = (i + 1) * P
                dve.wait_ge(logit_done, n + 1)
                if n >= 2:
                    dve.wait_ge(prob_turned, n - 1)
                if n == 0:
                    dve.wait_ge(bias_moved, 32)
                link(V.scalar_tensor_tensor(prob[n % 2][:, 0:w], ps[:, n % 2, 0:w], SCALE, toep[:, h, SEQ - w:SEQ], ALU.mult, ALU.add))
                V.tensor_reduce(astat[:, n:n + 1], prob[n % 2][:, 0:w], AX.X, ALU.max, negate=True).then_inc(logit_ready, 1)

            def normed(n):
                w = (n % NT + 1) * P
                dve.wait_ge(prob_ready, n + 1)
                link(V.reciprocal(astat[:, 32 + n:33 + n], astat[:, 16 + n:17 + n]))
                V.tensor_scalar(prob[n % 2][:, 0:w], prob[n % 2][:, 0:w], astat[:, 32 + n:33 + n], None, ALU.mult).then_inc(prob_normed, 1)

            def out_heads(n):
                h, i = n // NT, n % NT
                dve.wait_ge(att_done, n + 1)
                V.tensor_copy(catT[:, h, i * P:(i + 1) * P], ps[:, 4, 0:P]).then_inc(att_out, 1)

            def head_squares(t):
                dve.wait_ge(ohead_sq, t + 1)
                link(V.tensor_reduce(hstat[:, 8 * t:8 * t + 4], sq, AX.X, ALU.add))
                V.tensor_scalar(hstat[:, 8 * t:8 * t + 4], hstat[:, 8 * t:8 * t + 4], 1.0 / DH, EPS, ALU.mult, ALU.add).then_inc(ohead_ms, 1)

            def head_scaled(t):
                dve.wait_ge(ohead_root, t + 1)
                r_ = hstat[:, 8 * t + 4:8 * t + 8]
                link(V.reciprocal(r_, r_))
                if t:
                    dve.wait_ge(og_turned, t)
                o_ = ib[:, t, :].rearrange("p (h v) -> p h v", h=HEADS)
                link(V.tensor_tensor(ostage, o_, wide(r_, [P, HEADS, DH], 2), ALU.mult))
                link(V.tensor_tensor(ostage, ostage, wide(gnb, [P, HEADS, DH], 1), ALU.mult))
                V.tensor_tensor(ostage.rearrange("p h v -> p (h v)"), ostage.rearrange("p h v -> p (h v)"), gb[:, t, :],
                                ALU.mult).then_inc(og_ready, 1)

            fs = fT[:, :, SEQ:TOK]
            ks = sstat[:, 64:96].rearrange("p (h b) -> p h b", h=HEADS)

            def value_of(b):
                if b >= 2:
                    dve.wait_ge(vb_done, b - 1)
                V.tensor_scalar(vonly[b % 2][0:NB], ib[0:NB, NT, :], ident[0:NB, b:b + 1], None, ALU.mult).then_inc(vonly_ready, 1)

            def sample_state(b):
                dve.wait_ge(vb_done, b + 1)
                if b >= 2:
                    dve.wait_ge(snew_ready, b - 1)
                V.tensor_tensor(tmp_kv[b % 2], ps[:, 6, :].rearrange("p (h v) -> p h v", h=HEADS),
                                ks[:, :, b:b + 1].broadcast_to([P, HEADS, DH]), ALU.mult).then_inc(kv_ready, 1)

            link(V.tensor_scalar(ks, fs, -1.0, 1.0, ALU.mult, ALU.add))
            dve.sem_inc(fs_ready, 1)
            dve.wait_ge(part_out, GB + 1)
            logits(0)
            for n in range(HEADS * NT):
                if n + 1 < HEADS * NT:
                    logits(n + 1)
                normed(n)
                if n:
                    out_heads(n - 1)
                if 0 <= n - 9 < NT:
                    head_scaled(n - 9)
                if 0 <= n - 7 < NT:
                    head_squares(n - 7)
                t = n - NB
                if t == -1:
                    dve.wait_ge(ktok_stored[1], 32)
                    dve.wait_ge(gn_in, 16)
                    value_of(0)
                if t >= 0:
                    if t + 1 < NB:
                        value_of(t + 1)
                    sample_state(t)
            out_heads(HEADS * NT - 1)
            dve.wait_ge(att_out, HEADS * NT)
            V.tensor_tensor(qkself.rearrange("p b h -> p h b"), qT[:, :, SEQ:TOK], kT[:, :, SEQ:TOK], ALU.mult).then_inc(qkself_ready, 1)
            dve.wait_ge(dscore_done, NB)
            V.tensor_copy(dscT.rearrange("p t b h -> p (t b h)"), ps[:, 5, 0:64]).then_inc(dscT_ready, 1)
            link(V.memset(pspread, 0.0))
            dve.wait_ge(sample_step, BIASES)
            link(V.tensor_copy(dbias[0:32], ps[0:32, 0, 0:NDEC]))
            dve.wait_ge(sample_step, LOGITS)
            link(V.scalar_tensor_tensor(dlog[0:32], ps[0:32, 2, 0:NDEC], SCALE, dbias[0:32], ALU.mult, ALU.add))
            V.tensor_reduce(dstat[0:32, 0:1], dlog[0:32], AX.X, ALU.max, negate=True).then_inc(dlog_ready, 1)
            dve.wait_ge(dprob_exp, 1)
            link(V.reciprocal(dstat[0:32, 2:3], dstat[0:32, 1:2]))
            link(V.tensor_scalar(dprob[0:32], dprob[0:32], dstat[0:32, 2:3], None, ALU.mult))
            V.tensor_scalar(diag[0:32], ident[0:32, 0:32], dprob[0:32, NDEC - 1:NDEC], None, ALU.mult).then_inc(dprob_ready, 1)
            dve.wait_ge(sample_step, PROBS_TURNED)
            for t in range(2):
                V.tensor_copy(pspread[:, t, :].rearrange("p (b r) -> p b r", b=NB)[:, :, 0:HEADS],
                              ps[:, 3, t * 32:(t + 1) * 32].rearrange("p (b h) -> p b h", b=NB)).then_inc(dprobT_ready, 1)
            dve.wait_ge(sample_step, STATE_OUT)
            V.tensor_copy(gsT.rearrange("p h b -> p (h b)"), ps[:, 1, 32:64])
            link(V.tensor_copy(osT.rearrange("p h b -> p (h b)"), ps[:, 1, 0:32]))
            V.tensor_tensor(osq, osT.rearrange("p h b -> p (h b)"), osT.rearrange("p h b -> p (h b)"), ALU.mult).then_inc(osq_ready, 1)
            dve.wait_ge(sample_step, SQUARES_SUMMED)
            V.tensor_scalar(sstat[:, 0:32], ps[:, 1, 0:32], 1.0 / DH, EPS, ALU.mult, ALU.add).then_inc(oms_ready, 1)
            dve.wait_ge(oroot, 1)
            link(V.reciprocal(sstat[:, 32:64], sstat[:, 32:64]))
            dve.wait_ge(gn_in, 32)
            link(V.scalar_tensor_tensor(osT.rearrange("p h b -> p (h b)"), osT.rearrange("p h b -> p (h b)"), gncol[:, 0:1],
                                        sstat[:, 32:64], ALU.mult, ALU.mult))
            V.tensor_tensor(catT[:, HEADS:, SEQ:TOK], osT, gsT, ALU.mult).then_inc(cat_ready, 1)
            dve.wait_ge(sample_step, ATTENDED)
            V.tensor_copy(dheads[0:32], ps[0:32, 0, :]).then_inc(dheads_ready, 1)
            dve.wait_ge(sample_step, HEADS_TURNED)
            V.tensor_copy(catT[:, 0:HEADS, SEQ:TOK],
                          ps[:, 3, 0:HEADS * (4 * NB + 1)].rearrange("p (h r) -> p h r", h=HEADS)[:, :, 0:4 * NB:HEADS]).then_inc(cat_ready, 1)
            dve.wait_ge(cat_ready, 2)
            dve.wait_ge(og_out, NT)
            dve.wait_ge(state_stored, 16 * HEADS)
            dve.wait_ge(stored, 16)
            dve.wait_ge(vs_stored, 16)
            for i in range(2):
                dve.wait_ge(ktok_stored[i], 16 * len(range(i, TILES, 2)))
            dve.sem_inc(mixers_done, 1)
            V.memset(partial_late, 0.0)
            V.tensor_tensor(pick_late, ident[:, 32 - NB:32], ident[:, 96 - NB:96], ALU.add).then_inc(partial_clear, 1)
            def taken(t):
                return mem[:, 0, :] if t == 1 else over[:, t - 1, :]

            def combine(l, t):
                n = rows_of(t)
                uses = len(range(t % 2, TILES, 2)) * l + t // 2 + 1
                dve.wait_ge(gathered[t % 2], 32 * uses)
                link(V.scalar_tensor_tensor(x[0:n, t, :], gat[2 * (t % 2)][0:n], gates[0:n, t, 0:1], x[0:n, t, :], ALU.mult, ALU.add))
                V.scalar_tensor_tensor(x[0:n, t, :], gat[2 * (t % 2) + 1][0:n], gates[0:n, t, 1:2], x[0:n, t, :],
                                       ALU.mult, ALU.add).then_inc(gat_used, 1)

            def add_mix(l, t):
                n = rows_of(t)
                if l == 0:
                    dve.wait_ge(wo_done, (3, 4, 6, 8, 11)[t])
                    if t == 0:
                        dve.wait_ge(xres_in, 16 * TILES)
                    b = (4, 6, 4, 6, 6)[t]
                else:
                    dve.wait_ge(pool_done, t + 1)
                    b = 4
                V.tensor_tensor(x[0:n, t, :], x[0:n, t, :], ps[0:n, b:b + 2, :].rearrange("p a b -> p (a b)"), ALU.add).then_inc(x_added, 1)

            def experts(l):
                link(V.memset(lg, 0.0))
                link(V.memset(g8, NEG))

                if l == 0:
                    link(V.tensor_scalar(spares, iota[:, 0:2 * TILES], float(P), None, ALU.mult))
                    link(V.tensor_tensor(spares, spares, spare_row.broadcast_to([P, 2 * TILES]), ALU.add))

                def normed_h(t):
                    if t == 0:
                        dve.wait_ge(router_in, 16 * (9 + l))
                    if l:
                        dve.wait_ge(mix_done, min(t + 2, TILES))
                        if t == NT - 1:
                            dve.wait_ge(pooled_stored, 32)
                    normed_rows(1 + 2 * l, t, x[0:rows_of(t), t, :], gain[1], hall[0:rows_of(t), t, :]).then_inc(hn_ready, 1)

                def route(t):
                    n = rows_of(t)
                    g = TILES * l + t
                    one = slice(t, t + 1)
                    dve.wait_ge(rlog_done, g + 1)
                    V.tensor_tensor(lg[0:n, t, :], ps[0:n, 2, 0:NG + NE], rbias[0:n, l, :], ALU.add).then_inc(lg_ready, 1)
                    dve.wait_ge(lg_ready, g + 1)
                    link(V.tensor_copy(g8[:, t, 0:NG], lg[:, t, 0:NG]))
                    link(V.max(gm8[:, t, :], g8[:, t, :]))
                    link(V.max_index(gi8[:, t, :], gm8[:, t, :], g8[:, t, :]))
                    link(V.tensor_copy(gsel[:, one], gi8[:, t, 0:1]))
                    link(V.tensor_tensor(g4[:, t, :], iota[:, 0:NG], gsel[:, one].broadcast_to([P, NG]), ALU.is_equal))
                    link(V.tensor_tensor(sel[:, t], lg[:, t, NG:].rearrange("p (g e) -> p g e", g=NG),
                                         wide(g4[:, t, :], [P, NG, EPG], 2), ALU.mult))
                    link(V.tensor_reduce(e8[:, t, :], sel[:, t].rearrange("p g e -> p e g"), AX.X, ALU.add))
                    link(V.max(em8[:, t, :], e8[:, t, :]))
                    link(V.max_index(ei8[:, t, :], em8[:, t, :], e8[:, t, :]))
                    V.tensor_tensor(dexp[:, t, 0:NG], lg[:, t, 0:NG], gm8[:, t, 0:1].broadcast_to([P, NG]), ALU.subtract)
                    V.tensor_tensor(dexp[:, t, NG:NG + 1], em8[:, t, 1:2], em8[:, t, 0:1], ALU.subtract)
                    link(V.tensor_copy(eid[:, t, :], ei8[:, t, 0:2]))
                    link(V.scalar_tensor_tensor(eid[:, t, :], gsel[:, one].broadcast_to([P, 2]), float(EPG), eid[:, t, :], ALU.mult, ALU.add))
                    link(V.tensor_tensor(oh[:, t], wide(iota, [P, 2, NE], 1), wide(eid[:, t, :], [P, 2, NE], 2), ALU.is_equal))
                    link(V.tensor_tensor(mem[:, t, :], oh[:, t, 0, :], oh[:, t, 1, :], ALU.add))
                    last = V.tensor_tensor(mem[:, t, :], mem[:, t, :], valid[:, one].broadcast_to([P, NE]), ALU.mult)
                    if t:
                        link(last)
                        last = V.tensor_tensor(taken(t + 1), taken(t), mem[:, t, :], ALU.add)
                    last.then_inc(mem_ready, 1)
                    dve.wait_ge(mem_ready, g + 1)

                def first_slots(t):
                    g = TILES * l + t
                    dve.wait_ge(rank_done, g + 1)
                    rank = ps[:, 3, t * NE:(t + 1) * NE]
                    V.tensor_scalar(novx, rank, float(CAP), None, ALU.is_ge)
                    link(V.tensor_tensor(place, rank, ebase, ALU.add))
                    for k in range(2):
                        link(V.scalar_tensor_tensor(placed[:, k, :], novx, spares[:, 2 * t + k:2 * t + k + 1], place, ALU.mult, ALU.max))
                    link(V.tensor_tensor(placed, oh[:, t], placed, ALU.mult))
                    link(V.tensor_reduce(firstf, placed, AX.X, ALU.add))
                    V.tensor_copy(firstu[:, t, :], firstf).then_inc(first_ready, 1)
                    dve.wait_ge(first_ready, g + 1)

                if l == 0:
                    for u in range(TILES + 3):
                        if 0 <= u - 1 < TILES:
                            normed_h(u - 1)
                        if u >= 3:
                            first_slots(u - 3)
                        if 2 <= u < TILES + 2:
                            route(u - 2)
                        if u < TILES:
                            add_mix(0, u)
                else:
                    for u in range(TILES + 5):
                        if u < TILES:
                            combine(0, u)
                        t = u - 1
                        if 0 <= t < TILES:
                            if t == 0:
                                dve.wait_ge(pool_in, 16 * (4 + NG))
                            normed_rows(2, t, x[0:rows_of(t), t, :], gain[0], hall[0:rows_of(t), t, :]).then_inc(pooled_in, 1)
                        if 0 <= u - 2 < TILES:
                            add_mix(1, u - 2)
                        if 0 <= u - 3 < TILES:
                            normed_h(u - 3)
                        if u >= 5:
                            first_slots(u - 5)
                        if 4 <= u < TILES + 4:
                            route(u - 4)
                rank = ps[:, 3, 0:TILES * NE].rearrange("p (t e) -> p t e", e=NE)
                count = ps[:, 3, TILES * NE:(TILES + 1) * NE]
                link(V.tensor_tensor(cmp, wide(count, [P, NE, THR], 2), wide(thr, [P, NE, THR], 1), ALU.is_gt))
                link(V.tensor_reduce(novx, cmp, AX.X, ALU.add))
                link(V.tensor_tensor_scan(ovend, ones32, novx, 0.0, ALU.mult, ALU.add))
                V.tensor_copy(tables[l][:, NOV:NOV + 1], ovend[:, NE - 1:NE]).then_inc(over_counted, 1)
                link(V.tensor_tensor(dbase, ovend, novx, ALU.subtract))
                link(V.tensor_scalar(dbase, dbase, float(CAP), float((NE - 1) * CAP), ALU.mult, ALU.add))
                link(V.tensor_tensor(dbase, dbase, ebase, ALU.subtract))
                link(V.tensor_scalar(over, rank, float(CAP), None, ALU.is_ge))
                link(V.tensor_tensor(over, over, wide(dbase, [P, TILES, NE], 1), ALU.mult))
                link(V.tensor_tensor(over, over, rank, ALU.add))
                link(V.tensor_tensor(over, over, wide(ebase, [P, TILES, NE], 1), ALU.add))
                V.tensor_tensor(ohs[:, :, 0, :], oh[:, :, 0, :], over, ALU.mult)
                link(V.tensor_tensor(ohs[:, :, 1, :], oh[:, :, 1, :], over, ALU.mult))
                link(V.tensor_reduce(slotf, ohs, AX.X, ALU.add))
                V.tensor_copy(slotu, slotf).then_inc(slots_ready, 1)
                link(V.tensor_tensor(ecmp, wide(ovend, [P, NOV, NE], 1), wide(small[:, 0:NOV], [P, NOV, NE], 2), ALU.is_le))
                link(V.tensor_reduce(ovf, ecmp, AX.X, ALU.add))
                link(V.tensor_scalar(ovf, ovf, float(NE - 1), None, ALU.min))
                V.tensor_copy(tables[l][:, 0:NOV], ovf).then_inc(tables_ready, 1)
                dve.wait_ge(gexp_ready, l + 1)
                link(V.tensor_reduce(gden, dexp[:, :, 0:NG], AX.X, ALU.add))
                w_ = dexp[:, :, NG:NG + 1]
                link(V.tensor_scalar(gates[:, :, 1:2], w_, 1.0, None, ALU.add))
                link(V.tensor_tensor(gates[:, :, 1:2], gates[:, :, 1:2], gden.unsqueeze(2), ALU.mult))
                link(V.reciprocal(gates[:, :, 0:1], gates[:, :, 1:2]))
                link(V.tensor_tensor(gates[:, :, 1:2], gates[:, :, 0:1], w_, ALU.mult))

                def gated(i, first):
                    dve.wait_ge(silu_ready, PAIRS * l + i + 1)
                    if not first:
                        dve.wait_ge(hact_turned, PAIRS * l + i)
                    V.tensor_tensor(hact, sg, ps[:, 3, :], ALU.mult).then_inc(hact_ready, 1)
                    dve.wait_ge(hact_turned, PAIRS * l + i + 1)
                    if not first:
                        dve.wait_ge(y_done, PAIRS * l + i)
                    V.tensor_copy(hactT.rearrange("p k c -> p (k c)"), ps[:, 4, :]).then_inc(hactT_ready, 1)

                def columns(i, first):
                    dve.wait_ge(x_turned, PAIRS * l + i + 1)
                    if not first:
                        dve.wait_ge(h_done, PAIRS * l + i)
                    V.tensor_copy(xgT.rearrange("p k c -> p (k c)"), ps[:, 0:2, :].rearrange("p a b -> p (a b)")).then_inc(xT_ready, 1)

                columns(0, True)
                gated(0, True)
                columns(1, False)
                if l == 0:
                    dve.wait_ge(pool_in, 16 * (4 + NG))
                    link(V.tensor_tensor(poolw, poolw, wide(pscale.rearrange("p (g c) -> p g c", g=NG), [P, NG, 2, 256], 2), ALU.mult))
                with dve.Fori(1, PAIRS - 1) as i:
                    gated(i, False)
                    columns(i + 1, False)
                gated(PAIRS - 1, False)
                n_over = dve.value_load(tables[l][0:1, NOV:NOV + 1], min_val=0, max_val=NOV)
                with dve.If(n_over > 0):
                    with dve.Fori(0, NOV) as j:
                        with dve.If(n_over > j):
                            dve.wait_ge(over_step[l], over_count(j, TURNED))
                            V.tensor_copy(xgT[:, :, 0:CAP], ps[:, 0, :].rearrange("p (k c) -> p k c", k=KC)).then_inc(over_step[l], 1)
                            dve.wait_ge(over_step[l], over_count(j, SILU))
                            V.tensor_tensor(hact[0:CAP], sg[0:CAP], ps[0:CAP, 3, :], ALU.mult).then_inc(over_step[l], 1)
                            dve.wait_ge(over_step[l], over_count(j, ACT_TURNED))
                            V.tensor_copy(hactT[:, :, 0:CAP], ps[:, 4, 0:FC * CAP].rearrange("p (k c) -> p k c", k=FC)).then_inc(over_step[l], 1)
                        with dve.Else():
                            dve.nop()
                    dve.nop()
                with dve.Else():
                    dve.nop()

            experts(0)
            experts(1)
            for u in range(TILES + 1):
                if u < TILES:
                    combine(1, u)
                t = u - 1
                if t >= 0:
                    if t == 0:
                        dve.wait_ge(router_in, 16 * 11)
                    normed_rows(4, t, x[0:rows_of(t), t, :], gain[0], x[0:rows_of(t), t, :]).then_inc(y_final, 1)

        @block.tensor
        def _(pe):
            T = nc.tensor
            pe.wait_ge(consts_in, 32)
            for t in range(TILES):
                n = rows_of(t)
                pe.wait_ge(h_ready, t + 1)
                if t >= 2:
                    pe.wait_ge(hT_ready, t - 1)
                for k in range(KC):
                    last = T.transpose(ps[:, 2 * (t % 2) + k // 4, (k % 4) * P:(k % 4) * P + n], hrow[0:n, k * P:(k + 1) * P], ident[0:n, 0:n])
                last.then_inc(h_turned, 1)
            pe.wait_ge(rel_ready, 2)
            for j, (lo, hi) in enumerate(((0, 512), (512, ROWW))):
                last = T.matmul(ps[0:HEADS, 6 + j, 0:hi - lo], relx[0:BUCKETS + 1, :], onehot[0:BUCKETS + 1, lo:hi], start=True, stop=True)
            last.then_inc(brow_done, 1)
            pe.wait_ge(hT_ready, TILES)
            def project(unit):
                c = next(c for c in range(7) if unit < UNITS[c])
                m = unit - (UNITS[c - 1] if c else 0)
                slot = c % RING
                pe.wait_ge(w_in[slot], 16 * (c // RING + 1))
                if unit >= 2:
                    pe.wait_ge(unit_out, unit - 1)
                if m == NT:
                    for k in range(KC):
                        r_ = slice(64 * (k % 2), 64 * (k % 2) + 32)
                        last = T.matmul(ps[r_, unit % 2, :], hT[:, k, TOK - 32:TOK], w1v[:, slot, k, :],
                                        start=(k < 2), stop=(k >= KC - 2))
                elif c in TURNED_PARTS:
                    for k in range(KC):
                        last = T.matmul(ps[:, unit % 2, :], w1v[:, slot, k, m * P:(m + 1) * P], hT[:, k, 0:SEQ],
                                        start=(k == 0), stop=(k == KC - 1))
                else:
                    for k in range(KC):
                        last = T.matmul(ps[:, unit % 2, :], hT[:, k, m * P:(m + 1) * P], w1v[:, slot, k, :],
                                        start=(k == 0), stop=(k == KC - 1))
                last.then_inc(unit_done, 1)

            def pick_samples(c):
                pe.wait_ge(unit_out, UNITS[c])
                if c:
                    pe.wait_ge(part_out, c)
                sums = partial[c > IB]
                if c in TURNED_PARTS:
                    for h in range(HEADS):
                        last = T.matmul(ps[:, 2, h * NB:(h + 1) * NB], sums[:, h * P:(h + 1) * P], pick, start=True, stop=True)
                else:
                    last = T.matmul(ps[0:NB, 2, :], pick, sums, start=True, stop=True)
                last.then_inc(part_picked, 1)

            def levels(m):
                h, t = m // NT, m % NT
                s, cols = h % 2, slice(t * P, (t + 1) * P)
                pe.wait_ge(ops_ready, h + 1)
                for j in range(3):
                    T.matmul(ps[:, 3, j * P:(j + 1) * P], wl[s][j][:, cols], wl[s][j][:, cols], start=True, stop=True)
                T.matmul(ps[:, 3, 3 * P:4 * P], k16[s][:, cols], q16[s][:, cols], start=True, stop=True).then_inc(lvl_done, 1)
                T.transpose(ps[:, 4, 0:P], kdT[s][:, cols], ident).then_inc(kd_turned, 1)

            def outputs(m):
                h, t = m // NT, m % NT
                s, cols = h % 2, slice(t * P, (t + 1) * P)
                v_ = ib[:, t, h * DH:(h + 1) * DH]
                pe.wait_ge(smask_ready, m + 1)
                if m:
                    pe.wait_ge(o_out, m)
                    pe.wait_ge(state_ready, m)
                if t:
                    T.matmul(ps[:, 5, 0:P], qc[s][:, cols], state[:, h, :], start=True, stop=False)
                for j in range(4):
                    T.matmul(ps[:, 5, 0:P], smask[:, j, :], v_, start=(t == 0 and j == 0), stop=(j == 3))
                pe.wait_ge(kdtok_ready, m + 1)
                T.matmul(ps[:, 6, 0:P], kdtok, v_, start=True, stop=True).then_inc(o_done, 1)

            pe.wait_ge(partial_clear, 1)
            for unit in range(UNITS[IB]):
                project(unit)
                if unit and unit % TILES == 0:
                    pick_samples(unit // TILES - 1)
            for unit in range(UNITS[IB], UNITS[GB]):
                m = unit - UNITS[IB]
                if m == 0:
                    pick_samples(IB)
                if m < HEADS * NT:
                    levels(m)
                project(unit)
                if m and m % TILES == 0:
                    pick_samples(unit // TILES - 1)
                if m < HEADS * NT:
                    outputs(m)
                k = unit - UNITS[VA]
                if k >= 0:
                    n = rows_of(k)
                    pe.wait_ge(unit_out, UNITS[KA])
                    pe.wait_ge(part_out, KA + 1)
                    if k:
                        pe.wait_ge(ktok_ready, k)
                    for h in range(HEADS):
                        last = T.transpose(ps[0:n, 7, h * P:(h + 1) * P], kT[:, h, k * P:k * P + n], ident)
                    last.then_inc(kt_turned, 1)
            pick_samples(GB)
            pe.wait_ge(part_out, GB + 1)
            pe.wait_ge(ktok_ready, TILES)
            pe.wait_ge(o_out, HEADS * NT)
            pe.wait_ge(state_ready, HEADS * NT)

            def scores(n):
                h, i = n // NT, n % NT
                if n >= 2:
                    pe.wait_ge(logit_ready, n - 1)
                T.matmul(ps[:, n % 2, 0:(i + 1) * P], qT[:, h, i * P:(i + 1) * P], kT[:, h, 0:(i + 1) * P],
                         start=True, stop=True).then_inc(logit_done, 1)

            def key_scores(b):
                pe.wait_ge(keyT_ready, b + 1)
                for t in range(2):
                    for h in range(HEADS):
                        c = t * 32 + b * HEADS + h
                        last = T.matmul(ps[:, 5, c:c + 1], keyT[b % 2][:, t, h * P:(h + 1) * P], qT[:, h, SEQ + b:SEQ + b + 1],
                                        start=True, stop=True)
                last.then_inc(dscore_done, 1)

            def keys(b):
                if b in (0, 6):
                    pe.wait_ge(kv_in[b // 6], 16 * (36 if b == 0 else 12))
                if b:
                    pe.wait_ge(keyT_ready, b)
                for t in range(2):
                    for h in range(HEADS):
                        last = T.transpose(ps[:, 6 + t, h * P:(h + 1) * P],
                                           kvv[:, (KV_SLOT + b // 2) % RING, b % 2, 0, t, h * DH:(h + 1) * DH], ident)
                last.then_inc(key_turned, 1)

            def gated_heads(t):
                pe.wait_ge(og_ready, t + 1)
                if t:
                    pe.wait_ge(og_out, t)
                for h in range(HEADS):
                    last = T.transpose(ps[:, 7, h * P:(h + 1) * P], ostage[:, h, :], ident)
                last.then_inc(og_turned, 1)

            def spread_value(b):
                pe.wait_ge(vonly_ready, b + 1)
                if b:
                    pe.wait_ge(kv_ready, b)
                T.matmul(ps[:, 6, :], ones[0:NB, :], vonly[b % 2][0:NB], start=True, stop=True).then_inc(vb_done, 1)

            scores(0)
            for n in range(HEADS * NT):
                h, i = n // NT, n % NT
                if n + 1 < HEADS * NT:
                    scores(n + 1)
                if 0 < n <= NB:
                    key_scores(n - 1)
                pe.wait_ge(prob_normed, n + 1)
                if n >= 2:
                    pe.wait_ge(probT_ready, n - 1)
                for j in range(i + 1):
                    last = T.transpose(ps[:, 2 + n % 2, j * P:(j + 1) * P], prob[n % 2][:, j * P:(j + 1) * P], ident)
                last.then_inc(prob_turned, 1)
                if n < NB:
                    keys(n)
                else:
                    t = n - NB
                    spread_value(t)
                    if 0 <= n - 10 < NT:
                        gated_heads(n - 10)
                pe.wait_ge(probT_ready, n + 1)
                if n:
                    pe.wait_ge(att_out, n)
                for j in range(i + 1):
                    last = T.matmul(ps[:, 4, 0:P], vtok[:, j, h * DH:(h + 1) * DH], probT[n % 2][:, j, :],
                                    start=(j == 0), stop=(j == i))
                last.then_inc(att_done, 1)
            pe.wait_ge(att_out, HEADS * NT)
            def project_out(t, c):
                if t >= 2:
                    pe.wait_ge(x_added, t - 1)
                pe.wait_ge(wout_in[c], 16)
                for k in range(KC):
                    if t < NT:
                        last = T.matmul(ps[:, 4 + 2 * (t % 2) + c, :], catT[:, k, t * P:(t + 1) * P], w1v[:, WOUT_SLOT + c, k, :],
                                        start=(k == 0), stop=(k == KC - 1))
                    else:
                        r_ = slice(64 * (k % 2), 64 * (k % 2) + 32)
                        last = T.matmul(ps[r_, 4 + c, :], catT[:, k, TOK - 32:TOK], w1v[:, WOUT_SLOT + c, k, :],
                                        start=(k < 2), stop=(k >= KC - 2))
                last.then_inc(wo_done, 1)

            def pick_out():
                pe.wait_ge(part_out, GB + 2)
                pe.wait_ge(x_added, NT)
                for c in range(2):
                    last = T.matmul(ps[0:NB, 6 + c, :], pick_late, partial_late[:, c, :], start=True, stop=True)
                last.then_inc(wo_done, 1)

            T.matmul(ps[0:32, 0, 0:NDEC], relrep[0:BUCKETS + 1].rearrange("p b h -> p (b h)"), onehot[0:BUCKETS + 1, ROWW:],
                     start=True, stop=True).then_inc(sample_step, 1)
            pe.wait_ge(dscT_ready, 1)
            for t in range(2):
                T.transpose(ps[0:32, 2, t * P:(t + 1) * P], dscT[:, t].rearrange("p b h -> p (b h)"), ident)
            pe.wait_ge(qkself_ready, 1)
            T.matmul(ps[0:32, 2, NDEC - 1:NDEC], qkself.rearrange("p b h -> p (b h)"), ones[:, 0:1], start=True, stop=True).then_inc(sample_step, 1)
            pe.wait_ge(og_out, NT)
            project_out(0, 0)
            pe.wait_ge(dprob_ready, 1)
            for t in range(2):
                last = T.transpose(ps[:, 3, t * 32:(t + 1) * 32], dprob[0:32, t * P:(t + 1) * P], ident[0:32, 0:32])
            last.then_inc(sample_step, 1)
            pe.wait_ge(snew_ready, NB)
            for h in range(HEADS):
                T.transpose(ps[:, 1, 32 + h * NB:32 + (h + 1) * NB], gb[0:NB, NT, h * DH:(h + 1) * DH], ident[0:NB, 0:NB])
            for b in range(NB):
                for h in range(HEADS):
                    last = T.matmul(ps[:, 1, h * NB + b:h * NB + b + 1], stv[:, b, h, :], qbT[:, h, SEQ + b:SEQ + b + 1],
                                    start=True, stop=True)
            last.then_inc(sample_step, 1)
            pe.wait_ge(dprobT_ready, 2)
            for b in range(NB):
                for t in range(2):
                    last = T.matmul(ps[0:32, 0, :], pspread[:, t, b * 32:(b + 1) * 32], kvv[:, (KV_SLOT + b // 2) % RING, b % 2, 1, t, :],
                                    start=(b == 0 and t == 0), stop=False, skip_group_check=True)
                if b % 2:
                    last.then_inc(kv_used, 1)
            pe.wait_ge(vrow_in, 16)
            for h in range(HEADS):
                last = T.matmul(ps[0:32, 0, h * DH:(h + 1) * DH], diag[0:32], vrow[0:32], start=False, stop=True, skip_group_check=True)
            last.then_inc(sample_step, 1)
            pe.wait_ge(osq_ready, 1)
            T.matmul(ps[:, 1, 0:32], ones, osq, start=True, stop=True).then_inc(sample_step, 1)
            project_out(1, 0)
            pe.wait_ge(dheads_ready, 1)
            for h in range(HEADS):
                last = T.transpose(ps[:, 3, h * 32:(h + 1) * 32], dheads[0:32, h * DH:(h + 1) * DH], ident[0:32, 0:32])
            last.then_inc(sample_step, 1)

            def mix(t):
                n = rows_of(t)
                pe.wait_ge(pooled_in, t + 1)
                if t:
                    pe.wait_ge(mixT_ready, t)
                for k in range(KC):
                    g = k // 2
                    out = ps[:, k // 4, (k % 4) * P:(k % 4) * P + n]
                    cols = slice(k * P, (k + 1) * P)
                    if t < NT:
                        last = T.matmul(out, hall[:, t, cols], poolc[:, 0 if t == 0 else 1, g, :], start=True, stop=(t == 0))
                        if t:
                            last = T.matmul(out, hall[:, t - 1, cols], poolc[:, 2, g, :], start=False, stop=True)
                    else:
                        T.matmul(out, prev[0:NB * KEEP, cols], poolstate[0:NB * KEEP, 0, g, :], start=True, stop=False)
                        last = T.matmul(out, hall[0:NB, t, cols], poolstate[0:NB, 1, g, :], start=False, stop=True)
                last.then_inc(mix_done, 1)

            def maps(t):
                n = rows_of(t)
                pe.wait_ge(mixT_ready, t + 1)
                if t:
                    pe.wait_ge(x_added, TILES + t)
                for g in range(NG):
                    for k in range(2):
                        last = T.matmul(ps[0:n, 4 + g // 2, (g % 2) * 256:(g % 2 + 1) * 256], mixT[:, 2 * g + k, 0:n],
                                        poolw[:, g, k, :], start=(k == 0), stop=(k == 1))
                last.then_inc(pool_done, 1)

            def products(j, halves):
                for k in range(KC):
                    for half in halves:
                        r_ = slice(half * CAP, (half + 1) * CAP)
                        last = T.matmul(ps[r_, 2 + j, :], xgT[:, k, r_], w1v[:, piece_slot(half, j), k, :],
                                        start=(k == 0), stop=(k == KC - 1))
                return last

            def results(halves):
                for c in range(2):
                    for k in range(FC):
                        for half in halves:
                            r_ = slice(half * CAP, (half + 1) * CAP)
                            last = T.matmul(ps[r_, 5 + c, :], hactT[:, k, r_], w2v[:, piece_slot(half, 2), k, c * 512:(c + 1) * 512],
                                            start=(k == 0), stop=(k == FC - 1))
                return last

            def experts(l):
                def turn_h(t):
                    n = rows_of(t)
                    g = TILES * l + t
                    pe.wait_ge(hn_ready, g + 1)
                    if t:
                        pe.wait_ge(htile_ready, g)
                    for k in range(KC):
                        last = T.transpose(ps[:, 6 * l + k // 4, (k % 4) * P:(k % 4) * P + n], hall[0:n, t, k * P:(k + 1) * P],
                                           ident[0:n, 0:n])
                    last.then_inc(hn_turned, 1)

                def router_logits(t):
                    n = rows_of(t)
                    g = TILES * l + t
                    pe.wait_ge(htile_ready, g + 1)
                    if t:
                        pe.wait_ge(lg_ready, g)
                    for k in range(KC):
                        last = T.matmul(ps[0:n, 2, 0:NG + NE], htile[:, k, 0:n], wr[:, l, k, :], start=(k == 0), stop=(k == KC - 1))
                    last.then_inc(rlog_done, 1)

                def ranks(t):
                    pe.wait_ge(mem_ready, TILES * l + t + 1)
                    if t:
                        pe.wait_ge(first_ready, TILES * l + t)
                    out = ps[:, 3, t * NE:(t + 1) * NE]
                    last = T.matmul(out, tri, mem[:, t, :], start=True, stop=(t == 0))
                    if t:
                        last = T.matmul(out, ones, before(t), start=False, stop=True)
                    if t == TILES - 1:
                        last = T.matmul(ps[:, 3, TILES * NE:(TILES + 1) * NE], ones, before(TILES), start=True, stop=True)
                    last.then_inc(rank_done, 1)

                def before(t):
                    return mem[:, 0, :] if t == 1 else over[:, t - 1, :]

                if l == 0:
                    for u in range(TILES + 2):
                        if u == NT:
                            pe.wait_ge(cat_ready, 2)
                        if 2 <= u < TILES:
                            project_out(u, 0)
                        if 0 <= u - 1 < TILES:
                            turn_h(u - 1)
                        if u < TILES:
                            project_out(u, 1)
                        if u == NT:
                            pick_out()
                        if u == 1:
                            pe.wait_ge(router_in, 16 * 9)
                        if 0 <= u - 1 < TILES:
                            router_logits(u - 1)
                        if u >= 2:
                            ranks(u - 2)
                else:
                    for u in range(TILES + 5):
                        if u >= 5:
                            ranks(u - 5)
                        if 0 <= u - 1 < TILES:
                            maps(u - 1)
                        if 0 <= u - 3 < TILES:
                            turn_h(u - 3)
                            router_logits(u - 3)
                        if u < TILES:
                            mix(u)
                pe.wait_ge(slots_ready, l + 1)

                def turn(i, first):
                    pe.wait_ge(xg_in, 16 * PAIRS * l + 16 * i + 16)
                    if not first:
                        pe.wait_ge(xT_ready, PAIRS * l + i)
                    for k in range(KC):
                        last = T.transpose(ps[:, k // 4, (k % 4) * P:(k % 4 + 1) * P], xg[:, k * P:(k + 1) * P], ident)
                    last.then_inc(x_turned, 1)

                def pair(i, first, last):
                    pe.wait_ge(xT_ready, PAIRS * l + i + 1)
                    if not first:
                        pe.wait_ge(hact_ready, PAIRS * l + i)
                    for j in range(2):
                        for half in range(2):
                            pe.wait_ge(wt_in[piece_slot(half, j)], 16 * PAIRS * l + 16 * i + 16)
                        products(j, (0, 1)).then_inc((w1_used, h_done)[j], 1)
                    if not last:
                        turn(i + 1, False)
                    pe.wait_ge(hact_ready, PAIRS * l + i + 1)
                    if not first:
                        pe.wait_ge(hactT_ready, PAIRS * l + i)
                    for k in range(FC):
                        t_ = T.transpose(ps[:, 4, k * P:(k + 1) * P], hact[:, k * P:(k + 1) * P], ident)
                    t_.then_inc(hact_turned, 1)
                    for half in range(2):
                        pe.wait_ge(wt_in[piece_slot(half, 2)], 16 * PAIRS * l + 16 * i + 16)
                    pe.wait_ge(hactT_ready, PAIRS * l + i + 1)
                    if not first:
                        pe.wait_ge(y_out, PAIRS * l + i)
                    results((0, 1)).then_inc(y_done, 1)

                turn(0, True)
                pair(0, True, False)
                with pe.Fori(1, PAIRS - 1) as i:
                    pair(i, False, False)
                pair(PAIRS - 1, False, True)
                pe.wait_ge(y_out, PAIRS * (l + 1))
                pe.wait_ge(tables_ready, l + 1)
                n_over = pe.value_load(tables[l][0:1, NOV:NOV + 1], min_val=0, max_val=NOV)
                with pe.If(n_over > 0):
                    with pe.Fori(0, NOV) as j:
                        with pe.If(n_over > j):
                            pe.wait_ge(over_in[l], 64 * j + 64)
                            pe.sem_inc(over_seen, 1)
                            for k in range(KC):
                                last = T.transpose(ps[:, 0, k * CAP:(k + 1) * CAP], xg[0:CAP, k * P:(k + 1) * P], ident[0:CAP, 0:CAP])
                            last.then_inc(over_step[l], 1)
                            pe.wait_ge(over_step[l], over_count(j, COLUMNS))
                            products(0, (0,))
                            products(1, (0,)).then_inc(over_step[l], 1)
                            pe.wait_ge(over_step[l], over_count(j, GATED))
                            pe.sem_inc(over_seen, 1)
                            for k in range(FC):
                                last = T.transpose(ps[:, 4, k * CAP:(k + 1) * CAP], hact[0:CAP, k * P:(k + 1) * P], ident[0:CAP, 0:CAP])
                            last.then_inc(over_step[l], 1)
                            pe.wait_ge(over_step[l], over_count(j, ACT_COLUMNS))
                            results((0,)).then_inc(over_step[l], 1)
                        with pe.Else():
                            pe.nop()
                    pe.nop()
                with pe.Else():
                    pe.nop()
                pe.nop()

            experts(0)
            experts(1)


_INS = ["x_prompt", "x_sample", "cache_win_k", "cache_win_v", "state_hgrn", "state_pool", "rel_bias", "norm_mix",
        "norm_ffn", "norm_final", "w_in", "w_out", "hgrn_lb", "hgrn_gnorm", "pool_w", "pool_scale", "moe_wg_group",
        "moe_bg_group", "moe_wg_exp", "moe_bg_exp", "moe_w1", "moe_w3", "moe_w2"]
_OUTS = [(1, SEQ, D), (NB, 1, D), (1, 1, SEQ, HEADS, DH), (1, 1, SEQ, HEADS, DH), (1, 1, HEADS, DH, DH), (1, 1, KEEP, D),
         (1, NB, 1, HEADS, DH), (1, NB, 1, HEADS, DH), (1, NB, HEADS, DH, DH), (1, NB, 1, D)]


def kernel(**inputs):
    import numpy as _np
    import concourse.bacc as _bacc
    from concourse import mybir as _mybir
    from concourse.bass_utils import run_bass_kernel_spmd as _run

    nc = _bacc.Bacc("TRN2", target_bir_lowering=False, num_devices=1)
    arrays, a, consts = {}, {}, {}
    for name in _INS:
        v = _np.ascontiguousarray(inputs[name])
        arrays[f"in_{name}"] = v
        a[name] = nc.dram_tensor(f"in_{name}", v.shape, _mybir.dt.from_np(v.dtype), kind="ExternalInput").ap()
    for name, v in shape_constants().items():
        arrays[name] = v
        consts[name] = nc.dram_tensor(name, v.shape, _mybir.dt.from_np(v.dtype), kind="ExternalInput").ap()
    outs = [nc.dram_tensor(f"out_{i}", s, _mybir.dt.float32, kind="ExternalOutput").ap() for i, s in enumerate(_OUTS)]
    build(nc, a, outs, consts)
    r = _run(nc, [arrays], core_ids=[0])
    return tuple(r.results[0][f"out_{i}"] for i in range(len(_OUTS)))
```
